# Optimizing a Trainium2 kernel written in Bass

```python
import math
import jax
import jax.numpy as jnp
from jax import lax
import numpy as np

D_MODEL = 1024
BATCH = 1
SEQ = 512
DEPTH = 1

CTX_LEN = 256
GRID_W = 64
EPS = 1e-6

DN_HEADS = 8
DN_DK = 128
DN_DV = 128
DN_QK = DN_HEADS * DN_DK
DN_V = DN_HEADS * DN_DV
DN_CONV = 3
DN_CHUNK = 64

ATTN_HEADS = 8
ATTN_KV_HEADS = 2
ATTN_GROUP = ATTN_HEADS // ATTN_KV_HEADS
ATTN_DH = 128
ATTN_Q = ATTN_HEADS * ATTN_DH
ATTN_KV = ATTN_KV_HEADS * ATTN_DH
Q_BLOCK = 128
ROPE_THETA = 10000.0
ROPE_FREQS = ATTN_DH // 4

FFN_HIDDEN = 2816
FFN_RES_WEIGHT = 0.5

N_MOD = 9

IN_SIZES = (2 * DN_QK + DN_V, DN_V, 4 * DN_HEADS, ATTN_Q, 2 * ATTN_KV, 2 * D_MODEL)
IN_W = 2 * DN_QK + DN_V + DN_V + 4 * DN_HEADS + ATTN_Q + 2 * ATTN_KV + 2 * D_MODEL

kernel_name = 'hybrid_deltanet_gqa_macaron_prefix_block'

def _rmsnorm(x, g):
    xf = x.astype(jnp.float32)
    y = xf * lax.rsqrt(jnp.mean(xf * xf, axis=-1, keepdims=True) + EPS)
    return (y * g.astype(jnp.float32)).astype(x.dtype)

def _l2norm(x):
    xf = x.astype(jnp.float32)
    return xf * lax.rsqrt(jnp.sum(xf * xf, axis=-1, keepdims=True) + EPS)

def _modulate(h, shift, scale):
    return h * (1.0 + scale) + shift

def _ffn_sublayer(x, shift, scale, gate, pre_g, post_g, w_gu, w_down):
    h = _modulate(_rmsnorm(x, pre_g), shift, scale)
    a, b = jnp.split(h @ w_gu, 2, axis=-1)
    y = (jax.nn.silu(a) * b) @ w_down
    return x + FFN_RES_WEIGHT * gate * _rmsnorm(y, post_g)

def _short_conv(u, w):
    l = u.shape[1]
    pad = DN_CONV // 2
    up = jnp.pad(u, ((0, 0), (pad, pad), (0, 0)))
    out = up[:, 0:l] * w[0]
    for j in range(1, DN_CONV):
        out = out + up[:, j:j + l] * w[j]
    return out

def _rope_tables(l, dtype):
    rows = l // GRID_W
    row = jnp.repeat(jnp.arange(rows, dtype=jnp.int32), GRID_W)
    col = jnp.tile(jnp.arange(GRID_W, dtype=jnp.int32), rows)
    pos = jnp.stack([row, col], axis=-1).astype(jnp.float32)
    inv_freq = ROPE_THETA ** (-jnp.arange(ROPE_FREQS, dtype=jnp.float32) / ROPE_FREQS)
    ang = pos[:, :, None] * inv_freq
    return jnp.cos(ang).astype(dtype), jnp.sin(ang).astype(dtype)

def _rope(x, cos, sin):
    xr = x.reshape(*x.shape[:-1], 2, 2, ROPE_FREQS)
    x1, x2 = xr[..., 0, :], xr[..., 1, :]
    c, s = cos[:, None], sin[:, None]
    out = jnp.stack([x1 * c - x2 * s, x2 * c + x1 * s], axis=-2)
    return out.reshape(x.shape)

def _delta_rule(q, k, v, beta, g, s0):
    b, h, l, _ = q.shape
    dv = v.shape[-1]
    n = l // DN_CHUNK

    def chunk(t):
        return jnp.moveaxis(t.reshape(b, h, n, DN_CHUNK, *t.shape[3:]), 2, 0)

    qc, kc, vc, bc, gc = chunk(q), chunk(k), chunk(v), chunk(beta), chunk(g)
    gcum = jnp.cumsum(gc, axis=-1)
    idx = jnp.arange(DN_CHUNK)
    lower_incl = idx[:, None] >= idx[None, :]
    strict = idx[:, None] > idx[None, :]
    decay = jnp.exp(jnp.where(lower_incl, gcum[..., :, None] - gcum[..., None, :], -jnp.inf))
    kb = kc * bc[..., None]
    l_mat = jnp.where(strict, jnp.einsum('nbhid,nbhjd->nbhij', kb, kc) * decay, 0.0)
    rhs = jnp.concatenate([vc * bc[..., None], kb * jnp.exp(gcum)[..., None]], axis=-1)
    sol = lax.linalg.triangular_solve(l_mat, rhs, left_side=True, lower=True, unit_diagonal=True)
    u, w = sol[..., :dv], sol[..., dv:]
    intra = jnp.where(lower_incl, jnp.einsum('nbhid,nbhjd->nbhij', qc, kc) * decay, 0.0)
    q_dec = qc * jnp.exp(gcum)[..., None]
    k_dec = kc * jnp.exp(gcum[..., -1:] - gcum)[..., None]
    chunk_decay = jnp.exp(gcum[..., -1])

    def step(s, xs):
        q_d, k_d, u_c, w_c, a_c, d_c = xs
        v_new = u_c - jnp.einsum('bhcd,bhde->bhce', w_c, s)
        o = jnp.einsum('bhcd,bhde->bhce', q_d, s) + jnp.einsum('bhij,bhje->bhie', a_c, v_new)
        s = s * d_c[..., None, None] + jnp.einsum('bhcd,bhce->bhde', k_d, v_new)
        return s, o

    s_final, o = lax.scan(step, s0, (q_dec, k_dec, u, w, intra, chunk_decay))
    return jnp.moveaxis(o, 0, 2).reshape(b, h, l, dv), s_final

def _flip(t):
    return jnp.flip(t, axis=2)

def _attend(q, k, v):
    b, lq = q.shape[:2]
    qg = q.reshape(b, lq, ATTN_KV_HEADS, ATTN_GROUP, ATTN_DH)
    s = jnp.einsum('bqkgd,bskd->bkgqs', qg, k).astype(jnp.float32) * (ATTN_DH ** -0.5)
    p = jax.nn.softmax(s, axis=-1).astype(v.dtype)
    o = jnp.einsum('bkgqs,bskd->bqkgd', p, v)
    return o.reshape(b, lq, ATTN_Q)

def _block_attention(q, k, v):
    b, l = q.shape[:2]
    nb = l // Q_BLOCK
    qb = jnp.moveaxis(q.reshape(b, nb, Q_BLOCK, ATTN_HEADS, ATTN_DH), 1, 0)
    o = lax.map(lambda blk: _attend(blk, k, v), qb)
    return jnp.moveaxis(o, 0, 1).reshape(b, l, ATTN_Q)

def _mixer_inputs(h, w_in, conv_w, a_log, dt_bias, q_norm, k_norm, rope):
    b, l, _ = h.shape
    split_at = np.cumsum(IN_SIZES)[:-1].tolist()
    qkv, z, ba, q_a, kv_a, gates = jnp.split(h @ w_in, split_at, axis=-1)
    qkv = jax.nn.silu(_short_conv(qkv, conv_w))
    q_d, k_d, v_d = jnp.split(qkv, [DN_QK, 2 * DN_QK], axis=-1)
    q_d = _l2norm(q_d.reshape(b, l, DN_HEADS, DN_DK)) * (DN_DK ** -0.5)
    k_d = _l2norm(k_d.reshape(b, l, DN_HEADS, DN_DK))
    v_d = v_d.reshape(b, l, DN_HEADS, DN_DV).astype(jnp.float32)
    ba = ba.astype(jnp.float32).reshape(b, l, 2, 2, DN_HEADS)
    beta = jax.nn.sigmoid(ba[:, :, 0])
    g = -jnp.exp(a_log.astype(jnp.float32)) * jax.nn.softplus(ba[:, :, 1] + dt_bias.astype(jnp.float32))
    dn = (jnp.swapaxes(q_d, 1, 2), jnp.swapaxes(k_d, 1, 2), jnp.swapaxes(v_d, 1, 2),
          jnp.moveaxis(beta, 1, 3), jnp.moveaxis(g, 1, 3))
    q_a = _rmsnorm(q_a.reshape(b, l, ATTN_HEADS, ATTN_DH), q_norm)
    k_a, v_a = jnp.split(kv_a, 2, axis=-1)
    k_a = _rmsnorm(k_a.reshape(b, l, ATTN_KV_HEADS, ATTN_DH), k_norm)
    v_a = v_a.reshape(b, l, ATTN_KV_HEADS, ATTN_DH)
    if rope is not None:
        q_a = _rope(q_a, *rope)
        k_a = _rope(k_a, *rope)
    return dn, (q_a, k_a, v_a), z, gates

def _merge(o_dn, z, o_at, gates, dn_norm, w_dn_out, w_attn_out, w_out):
    b, l, _ = z.shape
    o = _rmsnorm(jnp.swapaxes(o_dn, 1, 2), dn_norm).astype(z.dtype)
    o = o * jax.nn.silu(z.reshape(b, l, DN_HEADS, DN_DV))
    y_dn = o.reshape(b, l, DN_V) @ w_dn_out
    y_at = o_at @ w_attn_out
    g_dn, g_at = jnp.split(gates, 2, axis=-1)
    return (jax.nn.sigmoid(g_dn) * y_dn + jax.nn.sigmoid(g_at) * y_at) @ w_out

def _mixer(h, hc, w_in, conv_w, a_log, dt_bias, dn_norm, w_dn_out, q_norm, k_norm, w_attn_out, w_out, ctx_out):
    b = h.shape[0]
    rope = _rope_tables(h.shape[1], h.dtype)
    (q_d, k_d, v_d, beta, g), (q_a, k_a, v_a), z, gates = _mixer_inputs(
        h, w_in, conv_w, a_log, dt_bias, q_norm, k_norm, rope)
    (qc_d, kc_d, vc_d, betac, gc), (qc_a, kc_a, vc_a), zc, gatesc = _mixer_inputs(
        hc, w_in, conv_w, a_log, dt_bias, q_norm, k_norm, None)
    s0 = jnp.zeros((b, DN_HEADS, DN_DK, DN_DV), jnp.float32)
    oc_f, s_f = _delta_rule(qc_d, kc_d, vc_d, betac[:, 0], gc[:, 0], s0)
    oc_b, s_b = _delta_rule(_flip(qc_d), _flip(kc_d), _flip(vc_d), _flip(betac[:, 1]), _flip(gc[:, 1]), s0)
    o_f, _ = _delta_rule(q_d, k_d, v_d, beta[:, 0], g[:, 0], s_f)
    o_b, _ = _delta_rule(_flip(q_d), _flip(k_d), _flip(v_d), _flip(beta[:, 1]), _flip(g[:, 1]), s_b)
    o_dn = o_f + _flip(o_b)
    k_all = jnp.concatenate([kc_a, k_a], axis=1)
    v_all = jnp.concatenate([vc_a, v_a], axis=1)
    o_at = _block_attention(q_a, k_all, v_all)
    y = _merge(o_dn, z, o_at, gates, dn_norm, w_dn_out, w_attn_out, w_out)
    if not ctx_out:
        return y, None
    yc = _merge(oc_f + _flip(oc_b), zc, _attend(qc_a, kc_a, vc_a), gatesc, dn_norm, w_dn_out, w_attn_out, w_out)
    return y, yc

def setup_inputs(seed: int = 0) -> dict:
    key = jax.random.key(seed)
    ks = jax.random.split(key, 28)
    f32 = jnp.float32

    def nrm(i, shape, std):
        return std * jax.random.normal(ks[i], shape, f32)

    def gain(i, shape):
        return 1.0 + 0.1 * jax.random.normal(ks[i], shape, f32)

    dt = jnp.exp(jax.random.uniform(ks[15], (DEPTH, 2, DN_HEADS), f32, math.log(1e-3), math.log(1e-1)))
    return {
        'x': nrm(0, (BATCH, SEQ, D_MODEL), 1.0),
        'c': nrm(1, (BATCH, D_MODEL), 1.0),
        'ctx': nrm(2, (BATCH, CTX_LEN, D_MODEL), 1.0),
        'c_ctx': nrm(3, (D_MODEL,), 1.0),
        'w_mod': nrm(4, (DEPTH, D_MODEL, N_MOD * D_MODEL), 0.5 * D_MODEL ** -0.5),
        'b_mod': nrm(5, (DEPTH, N_MOD * D_MODEL), 0.01),
        'ffn1_pre': gain(6, (DEPTH, D_MODEL)),
        'ffn1_post': gain(7, (DEPTH, D_MODEL)),
        'ffn1_w_gu': nrm(8, (DEPTH, D_MODEL, 2 * FFN_HIDDEN), D_MODEL ** -0.5),
        'ffn1_w_down': nrm(9, (DEPTH, FFN_HIDDEN, D_MODEL), FFN_HIDDEN ** -0.5),
        'mix_pre': gain(10, (DEPTH, D_MODEL)),
        'mix_post': gain(11, (DEPTH, D_MODEL)),
        'w_in': nrm(12, (DEPTH, D_MODEL, IN_W), D_MODEL ** -0.5),
        'dn_conv': nrm(13, (DEPTH, DN_CONV, 2 * DN_QK + DN_V), DN_CONV ** -0.5),
        'dn_a_log': jnp.log(jax.random.uniform(ks[14], (DEPTH, 2, DN_HEADS), f32, 1.0, 16.0)),
        'dn_dt_bias': dt + jnp.log(-jnp.expm1(-dt)),
        'dn_out_norm': gain(16, (DEPTH, DN_DV)),
        'w_dn_out': nrm(17, (DEPTH, DN_V, D_MODEL), DN_V ** -0.5),
        'attn_q_norm': gain(18, (DEPTH, ATTN_DH)),
        'attn_k_norm': gain(19, (DEPTH, ATTN_DH)),
        'w_attn_out': nrm(20, (DEPTH, ATTN_Q, D_MODEL), ATTN_Q ** -0.5),
        'w_out': nrm(21, (DEPTH, D_MODEL, D_MODEL), D_MODEL ** -0.5),
        'ffn2_pre': gain(22, (DEPTH, D_MODEL)),
        'ffn2_post': gain(23, (DEPTH, D_MODEL)),
        'ffn2_w_gu': nrm(24, (DEPTH, D_MODEL, 2 * FFN_HIDDEN), D_MODEL ** -0.5),
        'ffn2_w_down': nrm(25, (DEPTH, FFN_HIDDEN, D_MODEL), FFN_HIDDEN ** -0.5),
    }

def reference(x, c, ctx, c_ctx, w_mod, b_mod, ffn1_pre, ffn1_post, ffn1_w_gu, ffn1_w_down,
              mix_pre, mix_post, w_in, dn_conv, dn_a_log, dn_dt_bias, dn_out_norm, w_dn_out,
              attn_q_norm, attn_k_norm, w_attn_out, w_out, ffn2_pre, ffn2_post, ffn2_w_gu, ffn2_w_down):
    cx = ctx
    for i in range(DEPTH):
        last = i == DEPTH - 1
        mod = jnp.split((jax.nn.silu(c) @ w_mod[i] + b_mod[i])[:, None, :], N_MOD, axis=-1)
        mod_c = jnp.split((jax.nn.silu(c_ctx) @ w_mod[i] + b_mod[i])[None, None, :], N_MOD, axis=-1)
        x = _ffn_sublayer(x, mod[0], mod[1], mod[2], ffn1_pre[i], ffn1_post[i], ffn1_w_gu[i], ffn1_w_down[i])
        cx = _ffn_sublayer(cx, mod_c[0], mod_c[1], mod_c[2], ffn1_pre[i], ffn1_post[i], ffn1_w_gu[i], ffn1_w_down[i])
        h = _modulate(_rmsnorm(x, mix_pre[i]), mod[3], mod[4])
        hc = _modulate(_rmsnorm(cx, mix_pre[i]), mod_c[3], mod_c[4])
        y, yc = _mixer(h, hc, w_in[i], dn_conv[i], dn_a_log[i], dn_dt_bias[i], dn_out_norm[i], w_dn_out[i],
                       attn_q_norm[i], attn_k_norm[i], w_attn_out[i], w_out[i], not last)
        x = x + mod[5] * _rmsnorm(y, mix_post[i])
        x = _ffn_sublayer(x, mod[6], mod[7], mod[8], ffn2_pre[i], ffn2_post[i], ffn2_w_gu[i], ffn2_w_down[i])
        if not last:
            cx = cx + mod_c[5] * _rmsnorm(yc, mix_post[i])
            cx = _ffn_sublayer(cx, mod_c[6], mod_c[7], mod_c[8], ffn2_pre[i], ffn2_post[i], ffn2_w_gu[i], ffn2_w_down[i])
    return x


_drawn_inputs = setup_inputs


def setup_inputs(seed=0):
    import zlib

    import numpy as np

    out = dict(_drawn_inputs(seed))
    spreads = {}
    factors = {'b_mod': 3.823,
     'ffn1_post': 3.426,
     'attn_q_norm': 8.0,
     'attn_k_norm': 8.0,
     'ffn2_pre': 2.87,
     'ffn2_post': 3.91,
     'dn_out_norm': 3.493}
    for name, (base, spread) in spreads.items():
        noise = np.random.default_rng([zlib.crc32(name.encode()), seed]).standard_normal(out[name].shape)
        drawn = base * np.exp(spread * noise) if base else spread * noise
        out[name] = jnp.asarray(drawn.astype(out[name].dtype))
    for name, factor in factors.items():
        out[name] = (out[name] * factor).astype(out[name].dtype)
    return out
```

```python
import numpy as np

import concourse.bass as bass
from concourse import mybir
from concourse.alu_op_type import AluOpType as ALU
from contextlib import ExitStack

ACT = mybir.ActivationFunctionType
AX = mybir.AxisListType
F32 = mybir.dt.float32
F32R = mybir.dt.float32r

P = 128
D = 1024
KT = D // P
CTX, SEQ = 256, 512
T = CTX + SEQ
NC_CTX, NC_X = CTX // P, SEQ // P
NCH = NC_CTX + NC_X
EPS = 1e-6
H = 8
HKV = 2
DH = 128
HID = 2816 // P
FCH = [8, 8, 6]
RING = 4

N_FFN = 2 * HID + 3 * KT
B_FFN1 = 0
B_KV = B_FFN1 + N_FFN
B_Q = B_KV + 5
B_DN = B_Q + H
B_MERGE = B_DN + 4 * H
B_OUT = B_MERGE + 4 * KT
B_FFN2 = B_OUT + KT
NBLK = B_FFN2 + N_FFN

N_MOD = 72
LEVELS = 7

V_PRE1, V_POST1, V_PREM, V_POSTM, V_PRE2, V_POST2 = range(0, 48, 8)
V_BMOD = 48
V_QN, V_KN, V_DN, V_ALOG, V_DT = range(V_BMOD + N_MOD, V_BMOD + N_MOD + 5)
V_C = V_DT + 1
NV = V_C + 2 * KT
G_CONV, G_BETA, G_GC, G_BEG, G_KD, G_DCY = 0, 9, 21, 33, 45, 57
NG = 69


class Blk:

    def __init__(self, base, it, j):
        at = base + j
        self.n = at + it * 4
        self.raw = at % RING
        self.pair = at % 2
        self.turn = at // 2 + it * 2
        self.load = at // RING + it
        self.base, self.it, self.j = base, it, j

    def ahead(self, d):
        return Blk(self.base, self.it, self.j + d)


def build(nc, W, WMOD, XT, VEC, CONV, CA, CB, OUT, XS):
    ctx = ExitStack()
    with ctx:
        base0 = 16512

        def at(name, kb, shape, dt=F32):
            return nc.alloc_sbuf_tensor_at(name, [P] + shape, dt, offset=base0 + int(kb * 1024))

        def sem(name):
            return ctx.enter_context(nc.semaphore(name))

        raw = at("raw", 0, [RING, KT, P])
        w_hi = at("w_hi", 16, [2, KT, P], F32R)
        w_lo = at("w_lo", 24, [2, KT, P], F32R)
        h_hi = at("h_hi", 32, [KT, T], F32R)
        h_lo = at("h_lo", 56, [KT, T], F32R)
        ca = at("ca", 80, [5, P])
        vec = at("vec", 82.5, [NV])
        mod = at("mod", 83.25, [N_MOD, 2])
        drv = at("drv", 84, [6, KT, 2])
        silc = at("silc", 84.5, [KT, 2])
        small = at("small", 84.625, [32])
        gall = at("gall", 85, [H, NG])
        cb = at("cb", 87.5, [14 * P + 2 * SEQ])
        w_mod = at("w_mod", 87.5, [2, KT, P])
        ident, ones, tri_ge, tri_le, swap = (ca[:, i, :] for i in range(5))
        masks = cb[:, 0:14 * P].rearrange("p (d l m) -> p d l m", d=2, l=LEVELS)
        rope_c = cb[:, 14 * P:14 * P + SEQ]
        rope_s = cb[:, 14 * P + SEQ:14 * P + 2 * SEQ]
        X = at("X", 100, [KT, T])
        g_hi = at("g_hi", 124, [8, T], F32R)
        g_lo = at("g_lo", 148, [8, T], F32R)
        Y = at("Y", 172, [KT, T])
        sg = at("sg", 196, [T])
        gt = at("gt", 199, [T])
        n_sq = at("n_sq", 124, [2, T])
        n_acc = at("n_acc", 130, [T])
        n_rs = at("n_rs", 133, [T])
        n_t = at("n_t", 136, [2, T])
        n_t2 = at("n_t2", 142, [2, T])
        o_at = at("o_at", 100, [H, SEQ])
        a_kt = at("a_kt", 132, [HKV, T])
        a_v = at("a_v", 138, [NCH, HKV, P])
        a_vc = at("a_vc", 144, [NCH, P])
        a_raw = at("a_raw", 147, [T])
        a_sq = at("a_sq", 150, [T])
        a_rs = at("a_rs", 153, [T])
        a_n = at("a_n", 156, [T])
        a_t1 = at("a_t1", 159, [SEQ])
        a_t2 = at("a_t2", 161, [SEQ])
        a_q = at("a_q", 163, [SEQ])
        a_p = at("a_p", 165, [2, T])
        a_pt = at("a_pt", 171, [NCH, SEQ])
        a_m = at("a_m", 183, [3, 4])
        ba = at("ba", 184, [T])
        bx = at("bx", 187, [T])
        bt = at("bt", 190, [2, T])
        bg = at("bg", 196, [NCH, 48])
        bgt = at("bgt", 197.25, [3, 96])
        o_dn = at("o_dn", 116, [H, SEQ])
        M6 = NCH * P
        d_l = at("d_l", 132, [2, NCH, P])
        d_t = at("d_t", 138, [2, NCH, P])
        d_r = at("d_r", 144, [2, NCH, P])
        d_q = at("d_q", 150, [2, NCH, P])
        d_s = [at(f"d_s{i}", 156 + 6 * i, [2, NCH, P]) for i in range(2)]
        d_kd = at("d_kd", 168, [2, NCH, P])
        d_rs = at("d_rs", 168, [SEQ + T])
        d_at = at("d_at", 174, [2, NC_X, P])
        d_qd = at("d_qd", 178, [2, NC_X, P])
        d_ktok = at("d_ktok", 182, [NCH, P])
        d_vtok = at("d_vtok", 185, [NCH, P])
        d_sq = at("d_sq", 182, [SEQ + T])
        d_c = at("d_c", 188, [3, T + 2])
        d_up = at("d_up", 197.125, [T + 4])
        d_z = at("d_z", 200.25, [SEQ])
        d_st = at("d_st", 202.25, [2, P])
        d_vn = at("d_vn", 203.25, [2, P])
        d_o = at("d_o", 204.25, [SEQ])
        hc = at("hc", 206.25, [NG])
        odn_hi = at("odn_hi", 132, [H, SEQ], F32R)
        odn_lo = at("odn_lo", 148, [H, SEQ], F32R)
        oat_hi = at("oat_hi", 164, [H, SEQ], F32R)
        oat_lo = at("oat_lo", 180, [H, SEQ], F32R)
        m_hi = at("m_hi", 100, [KT, SEQ], F32R)
        m_lo = at("m_lo", 116, [KT, SEQ], F32R)
        m_a = at("m_a", 196, [SEQ])
        m_b = at("m_b", 198, [SEQ])
        m_s = at("m_s", 200, [2, SEQ])
        y_o = at("y_o", 132, [KT, SEQ])

        ps = ctx.enter_context(nc.psum_tensor("ps", [P, 8, 512], F32))

        S = {}

        def s(name):
            if name not in S:
                S[name] = sem(name)
            return S[name]

        w_loaded = [s(f"w_loaded{i}") for i in range(RING)]
        wmod_loaded = [s(f"wmod_loaded{i}") for i in range(2)]
        psum_read = [s(f"psum_read{i}") for i in range(2)]

        segs_all = [(0, CTX, 0), (CTX, T, 1)]
        segs_x = [(CTX, T, 1)]

        def bank(blk, seg):
            b = 2 * blk.pair + seg
            return ps[:, b, 0:(CTX, SEQ)[seg]]

        def loop(eng, iters, body, peel=False):
            if iters - peel > 0:
                with eng.Fori(0, iters - peel, 1) as it:
                    body(it)
            if peel:
                body(iters - 1)

        def all_read(eng, blocks):
            for p_ in range(2):
                eng.wait_ge(psum_read[p_], (blocks + 1 - p_) // 2 + 1)

        def ffn_parts(b0):
            b, hid = b0, 0
            for c, n in enumerate(FCH):
                yield "up", b, 2 * n, c, hid
                b += 2 * n
                yield "down", b, KT, c, hid
                b += KT
                hid += n


        block = ctx.enter_context(nc.Block())

        @block.sync
        def _(sp):
            sp.dma_start(vec[:], VEC).then_inc(s("tables_loaded"), 16)
            sp.dma_start(X[:], XT.rearrange("(k p) t -> p k t", p=P)).then_inc(s("x_loaded"), 16)
            sp.dma_start(ca[:], CA).then_inc(s("ca_loaded"), 16)
            sp.dma_start(gall[:, :, 0:9], CONV).then_inc(s("conv_loaded"), 16)
            Wv = W.rearrange("b p (k n) -> b p k n", k=KT)
            for b in range(RING):
                sp.dma_start(raw[:, b], Wv[b]).then_inc(w_loaded[b], 16)

            def load(n, slot):
                sp.wait_ge(s("w_split"), n - RING + 1)
                sp.dma_start(raw[:, slot], Wv[bass.ds(n, 1)].rearrange("b p k n -> p (b k) n"))\
                  .then_inc(w_loaded[slot], 16)

            with sp.Fori(0, NBLK // RING - 1, 1) as it:
                for j in range(RING):
                    load(it * RING + (RING + j), j)
            for n in range(NBLK // RING * RING, NBLK):
                load(n, n % RING)
            sp.wait_ge(s("x_new"), 3 * KT)
            sp.dma_start(OUT.rearrange("(k p) t -> p k t", p=P), X[:, :, CTX:T]).then_inc(s("stored"), 16)
            sp.wait_ge(s("stored"), 16)

        @block.gpsimd
        def _(g):
            g.sem_inc(psum_read[0], 1)
            g.sem_inc(psum_read[1], 1)
            g.sem_inc(s("g_ready"), 1)
            g.sem_inc(s("o_at"), 1)
            g.sem_inc(s("head_done"), 1)

            Mv = WMOD.rearrange("u p (k n) -> u p k n", k=KT)
            for u in range(2):
                g.dma_start(w_mod[:, u], Mv[u]).then_inc(wmod_loaded[u], 16)
            with g.Fori(0, N_MOD // 2 - 1, 1) as it:
                for u in range(2):
                    g.wait_ge(s("mod_mm"), it * 2 + (u + 1))
                    g.dma_start(w_mod[:, u], Mv[bass.ds(it * 2 + (2 + u), 1)].rearrange("b p k n -> p (b k) n"))\
                     .then_inc(wmod_loaded[u], 16)
            g.wait_ge(s("mod_mm"), N_MOD)
            g.dma_start(cb[:], CB).then_inc(s("cb_loaded"), 16)
            g.wait_ge(s("h_ready"), 2 * KT)
            g.dma_start(XS, X[:, :, CTX:T]).then_inc(s("x_spilled"), 16)
            g.wait_ge(s("x_spilled"), 16)
            g.wait_ge(s("cb_loaded"), 16)
            g.wait_ge(s("o_at"), H + 1)
            g.memset(d_up[:], 0.0).then_inc(s("d_up0"), 1)

            def bc(x):
                return x.unsqueeze(2).to_broadcast([P, x.shape[1], P])

            def head(h):
                for d in range(2):
                    g.wait_ge(s("d_e1"), h * 2 + (d + 1))
                    g.tensor_tensor(d_t[:, d], d_t[:, d], bc(hc[:, G_BETA + 6 * d:G_BETA + 6 * d + 6]), ALU.mult)\
                     .then_inc(s("d_eb"), 1)
                for d in range(2):
                    g.wait_ge(s("d_l"), h * 2 + (d + 1))
                    g.tensor_tensor(d_s[0][:, d], d_l[:, d], masks[:, d, 0, :].unsqueeze(1).to_broadcast([P, NCH, P]),
                                    ALU.mult).then_inc(s("lvl"), 1)
                for d in range(2):
                    g.wait_ge(s("d_am"), h * 2 + (d + 1))
                    tri = (tri_le, tri_ge)[d]
                    g.tensor_tensor(d_at[:, d], d_at[:, d], tri.unsqueeze(1).to_broadcast([P, NC_X, P]),
                                    ALU.mult).then_inc(s("d_at"), 1)
                for lv in range(1, LEVELS):
                    for d in range(2):
                        if lv == 2:
                            g.wait_ge(s("sv_r"), h * 28 + 1)
                        if lv > 1:
                            g.wait_ge(s("sv_q"), h * 28 + 4 * (lv - 2) + 2 * d + 2)
                        g.tensor_tensor(d_s[lv % 2][:, d], d_l[:, d],
                                        masks[:, d, lv, :].unsqueeze(1).to_broadcast([P, NCH, P]),
                                        ALU.mult).then_inc(s("lvl"), 1)
                    if lv == 1:
                        for d in range(2):
                            g.wait_ge(s("d_qe"), h * 2 + (d + 1))
                            g.tensor_tensor(d_qd[:, d], d_qd[:, d],
                                            d_c[:, 0, CTX + 2:T + 2].rearrange("p (c n) -> p c n", c=NC_X),
                                            ALU.mult).then_inc(s("d_qd"), 1)
                        g.wait_ge(s("d_tokc"), h * 2 + 2)
                    if lv == 2:
                        for d in range(2):
                            g.tensor_tensor(d_kd[:, d], d_ktok[:], bc(hc[:, G_KD + 6 * d:G_KD + 6 * d + 6]),
                                            ALU.mult).then_inc(s("d_kd"), 1)
                g.wait_ge(s("lvl"), h * 14 + 14)
                for d in range(2):
                    g.tensor_tensor(d_l[:, d], d_vtok[:], bc(hc[:, G_BETA + 6 * d:G_BETA + 6 * d + 6]),
                                    ALU.mult).then_inc(s("d_kbvb"), 1)
                g.wait_ge(s("sv_q"), h * 28 + 24)
                for d in range(2):
                    g.tensor_tensor(d_s[1][:, d], d_ktok[:], bc(hc[:, G_BEG + 6 * d:G_BEG + 6 * d + 6]),
                                    ALU.mult).then_inc(s("d_kbvb"), 1)

            with g.Fori(0, H, 1) as h:
                head(h)
            g.wait_ge(s("gemm_done"), B_OUT + KT)
            g.dma_start(X[:, :, CTX:T], XS).then_inc(s("x_back"), 16)
            g.wait_ge(s("x_back"), 16)

        @block.scalar
        def _(a):
            zero, one, eps, eps_q = (small[:, i:i + 1] for i in range(4))

            def split(b):
                a.wait_ge(w_loaded[b.raw], (b.load + 1) * 16)
                a.activation(w_hi[:, b.pair], raw[:, b.raw], ACT.Copy).then_inc(s("w_hi"), 1)

            def step(b):
                a.wait_ge(s("gemm_done"), b.n + 1)
                if not (isinstance(b.n, int) and b.n + 2 >= NBLK):
                    split(b.ahead(2))

            def read_out(b, dst, seg_list, func=ACT.Copy):
                for lo, hi, sg_ in seg_list:
                    last = a.activation(dst(lo, hi), bank(b, sg_), func)
                last.then_inc(psum_read[b.pair], 1)

            def sumsq(r, src, lo):
                for k in range(KT):
                    if r or k >= 2:
                        a.wait_ge(s("sq_used"), KT * r + k - 1)
                    a.activation(n_sq[:, k % 2, lo:T], src(k), ACT.Square).then_inc(s("sq_ready"), 1)
                a.wait_ge(s("ss_ready"), r + 1)
                segs = segs_all if lo == 0 else segs_x
                for l, h_, sg_ in segs:
                    last = a.activation(n_rs[:, l:h_], ps[:, 4 + sg_, 0:h_ - l], ACT.Sqrt, bias=eps, scale=1.0 / D)
                last.then_inc(s("std_ready"), 1)

            def pre_norm(r, p, lo):
                sumsq(r, lambda k: X[:, k, lo:T], lo)
                mi = (0, 3, 6)[p]
                for k in range(KT):
                    a.wait_ge(s("nrm_ready"), KT * p + k + 1)
                    for l, h_, sg_ in (segs_all if lo == 0 else segs_x):
                        last = a.activation(h_hi[:, k, l:h_], n_t[:, k % 2, l:h_], ACT.Identity,
                                            bias=mod[:, 8 * mi + k, sg_:sg_ + 1], scale=drv[:, 2 * p, k, sg_:sg_ + 1])
                    last.then_inc(s("h_rounded"), 1)

            def ffn(i, b0, seg_list, peel_last):
                lo = seg_list[0][0]
                for kind, b, n, c, hid in ffn_parts(b0):
                    last_part = peel_last and kind == "down" and c == 2

                    def up(it):
                        for j in range(4):
                            blk = Blk(b, it, j)
                            step(blk)
                            if j % 2 == 0:
                                read_out(blk, lambda l, h_: sg[:, l:h_], seg_list, ACT.Silu)
                            else:
                                a.wait_ge(psum_read[blk.pair], blk.turn + 2)
                                p_ = it * 2 + j // 2
                                a.activation(g_hi[:, bass.ds(p_, 1), lo:T].rearrange("p a n -> p (a n)"), gt[:, lo:T],
                                             ACT.Copy).then_inc(s("g_rounded"), 1)

                    def down(it):
                        for j in range(4):
                            blk = Blk(b, it, j)
                            step(blk)
                            if c == 0:
                                read_out(blk, lambda l, h_: Y[:, bass.ds(it * 4 + j, 1), l:h_].rearrange("p a n -> p (a n)"),
                                         seg_list)
                    loop(a, n // 4, up if kind == "up" else down, last_part)

            a.wait_ge(s("small_set"), 1)
            a.wait_ge(s("tables_loaded"), 16)
            a.activation(silc[:], vec[:, V_C:V_C + 2 * KT].rearrange("p (k c) -> p k c", c=2), ACT.Silu).then_inc(s("silc"), 1)
            split(Blk(0, 0, 0))
            split(Blk(0, 0, 1))
            a.wait_ge(s("x_loaded"), 16)
            pre_norm(0, 0, 0)
            ffn(0, B_FFN1, segs_all, False)
            all_read(a, B_FFN1 + N_FFN)
            sumsq(1, lambda k: Y[:, k, :], 0)
            a.wait_ge(s("x_new"), KT)
            pre_norm(2, 1, 0)

            def item_norm(n, width):
                a.activation(a_sq[:, 0:width], a_raw[:, 0:width], ACT.Square).then_inc(s("at_sq"), 1)
                a.wait_ge(s("at_ss"), n + 1)
                if width == T:
                    a.activation(a_rs[:, 0:CTX], ps[:, 4, 0:CTX], ACT.Sqrt, bias=eps, scale=1.0 / DH)
                    a.activation(a_rs[:, CTX:T], ps[:, 5, 0:SEQ], ACT.Sqrt, bias=eps, scale=1.0 / DH).then_inc(s("at_std"), 1)
                else:
                    a.activation(a_rs[:, 0:SEQ], ps[:, 4, 0:SEQ], ACT.Sqrt, bias=eps, scale=1.0 / DH).then_inc(s("at_std"), 1)

            for j in range(2):
                blk = Blk(B_KV, 0, j)
                step(blk)
                if j:
                    a.wait_ge(s("at_nrm"), j)
                read_out(blk, lambda l, h_: a_raw[:, l:h_], segs_all)
                a.wait_ge(psum_read[blk.pair], blk.turn + 2)
                item_norm(j, T)
            for j in range(2, 4):
                blk = Blk(B_KV, 0, j)
                step(blk)
                a.wait_ge(s("at_nrm"), 2)
                if j == 3:
                    a.wait_ge(s("at_vt"), 1)
                read_out(blk, lambda l, h_: a_raw[:, l:h_], segs_all)
                a.wait_ge(s("at_vt"), j - 1)
                a.activation(a_v[:, :, j - 2, :].rearrange("p (b c) n -> p b c n", b=2),
                             ps[:, 6:8, 0:384].rearrange("p b (c n) -> p b c n", c=3), ACT.Copy).then_inc(s("at_vc"), 1)
            blk = Blk(B_KV, 0, 4)
            step(blk)
            read_out(blk, lambda l, h_: ba[:, l:h_], segs_all)
            a.wait_ge(psum_read[blk.pair], blk.turn + 2)
            a.activation(bt[0:16, 0, :], ba[0:16, :], ACT.Exp, scale=-1.0).then_inc(s("ba_e"), 1)
            a.activation(small[32:48, 8:9], vec[32:48, V_ALOG:V_ALOG + 1], ACT.Exp).then_inc(s("ba_e"), 1)
            a.wait_ge(s("ba_abs"), 2)
            a.activation(bt[32:48, 0, :], bt[32:48, 0, :], ACT.Exp, scale=-1.0).then_inc(s("ba_e"), 1)
            a.wait_ge(s("ba_e"), 3)
            a.activation(bt[32:48, 0, :], bt[32:48, 0, :], ACT.Ln, bias=one[32:48]).then_inc(s("ba_e"), 1)
            a.wait_ge(s("ba_gc"), 1)
            a.activation(bgt[:, 1, :], bgt[:, 0, :], ACT.Exp).then_inc(s("ba_x"), 1)
            a.wait_ge(s("ba_gt"), 1)
            for d in range(2):
                a.activation(gall[:, :, G_DCY + 6 * d:G_DCY + 6 * d + 6],
                             ps[:, 6, 96:192].rearrange("p (c e h) -> p e h c", c=NCH, e=2)[:, d], ACT.Exp)\
                 .then_inc(s("ba_x"), 1)
            a.activation(bgt[:, 2, :], bgt[:, 2, :], ACT.Exp).then_inc(s("ba_x"), 1)

            def heads(it):
                a.wait_ge(s("o_at"), it * 4 + 1)
                a.activation(a_vc[:], a_v[:, :, bass.ds(it, 1), :].rearrange("p c a n -> p (c a) n"),
                             ACT.Copy).then_inc(s("at_vcur"), 1)
                for j in range(4):
                    n = it * 4 + j
                    blk = Blk(B_Q, it, j)
                    step(blk)
                    a.wait_ge(s("at_nrm"), n + 2)
                    a.activation(a_raw[:, 0:SEQ], bank(blk, 1), ACT.Copy).then_inc(psum_read[blk.pair], 1)
                    a.wait_ge(psum_read[blk.pair], blk.turn + 2)
                    item_norm(n + 2, SEQ)
                    def evac_pt(t):
                        a.wait_ge(s("at_tr"), n * 4 + (t + 1))
                        a.activation(a_pt[:, :, P * t:P * t + P].rearrange("p (b c) n -> p b c n", b=2),
                                     ps[:, 0:3:2, 0:384].rearrange("p b (c n) -> p b c n", c=3), ACT.Copy)\
                         .then_inc(s("at_pt"), 1)
                    for t in range(4):
                        a.wait_ge(s("at_max"), n * 4 + (t + 1))
                        a.activation(a_p[:, t % 2, :].rearrange("p (b n) -> p b n", b=2),
                                     ps[:, 4 + 2 * (t % 2):6 + 2 * (t % 2), 0:384],
                                     ACT.Exp, bias=a_m[:, 1, t:t + 1], scale=DH ** -0.5,
                                     accum_out=a_m[:, 2, t:t + 1]).then_inc(s("at_p"), 1)
                        if t:
                            evac_pt(t - 1)
                    evac_pt(3)
                    a.wait_ge(s("at_pv"), n + 1)
                    a.activation(o_at[:, bass.ds(n, 1), :].rearrange("p a n -> p (a n)"), ps[:, 4, 0:SEQ], ACT.Copy)\
                     .then_inc(s("o_at"), 1)
            a.wait_ge(s("x_spilled"), 16)
            loop(a, 2, heads)

            def dn_head(h):
                b = [Blk(B_DN, h, j) for j in range(4)]
                step(b[0])
                a.wait_ge(s("head_done"), h + 1)
                a.activation(d_up[:, CTX + 3:T + 3], bank(b[0], 1), ACT.Copy).then_inc(psum_read[b[0].pair], 1)
                for j in (1, 2):
                    step(b[j])
                    a.wait_ge(s("conv"), h * 3 + j)
                    a.activation(d_up[:, 1:CTX + 1], bank(b[j], 0), ACT.Copy)
                    a.activation(d_up[:, CTX + 3:T + 3], bank(b[j], 1), ACT.Copy).then_inc(psum_read[b[j].pair], 1)
                step(b[3])
                a.activation(d_z[:], bank(b[3], 1), ACT.Silu).then_inc(psum_read[b[3].pair], 1)
                a.activation(d_c[:, 0, CTX + 2:], d_c[:, 0, CTX + 2:], ACT.Silu)
                a.activation(d_c[:, 1, 0:CTX], d_c[:, 1, 0:CTX], ACT.Silu)
                a.activation(d_c[:, 1, CTX + 2:], d_c[:, 1, CTX + 2:], ACT.Silu).then_inc(s("d_silu"), 1)
                a.wait_ge(s("conv"), h * 3 + 3)
                a.activation(d_c[:, 2, :], d_c[:, 2, :], ACT.Silu).then_inc(s("d_silu"), 1)
                a.wait_ge(s("d_silu"), h * 2 + 1)
                a.activation(d_sq[:, 0:SEQ], d_c[:, 0, CTX + 2:], ACT.Square)
                a.activation(d_sq[:, SEQ:SEQ + CTX], d_c[:, 1, 0:CTX], ACT.Square)
                a.activation(d_sq[:, SEQ + CTX:], d_c[:, 1, CTX + 2:], ACT.Square).then_inc(s("d_sq"), 1)
                a.wait_ge(s("d_ss"), h + 1)
                a.activation(d_rs[:, 0:SEQ], ps[:, 4, :], ACT.Sqrt, bias=eps_q, scale=float(DH))
                a.activation(d_rs[:, SEQ:SEQ + CTX], ps[:, 5, 0:CTX], ACT.Sqrt, bias=eps)
                a.activation(d_rs[:, SEQ + CTX:], ps[:, 6, :], ACT.Sqrt, bias=eps).then_inc(s("d_std"), 1)
                for i, dst in enumerate((d_ktok, d_vtok)):
                    a.wait_ge(s("d_tok"), h * 2 + (i + 1))
                    a.activation(dst[:].rearrange("p (b c) n -> p b (c n)", b=2), ps[:, 2 * i:2 * i + 2, 0:384], ACT.Copy)\
                     .then_inc(s("d_tokc"), 1)
                for d in range(2):
                    a.wait_ge(s("d_mn"), h * 4 + 2 * d + 1)
                    a.activation(d_t[:, d], d_t[:, d], ACT.Exp).then_inc(s("d_e1"), 1)
                    a.wait_ge(s("d_mn"), h * 4 + 2 * d + 2)
                    a.activation(d_r[:, d, 0:NC_X], d_r[:, d, 0:NC_X], ACT.Exp, scale=-1.0).then_inc(s("d_e2"), 1)
                    a.activation(d_qd[:, d, 0], ps[:, 2 * d, 2 * P:3 * P], ACT.Exp)
                    a.activation(d_qd[:, d, 1:NC_X].rearrange("p c n -> p (c n)"), ps[:, 2 * d + 1, 0:384], ACT.Exp)\
                     .then_inc(s("d_qe"), 1)
                for lv in range(1, LEVELS):
                    for gr in range(4):
                        d, hf = gr // 2, gr % 2
                        a.wait_ge(s("sv_q"), h * 28 + 4 * lv + gr + 1)
                        a.activation(d_q[:, d, 3 * hf:3 * hf + 3].rearrange("p c n -> p (c n)"), ps[:, 4 + gr, 0:384],
                                     ACT.Copy).then_inc(s("sv_qc"), 1)
                for gr in range(4):
                    d, hf = gr // 2, gr % 2
                    a.wait_ge(s("uw"), h * 4 + gr + 1)
                    a.activation(d_q[:, d, 3 * hf:3 * hf + 3].rearrange("p c n -> p (c n)"), ps[:, 4 + gr, 0:384],
                                 ACT.Copy).then_inc(s("u_c"), 1)
                a.wait_ge(s("sc_o"), h * 8 + 8)
                a.activation(d_o[:], ps[:, 0, :], ACT.Copy).then_inc(s("od_copy"), 1)
                a.wait_ge(s("od_sum"), h + 1)
                a.activation(d_sq[:, 0:SEQ], d_o[:], ACT.Square).then_inc(s("od_sq"), 1)
                a.wait_ge(s("od_ss"), h + 1)
                a.activation(d_rs[:, 0:SEQ], ps[:, 2, :], ACT.Sqrt, bias=eps, scale=1.0 / DH).then_inc(s("od_std"), 1)
            a.wait_ge(s("d_up0"), 1)
            loop(a, H, dn_head)

            a.wait_ge(s("head_done"), H + 1)
            for src, dst in ((o_dn, odn_hi), (o_at, oat_hi)):
                a.activation(dst[:], src[:], ACT.Copy).then_inc(s("o_rounded"), 1)

            def merge(it):
                for j in range(4):
                    blk = Blk(B_MERGE, it, j)
                    step(blk)
                    dst = (m_a[:], m_s[:, 0, :], m_b[:], m_s[:, 1, :])[j]
                    if j < 2:
                        a.wait_ge(s("merged"), it + 1)
                    if j == 2:
                        a.wait_ge(s("gated"), it * 2 + 1)
                    read_out(blk, lambda l, h_: dst, segs_x, ACT.Sigmoid if j % 2 else ACT.Copy)
                a.wait_ge(s("merged"), it + 2)
                a.activation(m_hi[:, bass.ds(it, 1), :].rearrange("p a n -> p (a n)"), m_b[:], ACT.Copy).then_inc(s("m_rounded"), 1)
            loop(a, KT, merge)

            def out_proj(it):
                for j in range(4):
                    blk = Blk(B_OUT, it, j)
                    step(blk)
                    read_out(blk, lambda l, h_: Y[:, bass.ds(it * 4 + j, 1), l:h_].rearrange("p a n -> p (a n)"), segs_x)
            a.wait_ge(s("gemm_done"), B_OUT)
            loop(a, KT // 4, out_proj)
            all_read(a, B_OUT + KT)
            sumsq(3, lambda k: Y[:, k, CTX:T], CTX)
            a.wait_ge(s("x_new"), 2 * KT)
            pre_norm(4, 2, CTX)
            ffn(1, B_FFN2, segs_x, True)
            all_read(a, NBLK)
            sumsq(5, lambda k: Y[:, k, CTX:T], CTX)

        @block.vector
        def _(v):
            def split(b):
                v.wait_ge(s("w_hi"), b.n + 1)
                v.tensor_tensor(w_lo[:, b.pair], raw[:, b.raw], w_hi[:, b.pair].bitcast(F32), ALU.subtract)\
                 .then_inc(s("w_split"), 1)

            def step(b):
                if not (isinstance(b.n, int) and b.n + 2 >= NBLK):
                    split(b.ahead(2))

            def mod_out(u, slot):
                v.wait_ge(s("mod_mm"), u + 1)
                if isinstance(u, int):
                    dst, bias = mod[:, u, :], vec[:, V_BMOD + u:V_BMOD + u + 1]
                else:
                    dst = mod[:, bass.ds(u, 1), :].rearrange("p a c -> p (a c)")
                    bias = vec[:, bass.ds(u + V_BMOD, 1)]
                v.tensor_scalar(dst, ps[:, 6 + slot, 0:2], bias, None, ALU.add).then_inc(s("mod_out"), 1)

            def derive(i, mi, vcol, add, mul):
                gain = vec[:, vcol:vcol + KT].unsqueeze(2).to_broadcast([P, KT, 2])
                return v.scalar_tensor_tensor(drv[:, i], mod[:, 8 * mi:8 * mi + 8, :], add if add else mul, gain,
                                              ALU.add if add else ALU.mult, ALU.mult)

            def rstd(r, lo):
                for k in range(KT):
                    v.wait_ge(s("sq_ready"), KT * r + k + 1)
                    if k == 0:
                        if r:
                            v.wait_ge(s("sq_used"), KT * r)
                        v.tensor_copy(n_acc[:, lo:T], n_sq[:, 0, lo:T]).then_inc(s("sq_used"), 1)
                    else:
                        v.wait_ge(s("sq_used"), KT * r + k)
                        v.tensor_tensor(n_acc[:, lo:T], n_acc[:, lo:T], n_sq[:, k % 2, lo:T], ALU.add).then_inc(s("sq_used"), 1)
                v.wait_ge(s("std_ready"), r + 1)
                v.reciprocal(n_rs[:, lo:T], n_rs[:, lo:T]).then_inc(s("rstd"), 1)
                v.wait_ge(s("rstd"), r + 1)

            def pre_norm(r, p, lo):
                rstd(r, lo)
                mi = (0, 3, 6)[p]
                segs = segs_all if lo == 0 else segs_x

                def low(k):
                    v.wait_ge(s("h_rounded"), KT * p + k + 1)
                    v.wait_ge(s("h_full"), KT * p + k + 1)
                    v.tensor_tensor(h_lo[:, k, lo:T], n_t2[:, k % 2, lo:T], h_hi[:, k, lo:T].bitcast(F32), ALU.subtract)\
                     .then_inc(s("h_ready"), 1)
                if p:
                    v.wait_ge(s("h_ready"), KT * p)
                for k in range(KT):
                    v.tensor_tensor(n_t[:, k % 2, lo:T], X[:, k, lo:T], n_rs[:, lo:T], ALU.mult).then_inc(s("nrm_ready"), 1)
                    if k:
                        low(k - 1)
                    else:
                        v.wait_ge(s("nrm_ready"), KT * p + k + 1)
                    v.wait_ge(s("nrm_ready"), KT * p + k + 1)
                    if k >= 2:
                        v.wait_ge(s("h_ready"), KT * p + k - 1)
                    for l, h_, sg_ in segs:
                        last = v.tensor_scalar(n_t2[:, k % 2, l:h_], n_t[:, k % 2, l:h_], drv[:, 2 * p, k, sg_:sg_ + 1],
                                               mod[:, 8 * mi + k, sg_:sg_ + 1], ALU.mult, ALU.add)
                    last.then_inc(s("h_full"), 1)
                low(KT - 1)

            def post_norm(r, p, lo):
                rstd(r, lo)
                v.wait_ge(s("h_ready"), KT * (p + 1))
                for k in range(KT):
                    if k >= 2:
                        v.wait_ge(s("x_new"), KT * p + k - 1)
                    v.tensor_tensor(n_t[:, k % 2, lo:T], Y[:, k, lo:T], n_rs[:, lo:T], ALU.mult).then_inc(s("yn"), 1)
                    v.wait_ge(s("yn"), KT * p + k + 1)
                    for l, h_, sg_ in (segs_all if lo == 0 else segs_x):
                        last = v.scalar_tensor_tensor(X[:, k, l:h_], n_t[:, k % 2, l:h_], drv[:, 2 * p + 1, k, sg_:sg_ + 1],
                                                      X[:, k, l:h_], ALU.mult, ALU.add)
                    last.then_inc(s("x_new"), 1)
                v.wait_ge(s("x_new"), KT * (p + 1))

            def ffn(i, b0, seg_list, peel_last, mod_from=None):
                lo = seg_list[0][0]
                u0 = mod_from
                pairs = i * HID
                ys = 2 * KT * i
                for kind, b, n, c, hid in ffn_parts(b0):
                    last_part = peel_last and kind == "down" and c == 2

                    def up(it, b=b, hid=hid, u0=u0):
                        for j in range(4):
                            blk = Blk(b, it, j)
                            step(blk)
                            if j % 2:
                                v.wait_ge(s("gemm_done"), blk.n + 1)
                                v.wait_ge(psum_read[1 - blk.pair], blk.ahead(-1).turn + 2)
                                v.wait_ge(s("g_ready"), it * 2 + (pairs + hid + j // 2 + 1))
                                for l, h_, sg_ in seg_list:
                                    last = v.tensor_tensor(gt[:, l:h_], sg[:, l:h_], bank(blk, sg_), ALU.mult)
                                last.then_inc(psum_read[blk.pair], 1)
                                p_ = it * 2 + j // 2
                                v.wait_ge(s("g_rounded"), it * 2 + (pairs + hid + j // 2 + 1))
                                v.tensor_tensor(g_lo[:, bass.ds(p_, 1), lo:T].rearrange("p a n -> p (a n)"), gt[:, lo:T],
                                                g_hi[:, bass.ds(p_, 1), lo:T].rearrange("p a n -> p (a n)").bitcast(F32),
                                                ALU.subtract).then_inc(s("g_ready"), 1)
                            if u0 is not None:
                                mod_out(it * 4 + (u0 + j), j % 2)

                    def down(it, b=b, c=c, u0=u0):
                        for j in range(4):
                            blk = Blk(b, it, j)
                            step(blk)
                            if c:
                                v.wait_ge(s("gemm_done"), blk.n + 1)
                                yk = Y[:, bass.ds(it * 4 + j, 1), :].rearrange("p a n -> p (a n)")
                                for l, h_, sg_ in seg_list:
                                    last = v.tensor_tensor(yk[:, l:h_], yk[:, l:h_], bank(blk, sg_), ALU.add)
                                last.then_inc(psum_read[blk.pair], 1)
                            if u0 is not None and j % 2:
                                mod_out(it * 2 + (u0 + j // 2), j // 2)
                    if kind == "down" and c:
                        all_read(v, b - 2 * FCH[c])
                    loop(v, n // 4, up if kind == "up" else down, last_part)
                    if u0 is not None:
                        u0 += n if kind == "up" else n // 2
                all_read(v, b0 + N_FFN)

            zero, one, eps, eps_q = (small[:, i:i + 1] for i in range(4))
            v.memset(zero, 0.0)
            v.memset(one, 1.0)
            v.memset(eps, EPS)
            v.memset(eps_q, EPS * DH).then_inc(s("small_set"), 1)
            v.wait_ge(s("tables_loaded"), 16)
            split(Blk(0, 0, 0))
            split(Blk(0, 0, 1))
            for u in range(2):
                mod_out(u, u)

            def mod_pair_out(it):
                for j in range(2):
                    mod_out(it * 2 + (2 + j), j)
            loop(v, 7, mod_pair_out)
            v.wait_ge(s("mod_out"), 16)
            derive(0, 1, V_PRE1, 1.0, None).then_inc(s("drv"), 1)
            v.wait_ge(s("drv"), 1)
            pre_norm(0, 0, 0)
            ffn(0, B_FFN1, segs_all, False, 16)
            v.wait_ge(s("mod_out"), N_MOD)
            derive(1, 2, V_POST1, None, 0.5)
            derive(2, 4, V_PREM, 1.0, None)
            derive(3, 5, V_POSTM, None, 1.0)
            derive(4, 7, V_PRE2, 1.0, None)
            derive(5, 8, V_POST2, None, 0.5).then_inc(s("drv"), 1)
            v.wait_ge(s("drv"), 2)
            post_norm(1, 0, 0)
            pre_norm(2, 1, 0)

            def item(n, width, gain, dst_x, dst_c=None, last=None):
                v.wait_ge(s("at_std"), n + 1)
                v.reciprocal(a_rs[:, 0:width], a_rs[:, 0:width]).then_inc(s("at_rs"), 1)
                v.wait_ge(s("at_rs"), n + 1)
                if dst_c is not None:
                    v.scalar_tensor_tensor(dst_c, a_raw[:, 0:CTX], gain, a_rs[:, 0:CTX], ALU.mult, ALU.mult)
                o = width - SEQ
                v.scalar_tensor_tensor(a_n[:, 0:SEQ], a_raw[:, o:width], gain, a_rs[:, o:width], ALU.mult, ALU.mult)\
                 .then_inc(s("at_nrm"), 1)
                v.wait_ge(s("at_nrm"), n + 1)
                if not (isinstance(n, int) and n == 0):
                    v.wait_ge(s("at_rot"), n)
                v.tensor_tensor(a_t1[:], a_n[:, 0:SEQ], rope_c, ALU.mult)
                bk = 6 if width == T else 5
                v.wait_ge(s("at_swap"), n + 1)
                v.tensor_tensor(a_t2[:], ps[:, bk, :], rope_s, ALU.mult).then_inc(s("at_t2"), 1)
                v.wait_ge(s("at_t2"), n + 1)
                v.tensor_tensor(dst_x, a_t1[:], a_t2[:], ALU.add).then_inc(s("at_rot"), 1)

            v.wait_ge(s("cb_loaded"), 16)
            for j in range(2):
                step(Blk(B_KV, 0, j))
                item(j, T, vec[:, V_KN:V_KN + 1], a_kt[:, j, CTX:T], a_kt[:, j, 0:CTX])
            for j in range(2, 5):
                step(Blk(B_KV, 0, j))
            v.memset(bx[:], 0.0).then_inc(s("ba_bx"), 1)
            blk = Blk(B_KV, 0, 4)
            v.wait_ge(psum_read[blk.pair], blk.turn + 2)
            v.wait_ge(s("ba_bx"), 1)
            v.tensor_scalar(ba[32:48, :], ba[32:48, :], vec[32:48, V_DT:V_DT + 1], None, ALU.add).then_inc(s("ba_abs"), 1)
            v.wait_ge(s("ba_abs"), 1)
            v.scalar_tensor_tensor(bt[32:48, 0, :], ba[32:48, :], -1.0, ba[32:48, :], ALU.mult, ALU.max).then_inc(s("ba_abs"), 1)
            v.wait_ge(s("ba_e"), 1)
            v.tensor_scalar(bt[0:16, 1, :], bt[0:16, 0, :], 1.0, None, ALU.add).then_inc(s("ba_v"), 1)
            v.wait_ge(s("ba_v"), 1)
            v.reciprocal(bx[0:16, :], bt[0:16, 1, :])
            v.wait_ge(s("ba_e"), 4)
            v.scalar_tensor_tensor(bt[32:48, 1, :], ba[32:48, :], 0.0, bt[32:48, 0, :], ALU.max, ALU.add).then_inc(s("ba_v"), 1)
            v.wait_ge(s("ba_v"), 2)
            v.tensor_scalar(bx[32:48, :], bt[32:48, 1, :], small[32:48, 8:9], -1.0, ALU.mult, ALU.mult).then_inc(s("ba_bx"), 1)
            v.wait_ge(s("ba_tr"), 1)
            v.tensor_copy(bg[:].rearrange("p (b c) n -> p b c n", b=2),
                          ps[:, 6:8, 0:384].rearrange("p b (c n) -> p b c n", c=3)[:, :, :, 0:48]).then_inc(s("ba_bg"), 1)
            v.wait_ge(s("ba_sum"), 1)
            v.tensor_copy(bgt[:, 0, :], ps[:, 6, 0:96]).then_inc(s("ba_gc"), 1)
            v.wait_ge(s("ba_gc"), 1)
            def hc_of(t, d):
                return t[:, 48 * d:48 * d + 48].rearrange("p (c h) -> p h c", c=NCH)
            for d in range(2):
                v.tensor_copy(gall[:, :, G_GC + 6 * d:G_GC + 6 * d + 6], hc_of(bgt[:, 0], d))
                last = v.tensor_copy(gall[:, :, G_BETA + 6 * d:G_BETA + 6 * d + 6],
                                     bg[:, :, 8 * d:8 * d + 8].rearrange("p c h -> p h c"))
            last.then_inc(s("ba_gc"), 1)
            for d in range(2):
                last = v.tensor_tensor(hc_of(bgt[:, 2], d),
                                       ps[:, 6, 96:192].rearrange("p (c e h) -> p e h c", c=NCH, e=2)[:, d],
                                       hc_of(bgt[:, 0], d), ALU.subtract)
            last.then_inc(s("ba_gt"), 1)
            v.wait_ge(s("ba_x"), 1)
            v.wait_ge(s("ba_gc"), 2)
            for d in range(2):
                last = v.tensor_tensor(gall[:, :, G_BEG + 6 * d:G_BEG + 6 * d + 6],
                                       gall[:, :, G_BETA + 6 * d:G_BETA + 6 * d + 6], hc_of(bgt[:, 1], d), ALU.mult)
            v.wait_ge(s("ba_x"), 4)
            for d in range(2):
                last = v.tensor_copy(gall[:, :, G_KD + 6 * d:G_KD + 6 * d + 6], hc_of(bgt[:, 2], d))
            last.then_inc(s("gall"), 1)

            def heads(it):
                for j in range(4):
                    n = it * 4 + j
                    step(Blk(B_Q, it, j))
                    item(n + 2, SEQ, vec[:, V_QN:V_QN + 1], a_q[:])
                    for t in range(4):
                        v.wait_ge(s("at_s"), n * 4 + (t + 1))
                        v.tensor_reduce(out=a_m[:, 0, t:t + 1], in_=ps[:, 4 + 2 * (t % 2):6 + 2 * (t % 2), 0:384],
                                        op=ALU.max, axis=AX.XY).then_inc(s("at_mx"), 1)
                        v.wait_ge(s("at_mx"), n * 4 + (t + 1))
                        v.tensor_scalar(a_m[:, 1, t:t + 1], a_m[:, 0, t:t + 1], -DH ** -0.5, None, ALU.mult)\
                         .then_inc(s("at_max"), 1)
                        v.wait_ge(s("at_p"), n * 4 + (t + 1))
                        v.reciprocal(a_m[:, 2, t:t + 1], a_m[:, 2, t:t + 1]).then_inc(s("at_rc"), 1)
                        v.wait_ge(s("at_rc"), n * 4 + (t + 1))
                        v.tensor_scalar(a_p[:, t % 2, :], a_p[:, t % 2, :], a_m[:, 2, t:t + 1], None, ALU.mult)\
                         .then_inc(s("at_pn"), 1)
            loop(v, 2, heads)

            def bc(x):
                return x.unsqueeze(2).to_broadcast([P, x.shape[1], P])

            v.wait_ge(s("gall"), 1)
            v.wait_ge(s("d_up0"), 1)

            def dn_head(h):
                b = [Blk(B_DN, h, j) for j in range(4)]
                v.wait_ge(s("head_done"), h + 1)
                v.tensor_copy(hc[:], gall[:, bass.ds(h, 1), :].rearrange("p a n -> p (a n)")).then_inc(s("hc"), 1)
                v.wait_ge(s("hc"), h + 1)
                for j in range(3):
                    step(b[j])
                    v.wait_ge(psum_read[b[j].pair], b[j].turn + 2)
                    lo = CTX + 2 if j == 0 else 0
                    n = T + 2 - lo
                    c = d_c[:, j, lo:]
                    tap = [hc[:, 3 * j + i:3 * j + i + 1] for i in range(3)]
                    v.tensor_scalar(c, d_up[:, lo:lo + n], tap[0], None, ALU.mult).then_inc(s("tap"), 1)
                    v.wait_ge(s("tap"), h * 6 + 2 * j + 1)
                    v.scalar_tensor_tensor(c, d_up[:, lo + 1:lo + 1 + n], tap[1], c, ALU.mult, ALU.add).then_inc(s("tap"), 1)
                    v.wait_ge(s("tap"), h * 6 + 2 * j + 2)
                    v.scalar_tensor_tensor(c, d_up[:, lo + 2:lo + 2 + n], tap[2], c, ALU.mult, ALU.add).then_inc(s("conv"), 1)
                step(b[3])
                v.wait_ge(s("d_std"), h + 1)
                v.reciprocal(d_rs[:], d_rs[:]).then_inc(s("d_rcp"), 1)
                v.wait_ge(s("d_rcp"), h + 1)
                v.tensor_tensor(d_c[:, 0, CTX + 2:], d_c[:, 0, CTX + 2:], d_rs[:, 0:SEQ], ALU.mult)
                v.tensor_tensor(d_c[:, 1, 0:CTX], d_c[:, 1, 0:CTX], d_rs[:, SEQ:SEQ + CTX], ALU.mult)
                v.tensor_tensor(d_c[:, 1, CTX + 2:], d_c[:, 1, CTX + 2:], d_rs[:, SEQ + CTX:], ALU.mult).then_inc(s("d_qk"), 1)
                for d in range(2):
                    v.wait_ge(s("d_row"), h * 2 + (d + 1))
                    v.tensor_tensor(d_q[:, d].rearrange("p (b c) n -> p b c n", b=2),
                                    hc[:, G_GC + 6 * d:G_GC + 6 * d + 6].rearrange("p (b c) -> p b c", b=2)
                                    .unsqueeze(3).to_broadcast([P, 2, 3, P]),
                                    ps[:, 2 * d:2 * d + 2, 0:384].rearrange("p b (c n) -> p b c n", c=3), ALU.subtract)\
                     .then_inc(s("d_diff"), 1)
                    v.wait_ge(s("d_diff"), h * 2 + (d + 1))
                    v.tensor_scalar(d_t[:, d], d_q[:, d], 0.0, None, ALU.min).then_inc(s("d_mn"), 1)
                    v.tensor_scalar(d_r[:, d, 0:NC_X], d_q[:, d, NC_CTX:], 0.0, None, ALU.max).then_inc(s("d_mn"), 1)
                for d in range(2):
                    v.wait_ge(s("d_eb"), h * 2 + (d + 1))
                    v.wait_ge(s("d_kk"), h + 1)
                    v.tensor_tensor(d_l[:, d].rearrange("p (b c) n -> p b (c n)", b=2),
                                    d_t[:, d].rearrange("p (b c) n -> p b (c n)", b=2), ps[:, 4:6, 0:384], ALU.mult)\
                     .then_inc(s("d_l"), 1)
                for d in range(2):
                    v.wait_ge(s("d_e2"), h * 2 + (d + 1))
                    v.tensor_tensor(d_at[:, d].rearrange("p c n -> p (c n)"), d_r[:, d, 0:NC_X].rearrange("p c n -> p (c n)"),
                                    ps[:, 6, :], ALU.mult).then_inc(s("d_am"), 1)
                for d in range(2):
                    v.wait_ge(s("lvl"), h * 14 + d + 1)
                    v.tensor_tensor(d_t[:, d], ident.unsqueeze(1).to_broadcast([P, NCH, P]), d_s[0][:, d], ALU.subtract)
                for gr in range(4):
                    d, hf = gr // 2, gr % 2
                    v.wait_ge(s("sv_q"), h * 28 + gr + 1)
                    v.tensor_tensor(d_r[:, d, 3 * hf:3 * hf + 3], ident.unsqueeze(1).to_broadcast([P, 3, P]),
                                    ps[:, 4 + gr, 0:384].rearrange("p (c n) -> p c n", c=3), ALU.subtract)\
                     .then_inc(s("sv_r"), 1)
                for lv in range(1, LEVELS):
                    for gr in range(4):
                        d, hf = gr // 2, gr % 2
                        v.wait_ge(s("sv_d"), h * 24 + 4 * (lv - 1) + gr + 1)
                        r_ = d_r[:, d, 3 * hf:3 * hf + 3].rearrange("p c n -> p (c n)")
                        t_ = d_t[:, d, 3 * hf:3 * hf + 3].rearrange("p c n -> p (c n)")
                        if lv < LEVELS - 1:
                            v.tensor_tensor(t_, t_, ps[:, gr, 0:384], ALU.subtract)
                        v.tensor_tensor(r_, r_, ps[:, 4 + gr, 0:384], ALU.subtract).then_inc(s("sv_r"), 1)
                for gr in range(4):
                    d, hf = gr // 2, gr % 2
                    v.wait_ge(s("uw"), h * 4 + gr + 1)
                    v.tensor_copy(d_t[:, d, 3 * hf:3 * hf + 3].rearrange("p c n -> p (c n)"), ps[:, gr, 0:384])\
                     .then_inc(s("w_c"), 1)
                v.wait_ge(s("u_c"), h * 4 + 4)
                for t in range(NCH):
                    for d in range(2):
                        c = ORDER[d][t]
                        if t:
                            v.wait_ge(s("sc_w"), h * 10 + 2 * (t - 1) + d + 1)
                            v.tensor_tensor(d_vn[:, d], d_q[:, d, c], ps[:, 4 + d, 0:P], ALU.subtract).then_inc(s("sc_v"), 1)
                    if t < NCH - 1:
                        for d in range(2):
                            c = ORDER[d][t]
                            v.wait_ge(s("sc_s"), h * 10 + 2 * t + d + 1)
                            if t == 0:
                                v.tensor_copy(d_st[:, d], ps[:, 6 + d, 0:P]).then_inc(s("sc_st"), 1)
                            else:
                                v.scalar_tensor_tensor(d_st[:, d], d_st[:, d], hc[:, G_DCY + 6 * d + c:G_DCY + 6 * d + c + 1],
                                                       ps[:, 6 + d, 0:P], ALU.mult, ALU.add).then_inc(s("sc_st"), 1)
                v.wait_ge(s("od_copy"), h + 1)
                v.tensor_tensor(d_o[:], d_o[:], ps[:, 1, :], ALU.add).then_inc(s("od_sum"), 1)
                v.wait_ge(s("od_std"), h + 1)
                v.reciprocal(d_rs[:, 0:SEQ], d_rs[:, 0:SEQ]).then_inc(s("od_v"), 1)
                v.wait_ge(s("od_v"), h * 2 + 1)
                v.scalar_tensor_tensor(d_o[:], d_o[:], vec[:, V_DN:V_DN + 1], d_rs[:, 0:SEQ], ALU.mult, ALU.mult)\
                 .then_inc(s("od_v"), 1)
                v.wait_ge(s("od_v"), h * 2 + 2)
                v.tensor_tensor(o_dn[:, bass.ds(h, 1), :].rearrange("p a n -> p (a n)"), d_o[:], d_z[:], ALU.mult)\
                 .then_inc(s("head_done"), 1)
            loop(v, H, dn_head)

            for i, (src, hi, lo) in enumerate(((o_dn, odn_hi, odn_lo), (o_at, oat_hi, oat_lo))):
                v.wait_ge(s("o_rounded"), i + 1)
                v.tensor_tensor(lo[:], src[:], hi[:].bitcast(F32), ALU.subtract).then_inc(s("o_split"), 1)
            v.wait_ge(s("o_split"), 2)
            v.sem_inc(s("merged"), 1)

            def merge(it):
                for j in range(4):
                    blk = Blk(B_MERGE, it, j)
                    step(blk)
                    if j % 2:
                        v.wait_ge(psum_read[blk.pair], blk.turn + 2)
                        v.wait_ge(psum_read[1 - blk.pair], blk.ahead(-1).turn + 2)
                        m = (m_a, m_b)[j // 2]
                        v.tensor_tensor(m[:], m[:], m_s[:, j // 2, :], ALU.mult).then_inc(s("gated"), 1)
                v.wait_ge(s("gated"), it * 2 + 2)
                v.tensor_tensor(m_b[:], m_a[:], m_b[:], ALU.add).then_inc(s("merged"), 1)
                v.wait_ge(s("m_rounded"), it + 1)
                v.tensor_tensor(m_lo[:, bass.ds(it, 1), :].rearrange("p a n -> p (a n)"), m_b[:],
                                m_hi[:, bass.ds(it, 1), :].rearrange("p a n -> p (a n)").bitcast(F32), ALU.subtract)\
                 .then_inc(s("m_ready"), 1)
            loop(v, KT, merge)

            def out_proj(it):
                for j in range(4):
                    step(Blk(B_OUT, it, j))
            loop(v, KT // 4, out_proj)
            v.wait_ge(s("x_back"), 16)
            post_norm(3, 1, CTX)
            pre_norm(4, 2, CTX)
            ffn(1, B_FFN2, segs_x, True)
            post_norm(5, 2, CTX)

        @block.tensor
        def _(pe):
            def mm(out, lhsT, rhs, start=True, stop=True):
                return pe.matmul(out, lhsT, rhs, start=start, stop=stop)

            def gemm(b, hi, lo, seg_list, kt=KT, off=0, ready=None):
                pe.wait_ge(s("w_split"), b.n + 1)
                pe.wait_ge(psum_read[b.pair], b.turn + 1)
                for k in range(kt):
                    if ready is not None:
                        pe.wait_ge(s("h_ready"), ready + k + 1)
                    for i, (w, x) in enumerate(((w_hi, hi), (w_hi, lo), (w_lo, hi))):
                        for l, h_, sg_ in seg_list:
                            last = mm(bank(b, sg_), w[:, b.pair, k, :], x[:, k, l - off:h_ - off],
                                      k == 0 and i == 0, k == kt - 1 and i == 2)
                last.then_inc(s("gemm_done"), 1)

            def mod_mm(u, slot, load, first=False):
                pe.wait_ge(wmod_loaded[slot], (load + 1) * 16)
                if not first:
                    pe.wait_ge(s("mod_out"), u - 1)
                for k in range(KT):
                    last = mm(ps[:, 6 + slot, 0:2], w_mod[:, slot, k, :], silc[:, k, :], k == 0, k == KT - 1)
                last.then_inc(s("mod_mm"), 1)

            def sum_partitions(r, lo):
                pe.wait_ge(s("sq_used"), KT * (r + 1))
                for l, h_, sg_ in (segs_all if lo == 0 else segs_x):
                    last = mm(ps[:, 4 + sg_, 0:h_ - l], ones, n_acc[:, l:h_])
                last.then_inc(s("ss_ready"), 1)

            def ffn(i, b0, seg_list, mod_from=None):
                u0 = mod_from
                pairs = i * HID
                for kind, b, n, c, hid in ffn_parts(b0):
                    if kind == "up":
                        def body(it, b=b, u0=u0, c=c):
                            for j in range(4):
                                gemm(Blk(b, it, j), h_hi, h_lo, seg_list)
                                if u0 is not None:
                                    mod_mm(it * 4 + (u0 + j), j % 2, it * 2 + (u0 // 2 + j // 2))
                    else:
                        pe.wait_ge(s("g_ready"), pairs + hid + FCH[c] + 1)

                        def body(it, b=b, u0=u0, c=c):
                            for j in range(4):
                                gemm(Blk(b, it, j), g_hi, g_lo, seg_list, FCH[c])
                                if u0 is not None and j % 2:
                                    mod_mm(it * 2 + (u0 + j // 2), j // 2, it + u0 // 2)
                    loop(pe, n // 4, body)
                    if u0 is not None:
                        u0 += n if kind == "up" else n // 2

            pe.wait_ge(s("silc"), 1)
            for u in range(2):
                mod_mm(u, u, 0, True)

            def mod_pair(it):
                for j in range(2):
                    mod_mm(it * 2 + (2 + j), j, it + 1)
            loop(pe, 7, mod_pair)
            pe.wait_ge(s("ca_loaded"), 16)
            sum_partitions(0, 0)
            pe.wait_ge(s("h_ready"), KT)
            ffn(0, B_FFN1, segs_all, 16)
            sum_partitions(1, 0)
            sum_partitions(2, 0)
            pe.wait_ge(s("h_ready"), 2 * KT)

            for j in range(2):
                gemm(Blk(B_KV, 0, j), h_hi, h_lo, segs_all)
                pe.wait_ge(s("at_sq"), j + 1)
                mm(ps[:, 4, 0:CTX], ones, a_sq[:, 0:CTX])
                mm(ps[:, 5, 0:SEQ], ones, a_sq[:, CTX:T]).then_inc(s("at_ss"), 1)
                if j:
                    pe.wait_ge(s("at_rot"), j)
                pe.wait_ge(s("at_nrm"), j + 1)
                mm(ps[:, 6, :], swap, a_n[:, 0:SEQ]).then_inc(s("at_swap"), 1)
            pe.wait_ge(s("at_rot"), 2)
            for j in range(2, 4):
                blk = Blk(B_KV, 0, j)
                gemm(blk, h_hi, h_lo, segs_all)
                pe.wait_ge(psum_read[blk.pair], blk.turn + 2)
                if j == 3:
                    pe.wait_ge(s("at_vc"), 1)
                for c in range(NCH):
                    last = pe.transpose(ps[:, 6 + c // 3, P * (c % 3):P * (c % 3) + P], a_raw[:, P * c:P * c + P], ident)
                last.then_inc(s("at_vt"), 1)
            gemm(Blk(B_KV, 0, 4), h_hi, h_lo, segs_all)
            pe.wait_ge(s("ba_bx"), 2)
            pe.wait_ge(s("at_vc"), 2)
            for c in range(NCH):
                last = pe.transpose(ps[:, 6 + c // 3, P * (c % 3):P * (c % 3) + P], bx[:, P * c:P * c + P], ident)
            last.then_inc(s("ba_tr"), 1)
            pe.wait_ge(s("ba_bg"), 1)
            mm(ps[:, 6, 0:48], tri_le, bg[:, :, 32:40])
            mm(ps[:, 6, 48:96], tri_ge, bg[:, :, 40:48])
            mm(ps[:, 6, 96:192], ones, bg[:, :, 32:48]).then_inc(s("ba_sum"), 1)
            pe.wait_ge(s("ba_x"), 3)

            def heads(it):
                for j in range(4):
                    n = it * 4 + j
                    blk = Blk(B_Q, it, j)
                    gemm(blk, h_hi, h_lo, segs_x)
                    pe.wait_ge(s("at_sq"), n + 3)
                    pe.wait_ge(s("o_at"), n + 1)
                    mm(ps[:, 4, :], ones, a_sq[:, 0:SEQ]).then_inc(s("at_ss"), 1)
                    pe.wait_ge(s("at_nrm"), n + 3)
                    mm(ps[:, 5, :], swap, a_n[:, 0:SEQ]).then_inc(s("at_swap"), 1)
                    pe.wait_ge(s("at_rot"), n + 3)

                    def scores(t):
                        for i in range(2):
                            last = mm(ps[:, 4 + 2 * (t % 2) + i, 0:384], a_q[:, P * t:P * t + P],
                                      a_kt[:, bass.ds(it, 1), 384 * i:384 * i + 384].rearrange("p a n -> p (a n)"))
                        last.then_inc(s("at_s"), 1)
                    scores(0)
                    scores(1)
                    for t in range(4):
                        pe.wait_ge(s("at_pn"), n * 4 + (t + 1))
                        if t:
                            pe.wait_ge(s("at_pt"), n * 4 + t)
                        for c in range(NCH):
                            last = pe.transpose(ps[:, 2 * (c // 3), P * (c % 3):P * (c % 3) + P],
                                                a_p[:, t % 2, P * c:P * c + P], ident)
                        last.then_inc(s("at_tr"), 1)
                        if t < 2:
                            scores(t + 2)
                    pe.wait_ge(s("at_pt"), n * 4 + 4)
                    if j == 0:
                        pe.wait_ge(s("at_vcur"), it + 1)
                    for c in range(NCH):
                        last = mm(ps[:, 4, :], a_vc[:, c], a_pt[:, c], c == 0, c == NCH - 1)
                    last.then_inc(s("at_pv"), 1)
            loop(pe, 2, heads)

            pe.wait_ge(s("o_at"), H + 1)

            def dn_head(h):
                pe.wait_ge(s("head_done"), h + 1)
                for j in range(4):
                    gemm(Blk(B_DN, h, j), h_hi, h_lo, segs_x if j in (0, 3) else segs_all)
                pe.wait_ge(s("d_sq"), h + 1)
                mm(ps[:, 4, :], ones, d_sq[:, 0:SEQ])
                mm(ps[:, 5, 0:CTX], ones, d_sq[:, SEQ:SEQ + CTX])
                mm(ps[:, 6, :], ones, d_sq[:, SEQ + CTX:]).then_inc(s("d_ss"), 1)
                pe.wait_ge(s("d_qk"), h + 1)
                off = [c * P + (2 if c >= NC_CTX else 0) for c in range(NCH)]
                for i in range(2):
                    if i == 1:
                        pe.wait_ge(s("d_silu"), h * 2 + 2)
                    for c in range(NCH):
                        last = pe.transpose(ps[:, 2 * i + c // 3, P * (c % 3):P * (c % 3) + P],
                                            d_c[:, 1 + i, off[c]:off[c] + P], ident)
                    last.then_inc(s("d_tok"), 1)
                for c in range(NCH):
                    kc = d_c[:, 1, off[c]:off[c] + P]
                    mm(ps[:, 4 + c // 3, P * (c % 3):P * (c % 3) + P], kc, kc)
                for c in range(NC_X):
                    last = mm(ps[:, 6, P * c:P * c + P], d_c[:, 1, off[c + NC_CTX]:off[c + NC_CTX] + P],
                              d_c[:, 0, off[c + NC_CTX]:off[c + NC_CTX] + P])
                last.then_inc(s("d_kk"), 1)
                for d in range(2):
                    pe.wait_ge(s("d_tokc"), h * 2 + (d + 1))
                    for c in range(NCH):
                        g_ = hc[:, G_GC + 6 * d + c:G_GC + 6 * d + c + 1]
                        last = mm(ps[:, 2 * d + c // 3, P * (c % 3):P * (c % 3) + P], g_.to_broadcast([P, P]), ident)
                    last.then_inc(s("d_row"), 1)
                pe.wait_ge(s("d_l"), h * 2 + 2)
                pe.wait_ge(s("d_am"), h * 2 + 2)
                for gr in range(4):
                    d, hf = gr // 2, gr % 2
                    pe.wait_ge(s("lvl"), h * 14 + d + 1)
                    for i in range(3):
                        last = pe.transpose(ps[:, 4 + gr, P * i:P * i + P], d_s[0][:, d, 3 * hf + i], ident)
                    last.then_inc(s("sv_q"), 1)
                pe.wait_ge(s("d_qe"), h * 2 + 2)
                for lv in range(1, LEVELS):
                    for gr in range(4):
                        d, hf = gr // 2, gr % 2
                        pe.wait_ge(s("lvl"), h * 14 + 2 * lv + d + 1)
                        pe.wait_ge(s("sv_r"), h * 28 + 4 * (lv - 1) + gr + 1)
                        for i in range(3):
                            last = mm(ps[:, 4 + gr, P * i:P * i + P], d_s[lv % 2][:, d, 3 * hf + i], d_r[:, d, 3 * hf + i])
                        last.then_inc(s("sv_q"), 1)
                    for gr in range(4):
                        d, hf = gr // 2, gr % 2
                        pe.wait_ge(s("sv_qc"), h * 24 + 4 * (lv - 1) + gr + 1)
                        for i in range(3):
                            last = mm(ps[:, 4 + gr, P * i:P * i + P], d_t[:, d, 3 * hf + i], d_q[:, d, 3 * hf + i])
                        if lv < LEVELS - 1:
                            for i in range(3):
                                last = mm(ps[:, gr, P * i:P * i + P], d_q[:, d, 3 * hf + i], d_t[:, d, 3 * hf + i])
                        last.then_inc(s("sv_d"), 1)
                pe.wait_ge(s("d_kbvb"), h * 4 + 4)
                for gr in range(4):
                    d, hf = gr // 2, gr % 2
                    pe.wait_ge(s("sv_r"), h * 28 + 24 + gr + 1)
                    for i in range(3):
                        mm(ps[:, 4 + gr, P * i:P * i + P], d_r[:, d, 3 * hf + i], d_l[:, d, 3 * hf + i])
                    for i in range(3):
                        last = mm(ps[:, gr, P * i:P * i + P], d_s[1][:, d, 3 * hf + i], d_r[:, d, 3 * hf + i])
                    last.then_inc(s("uw"), 1)
                pe.wait_ge(s("w_c"), h * 4 + 4)
                pe.wait_ge(s("u_c"), h * 4 + 4)
                pe.wait_ge(s("d_kd"), h * 2 + 2)
                pe.wait_ge(s("d_qd"), h * 2 + 2)
                pe.wait_ge(s("d_at"), h * 2 + 2)
                for t in range(NCH):
                    if t:
                        for d in range(2):
                            pe.wait_ge(s("sc_st"), h * 10 + 2 * (t - 1) + d + 1)
                            mm(ps[:, 4 + d, 0:P], d_t[:, d, ORDER[d][t]], d_st[:, d]).then_inc(s("sc_w"), 1)
                    for d in range(2):
                        c = ORDER[d][t]
                        vn = d_q[:, d, c]
                        if t:
                            vn = d_vn[:, d]
                            if c >= NC_CTX:
                                mm(ps[:, d, P * (c - NC_CTX):P * (c - NC_CTX) + P], d_st[:, d], d_qd[:, d, c - NC_CTX], True, False)
                            pe.wait_ge(s("sc_v"), h * 10 + 2 * (t - 1) + d + 1)
                        if t < NCH - 1:
                            mm(ps[:, 6 + d, 0:P], d_kd[:, d, c], vn).then_inc(s("sc_s"), 1)
                        if c >= NC_CTX:
                            mm(ps[:, d, P * (c - NC_CTX):P * (c - NC_CTX) + P], vn, d_at[:, d, c - NC_CTX], False, True)\
                                .then_inc(s("sc_o"), 1)
                pe.wait_ge(s("od_sq"), h + 1)
                mm(ps[:, 2, :], ones, d_sq[:, 0:SEQ]).then_inc(s("od_ss"), 1)
            loop(pe, H, dn_head)

            pe.wait_ge(s("o_split"), 2)

            def merge(it):
                for j in range(4):
                    hi, lo, off = ((odn_hi, odn_lo, CTX), (h_hi, h_lo, 0), (oat_hi, oat_lo, CTX), (h_hi, h_lo, 0))[j]
                    gemm(Blk(B_MERGE, it, j), hi, lo, segs_x, off=off)
            loop(pe, KT, merge)
            pe.wait_ge(s("m_ready"), KT)

            def out_proj(it):
                for j in range(4):
                    gemm(Blk(B_OUT, it, j), m_hi, m_lo, segs_x, off=CTX)
            loop(pe, KT // 4, out_proj)
            sum_partitions(3, CTX)
            sum_partitions(4, CTX)
            pe.wait_ge(s("h_ready"), 3 * KT)
            ffn(1, B_FFN2, segs_x)
            sum_partitions(5, CTX)


ORDER = [list(range(NCH)), list(range(NC_CTX))[::-1] + list(range(NC_CTX, NCH))[::-1]]


def _constants():
    i = np.arange(P)
    eye = np.eye(P, dtype=np.float32)
    swap = np.zeros((P, P), np.float32)
    swap[i ^ 32, i] = 1.0
    ca = np.stack([eye, np.ones((P, P), np.float32), (i[:, None] >= i[None, :]).astype(np.float32),
                   (i[:, None] <= i[None, :]).astype(np.float32), swap], 1)
    masks = np.zeros((P, 2, LEVELS, P), np.float32)
    for l in range(LEVELS):
        b = 1 << l
        m = (i[:, None] // (2 * b) == i[None, :] // (2 * b)) & (i[:, None] // b % 2 == 1) & (i[None, :] // b % 2 == 0)
        masks[:, 0, l] = m
        masks[:, 1, l] = m.T
    nf = DH // 4
    inv = (np.float32(10000.0) ** (-np.arange(nf, dtype=np.float32) / np.float32(nf))).astype(np.float32)
    pos = np.stack([np.repeat(np.arange(SEQ // 64), 64), np.tile(np.arange(64), SEQ // 64)]).astype(np.float32)
    ang = pos[:, None, :] * inv[None, :, None]
    cos = np.cos(ang, dtype=np.float32)
    sin = np.sin(ang, dtype=np.float32)
    c = np.stack([cos, cos], 1).reshape(P, SEQ)
    s_ = np.stack([-sin, sin], 1).reshape(P, SEQ)
    cb = np.concatenate([masks.reshape(P, -1), c, s_], 1)
    return np.ascontiguousarray(ca), np.ascontiguousarray(cb, dtype=np.float32)


def _tiles(w):
    K, N = w.shape
    t = w.reshape(K // P, P, N // P, P).transpose(2, 1, 0, 3)
    if K < D:
        t = np.concatenate([t, np.zeros((N // P, P, KT - K // P, P), w.dtype)], 2)
    return t.reshape(N // P, P, D)


def _ffn_blocks(w_gu, w_down):
    gu = _tiles(w_gu)
    out, hid = [], 0
    for n in FCH:
        pair = np.stack([gu[hid:hid + n], gu[HID + hid:HID + hid + n]], 1)
        out += [pair.reshape(2 * n, P, D), _tiles(w_down[hid * P:(hid + n) * P])]
        hid += n
    return out


def layout(i):
    w_in = i["w_in"][0]
    qkv, z = w_in[:, 0:3072], w_in[:, 3072:4096]
    w_ba, w_q, w_kv, w_g = w_in[:, 4096:4128], w_in[:, 4128:5152], w_in[:, 5152:5664], w_in[:, 5664:7712]
    pad = np.zeros((D, P), w_in.dtype)
    pad[:, 0:16] = w_ba[:, 0:16]
    pad[:, 32:48] = w_ba[:, 16:32]
    dn = np.stack([_tiles(qkv[:, 0:1024]), _tiles(qkv[:, 1024:2048]), _tiles(qkv[:, 2048:3072]), _tiles(z)], 1)
    mg = np.stack([_tiles(i["w_dn_out"][0]), _tiles(w_g[:, 0:1024]), _tiles(i["w_attn_out"][0]),
                   _tiles(w_g[:, 1024:2048])], 1)
    W = np.concatenate(_ffn_blocks(i["ffn1_w_gu"][0], i["ffn1_w_down"][0])
                       + [_tiles(w_kv), _tiles(pad), _tiles(w_q), dn.reshape(-1, P, D), mg.reshape(-1, P, D),
                          _tiles(i["w_out"][0])]
                       + _ffn_blocks(i["ffn2_w_gu"][0], i["ffn2_w_down"][0]))
    col = lambda a: a.reshape(-1, P).T
    gates = np.zeros((P, 2), np.float32)
    gates[32:48, 0] = i["dn_a_log"][0].reshape(-1)
    gates[32:48, 1] = i["dn_dt_bias"][0].reshape(-1)
    cc = np.stack([col(i["c_ctx"]), col(i["c"][0])], 2).reshape(P, -1)
    vec = np.concatenate([col(i[n][0]) for n in ("ffn1_pre", "ffn1_post", "mix_pre", "mix_post", "ffn2_pre", "ffn2_post",
                                                 "b_mod", "attn_q_norm", "attn_k_norm", "dn_out_norm")] + [gates, cc], 1)
    conv = i["dn_conv"][0].reshape(3, 3, H, P).transpose(3, 2, 1, 0).reshape(P, H, 9)
    ca, cb = _constants()
    return dict(W=W, WMOD=_tiles(i["w_mod"][0]), XT=np.concatenate([i["ctx"][0], i["x"][0]]).T,
                VEC=vec, CONV=conv, CA=ca, CB=cb)


def kernel(**inputs):
    import concourse.bacc as bacc
    from concourse.bass_utils import run_bass_kernel_spmd as run

    arrays = {k: np.ascontiguousarray(a) for k, a in layout({k: np.asarray(a) for k, a in inputs.items()}).items()}
    nc = bacc.Bacc("TRN2", target_bir_lowering=False, num_devices=1)
    args = [nc.dram_tensor(k, a.shape, F32, kind="ExternalInput").ap() for k, a in arrays.items()]
    out = nc.dram_tensor("out", [D, SEQ], F32, kind="ExternalOutput").ap()
    spill = nc.dram_tensor("x_spill", [P, KT, SEQ], F32, kind="Internal").ap()
    build(nc, *args, out, spill)
    r = run(nc, [arrays], core_ids=[0])
    return np.ascontiguousarray(r.results[0]["out"].T).reshape(1, SEQ, D)
```

```python
import numpy as np

import concourse.bass as bass
from concourse import mybir
from concourse.alu_op_type import AluOpType as ALU
from contextlib import ExitStack

ACT = mybir.ActivationFunctionType
AX = mybir.AxisListType
F32 = mybir.dt.float32
F32R = mybir.dt.float32r

P = 128
D = 1024
KT = D // P
CTX, SEQ = 256, 512
T = CTX + SEQ
NC_CTX, NC_X = CTX // P, SEQ // P
NCH = NC_CTX + NC_X
EPS = 1e-6
H = 8
HKV = 2
DH = 128
HID = 2816 // P
FCH = [8, 8, 6]
RING = 4

N_FFN = 2 * HID + 3 * KT
B_FFN1 = 0
B_KV = B_FFN1 + N_FFN
B_Q = B_KV + 5
B_DN = B_Q + H
B_MERGE = B_DN + 4 * H
B_OUT = B_MERGE + 4 * KT
B_FFN2 = B_OUT + KT
NBLK = B_FFN2 + N_FFN

N_MOD = 72
LEVELS = 7

V_PRE1, V_POST1, V_PREM, V_POSTM, V_PRE2, V_POST2 = range(0, 48, 8)
V_BMOD = 48
V_QN, V_KN, V_DN, V_ALOG, V_DT = range(V_BMOD + N_MOD, V_BMOD + N_MOD + 5)
V_C = V_DT + 1
NV = V_C + 2 * KT
G_CONV, G_BETA, G_GC, G_BEG, G_KD, G_DCY = 0, 9, 21, 33, 45, 57
NG = 69


class Blk:

    def __init__(self, base, it, j):
        at = base + j
        self.n = at + it * 4
        self.raw = at % RING
        self.pair = at % 2
        self.turn = at // 2 + it * 2
        self.load = at // RING + it
        self.base, self.it, self.j = base, it, j

    def ahead(self, d):
        return Blk(self.base, self.it, self.j + d)


def build(nc, W, WMOD, XT, VEC, CONV, CA, CB, OUT, XS):
    ctx = ExitStack()
    with ctx:
        base0 = 16512

        def at(name, kb, shape, dt=F32):
            return nc.alloc_sbuf_tensor_at(name, [P] + shape, dt, offset=base0 + int(kb * 1024))

        def sem(name):
            return ctx.enter_context(nc.semaphore(name))

        raw = at("raw", 0, [RING, KT, P])
        w_hi = at("w_hi", 16, [2, KT, P], F32R)
        w_lo = at("w_lo", 24, [2, KT, P], F32R)
        h_hi = at("h_hi", 32, [KT, T], F32R)
        h_lo = at("h_lo", 56, [KT, T], F32R)
        ca = at("ca", 80, [5, P])
        vec = at("vec", 82.5, [NV])
        mod = at("mod", 83.25, [N_MOD, 2])
        drv = at("drv", 84, [6, KT, 2])
        silc = at("silc", 84.5, [KT, 2])
        small = at("small", 84.625, [32])
        gall = at("gall", 85, [H, NG])
        cb = at("cb", 87.5, [14 * P + 2 * SEQ])
        w_mod = at("w_mod", 87.5, [2, KT, P])
        ident, ones, tri_ge, tri_le, swap = (ca[:, i, :] for i in range(5))
        masks = cb[:, 0:14 * P].rearrange("p (d l m) -> p d l m", d=2, l=LEVELS)
        rope_c = cb[:, 14 * P:14 * P + SEQ]
        rope_s = cb[:, 14 * P + SEQ:14 * P + 2 * SEQ]
        X = at("X", 100, [KT, T])
        g_hi = at("g_hi", 124, [8, T], F32R)
        g_lo = at("g_lo", 148, [8, T], F32R)
        Y = at("Y", 172, [KT, T])
        sg = at("sg", 196, [T])
        gt = at("gt", 199, [T])
        n_sq = at("n_sq", 124, [2, T])
        n_acc = at("n_acc", 130, [T])
        n_rs = at("n_rs", 133, [T])
        n_t = at("n_t", 136, [2, T])
        n_t2 = at("n_t2", 142, [2, T])
        o_at = at("o_at", 100, [H, SEQ])
        a_kt = at("a_kt", 132, [HKV, T])
        a_v = at("a_v", 138, [NCH, HKV, P])
        a_vc = at("a_vc", 144, [NCH, P])
        a_raw = at("a_raw", 147, [T])
        a_sq = at("a_sq", 150, [T])
        a_rs = at("a_rs", 153, [T])
        a_n = at("a_n", 156, [T])
        a_t1 = at("a_t1", 159, [SEQ])
        a_t2 = at("a_t2", 161, [SEQ])
        a_q = at("a_q", 163, [2, SEQ])
        a_p = at("a_p", 200, [2, T])
        a_pt = [at("a_pt0", 167, [NCH, SEQ]), at("a_pt1", 184, [NCH, SEQ])]
        a_m = at("a_m", 183, [3, 4])
        q_raw, q_sq, q_rs, q_n = ([b0[:, 0:SEQ], at(f"q_{n}1", 171 + 2 * i, [SEQ])[:]]
                                  for i, (n, b0) in enumerate((("raw", a_raw), ("sq", a_sq), ("rs", a_rs), ("n", a_n))))
        ba = at("ba", 184, [T])
        bx = at("bx", 187, [T])
        bt = at("bt", 190, [2, T])
        bg = at("bg", 196, [NCH, 48])
        bgt = at("bgt", 197.25, [3, 96])
        o_dn = at("o_dn", 116, [H, SEQ])
        M6 = NCH * P
        d_l = at("d_l", 132, [2, NCH, P])
        d_t = at("d_t", 138, [2, NCH, P])
        d_r = at("d_r", 144, [2, NCH, P])
        d_q = at("d_q", 150, [2, NCH, P])
        d_s = [at(f"d_s{i}", 156 + 6 * i, [2, NCH, P]) for i in range(2)]
        d_kd = at("d_kd", 168, [2, NCH, P])
        d_rs = at("d_rs", 168, [SEQ + T])
        d_at = at("d_at", 174, [2, NC_X, P])
        d_qd = at("d_qd", 178, [2, NC_X, P])
        d_ktok = at("d_ktok", 182, [NCH, P])
        d_vtok = at("d_vtok", 185, [NCH, P])
        d_sq = at("d_sq", 182, [SEQ + T])
        d_c = at("d_c", 188, [3, T + 2])
        d_up = at("d_up", 197.125, [T + 4])
        d_z = at("d_z", 200.25, [SEQ])
        d_st = at("d_st", 202.25, [2, P])
        d_vn = at("d_vn", 203.25, [2, P])
        d_o = at("d_o", 204.25, [SEQ])
        hc = at("hc", 206.25, [NG])
        odn_hi = at("odn_hi", 132, [H, SEQ], F32R)
        odn_lo = at("odn_lo", 148, [H, SEQ], F32R)
        oat_hi = at("oat_hi", 164, [H, SEQ], F32R)
        oat_lo = at("oat_lo", 180, [H, SEQ], F32R)
        m_hi = at("m_hi", 100, [KT, SEQ], F32R)
        m_lo = at("m_lo", 116, [KT, SEQ], F32R)
        m_a = at("m_a", 196, [SEQ])
        m_b = at("m_b", 198, [SEQ])
        m_s = at("m_s", 200, [2, SEQ])
        y_o = at("y_o", 132, [KT, SEQ])

        ps = ctx.enter_context(nc.psum_tensor("ps", [P, 8, 512], F32))

        S = {}

        def s(name):
            if name not in S:
                S[name] = sem(name)
            return S[name]

        w_loaded = [s(f"w_loaded{i}") for i in range(RING)]
        wmod_loaded = [s(f"wmod_loaded{i}") for i in range(2)]
        psum_read = [s(f"psum_read{i}") for i in range(2)]

        segs_all = [(0, CTX, 0), (CTX, T, 1)]
        segs_x = [(CTX, T, 1)]

        def bank(blk, seg):
            b = 2 * blk.pair + seg
            return ps[:, b, 0:(CTX, SEQ)[seg]]

        def half(x, lv, odd):
            n = 1 << lv
            return x.rearrange("p c (b e n) -> p c b e n", e=2, n=n)[:, :, :, odd, :]

        def halves(x, lv):
            return x.rearrange("p (c b n) -> p c b n", c=3, n=1 << lv)

        def loop(eng, iters, body, peel=False):
            if iters - peel > 0:
                with eng.Fori(0, iters - peel, 1) as it:
                    body(it)
            if peel:
                body(iters - 1)

        def all_read(eng, blocks):
            for p_ in range(2):
                eng.wait_ge(psum_read[p_], (blocks + 1 - p_) // 2 + 1)

        def ffn_parts(b0):
            b, hid = b0, 0
            for c, n in enumerate(FCH):
                yield "up", b, 2 * n, c, hid
                b += 2 * n
                yield "down", b, KT, c, hid
                b += KT
                hid += n


        block = ctx.enter_context(nc.Block())

        @block.sync
        def _(sp):
            sp.dma_start(vec[:], VEC).then_inc(s("tables_loaded"), 16)
            sp.dma_start(X[:], XT.rearrange("(k p) t -> p k t", p=P)).then_inc(s("x_loaded"), 16)
            sp.dma_start(ca[:], CA).then_inc(s("ca_loaded"), 16)
            sp.dma_start(gall[:, :, 0:9], CONV).then_inc(s("conv_loaded"), 16)
            Wv = W.rearrange("b p (k n) -> b p k n", k=KT)
            for b in range(RING):
                sp.dma_start(raw[:, b], Wv[b]).then_inc(w_loaded[b], 16)

            def load(n, slot):
                sp.wait_ge(s("w_split"), n - RING + 1)
                sp.dma_start(raw[:, slot], Wv[bass.ds(n, 1)].rearrange("b p k n -> p (b k) n"))\
                  .then_inc(w_loaded[slot], 16)

            with sp.Fori(0, NBLK // RING - 1, 1) as it:
                for j in range(RING):
                    load(it * RING + (RING + j), j)
            for n in range(NBLK // RING * RING, NBLK):
                load(n, n % RING)
            sp.wait_ge(s("x_new"), 3 * KT)
            sp.dma_start(OUT.rearrange("(k p) t -> p k t", p=P), X[:, :, CTX:T]).then_inc(s("stored"), 16)
            sp.wait_ge(s("stored"), 16)

        @block.gpsimd
        def _(g):
            g.sem_inc(psum_read[0], 1)
            g.sem_inc(psum_read[1], 1)
            g.sem_inc(s("g_ready"), 1)
            g.sem_inc(s("o_at"), 1)
            g.sem_inc(s("head_done"), 1)

            Mv = WMOD.rearrange("u p (k n) -> u p k n", k=KT)
            for u in range(2):
                g.dma_start(w_mod[:, u], Mv[u]).then_inc(wmod_loaded[u], 16)
            with g.Fori(0, N_MOD // 2 - 1, 1) as it:
                for u in range(2):
                    g.wait_ge(s("mod_mm"), it * 2 + (u + 1))
                    g.dma_start(w_mod[:, u], Mv[bass.ds(it * 2 + (2 + u), 1)].rearrange("b p k n -> p (b k) n"))\
                     .then_inc(wmod_loaded[u], 16)
            g.wait_ge(s("mod_mm"), N_MOD)
            g.dma_start(cb[:], CB).then_inc(s("cb_loaded"), 16)
            g.wait_ge(s("h_ready"), 2 * KT)
            g.dma_start(XS, X[:, :, CTX:T]).then_inc(s("x_spilled"), 16)
            g.wait_ge(s("x_spilled"), 16)
            def q_copies(it):
                g.wait_ge(s("o_at"), it * 4 + 1)
                for j in range(4):
                    g.wait_ge(s("at_rot"), it * 4 + (j + 3))
                    if j >= 2:
                        g.wait_ge(s("at_s"), it * 16 + 4 * (j - 1))
                    g.tensor_copy(a_q[:, j % 2, :], o_at[:, bass.ds(it * 4 + j, 1), :].rearrange("p a n -> p (a n)"))\
                     .then_inc(s("at_qc"), 1)
            loop(g, 2, q_copies)
            g.wait_ge(s("cb_loaded"), 16)
            g.wait_ge(s("o_at"), H + 1)
            g.memset(d_up[:], 0.0).then_inc(s("d_up0"), 1)

            def bc(x):
                return x.unsqueeze(2).to_broadcast([P, x.shape[1], P])

            def head(h):
                g.wait_ge(s("d_e1"), h * 2 + 2)
                g.tensor_tensor(d_t[:, 1], d_t[:, 1], bc(hc[:, G_BETA + 6:G_BETA + 12]), ALU.mult).then_inc(s("d_eb1"), 1)

                def level(lv):
                    g.tensor_tensor(d_s[lv % 2][:, 1], d_l[:, 1], masks[:, 1, lv, :].unsqueeze(1).to_broadcast([P, NCH, P]),
                                    ALU.mult).then_inc(s("lvl1"), 1)
                g.wait_ge(s("d_l"), h * 2 + 2)
                level(0)
                level(1)
                for d in range(2):
                    g.wait_ge(s("d_am"), h * 2 + (d + 1))
                    tri = (tri_le, tri_ge)[d]
                    g.tensor_tensor(d_at[:, d], d_at[:, d], tri.unsqueeze(1).to_broadcast([P, NC_X, P]),
                                    ALU.mult).then_inc(s("d_at"), 1)
                for lv in range(2, LEVELS):
                    if lv == 2:
                        g.wait_ge(s("sv_r"), h * 28 + 4)
                    g.wait_ge(s("sv_q"), h * 28 + 4 * (lv - 2) + 4)
                    level(lv)
                    if lv == 2:
                        for d in range(2):
                            g.wait_ge(s("d_qe"), h * 2 + (d + 1))
                            g.tensor_tensor(d_qd[:, d], d_qd[:, d],
                                            d_c[:, 0, CTX + 2:T + 2].rearrange("p (c n) -> p c n", c=NC_X),
                                            ALU.mult).then_inc(s("d_qd"), 1)
                        g.wait_ge(s("d_tokc"), h * 2 + 2)
                    if lv in (3, 4):
                        d = lv - 3
                        g.tensor_tensor(d_kd[:, d], d_ktok[:], bc(hc[:, G_KD + 6 * d:G_KD + 6 * d + 6]),
                                        ALU.mult).then_inc(s("d_kd"), 1)
                for d in range(2):
                    g.wait_ge(s(f"lvl{d}"), h * 7 + 7)
                    g.tensor_tensor(d_l[:, d], d_vtok[:], bc(hc[:, G_BETA + 6 * d:G_BETA + 6 * d + 6]),
                                    ALU.mult).then_inc(s("d_kbvb"), 1)
                g.wait_ge(s("sv_q"), h * 28 + 24)
                g.tensor_tensor(d_s[1][:, 1], d_ktok[:], bc(hc[:, G_BEG + 6:G_BEG + 12]), ALU.mult).then_inc(s("d_kbvb"), 1)

            with g.Fori(0, H, 1) as h:
                head(h)
            g.wait_ge(s("gemm_done"), B_OUT + KT)
            g.dma_start(X[:, :, CTX:T], XS).then_inc(s("x_back"), 16)
            g.wait_ge(s("x_back"), 16)

        @block.scalar
        def _(a):
            zero, one, eps, eps_q = (small[:, i:i + 1] for i in range(4))

            def split(b):
                a.wait_ge(w_loaded[b.raw], (b.load + 1) * 16)
                a.activation(w_hi[:, b.pair], raw[:, b.raw], ACT.Copy).then_inc(s("w_hi"), 1)

            def step(b):
                a.wait_ge(s("gemm_done"), b.n + 1)
                if not (isinstance(b.n, int) and b.n + 2 >= NBLK):
                    split(b.ahead(2))

            def read_out(b, dst, seg_list, func=ACT.Copy):
                for lo, hi, sg_ in seg_list:
                    last = a.activation(dst(lo, hi), bank(b, sg_), func)
                last.then_inc(psum_read[b.pair], 1)

            def sumsq(r, src, lo):
                for k in range(KT):
                    if r or k >= 2:
                        a.wait_ge(s("sq_used"), KT * r + k - 1)
                    a.activation(n_sq[:, k % 2, lo:T], src(k), ACT.Square).then_inc(s("sq_ready"), 1)
                a.wait_ge(s("ss_ready"), r + 1)
                segs = segs_all if lo == 0 else segs_x
                for l, h_, sg_ in segs:
                    last = a.activation(n_rs[:, l:h_], ps[:, 4 + sg_, 0:h_ - l], ACT.Ln, bias=eps, scale=1.0 / D)
                last.then_inc(s("ln_ready"), 1)
                a.wait_ge(s("ln_ready"), r + 1)
                a.activation(n_rs[:, lo:T], n_rs[:, lo:T], ACT.Exp, scale=-0.5).then_inc(s("rstd"), 1)

            def pre_norm(r, p, lo):
                sumsq(r, lambda k: X[:, k, lo:T], lo)
                mi = (0, 3, 6)[p]
                for k in range(KT):
                    a.wait_ge(s("nrm_ready"), KT * p + k + 1)
                    for l, h_, sg_ in (segs_all if lo == 0 else segs_x):
                        last = a.activation(h_hi[:, k, l:h_], n_t[:, k % 2, l:h_], ACT.Identity,
                                            bias=mod[:, 8 * mi + k, sg_:sg_ + 1], scale=drv[:, 2 * p, k, sg_:sg_ + 1])
                    last.then_inc(s("h_rounded"), 1)

            def ffn(i, b0, seg_list, peel_last):
                lo = seg_list[0][0]
                for kind, b, n, c, hid in ffn_parts(b0):
                    lastpart = peel_last and kind == "down" and c == 2

                    def up(it):
                        for j in range(4):
                            blk = Blk(b, it, j)
                            step(blk)
                            if j % 2 == 0:
                                read_out(blk, lambda l, h_: sg[:, l:h_], seg_list, ACT.Silu)
                            else:
                                a.wait_ge(psum_read[blk.pair], blk.turn + 2)
                                p_ = it * 2 + j // 2
                                a.activation(g_hi[:, bass.ds(p_, 1), lo:T].rearrange("p a n -> p (a n)"), gt[:, lo:T],
                                             ACT.Copy).then_inc(s("g_rounded"), 1)

                    def down(it):
                        for j in range(4):
                            blk = Blk(b, it, j)
                            step(blk)
                            if c == 0:
                                read_out(blk, lambda l, h_: Y[:, bass.ds(it * 4 + j, 1), l:h_].rearrange("p a n -> p (a n)"),
                                         seg_list)
                    loop(a, n // 4, up if kind == "up" else down, lastpart)

            a.wait_ge(s("small_set"), 1)
            a.wait_ge(s("tables_loaded"), 16)
            a.activation(silc[:], vec[:, V_C:V_C + 2 * KT].rearrange("p (k c) -> p k c", c=2), ACT.Silu).then_inc(s("silc"), 1)
            split(Blk(0, 0, 0))
            split(Blk(0, 0, 1))
            a.wait_ge(s("x_loaded"), 16)
            pre_norm(0, 0, 0)
            ffn(0, B_FFN1, segs_all, False)
            all_read(a, B_FFN1 + N_FFN)
            sumsq(1, lambda k: Y[:, k, :], 0)
            a.wait_ge(s("x_new"), KT)
            pre_norm(2, 1, 0)

            def item_norm(n, width):
                a.activation(a_sq[:, 0:width], a_raw[:, 0:width], ACT.Square).then_inc(s("at_sq"), 1)
                a.wait_ge(s("at_ss"), n + 1)
                if width == T:
                    a.activation(a_rs[:, 0:CTX], ps[:, 4, 0:CTX], ACT.Ln, bias=eps, scale=1.0 / DH)
                    a.activation(a_rs[:, CTX:T], ps[:, 5, 0:SEQ], ACT.Ln, bias=eps, scale=1.0 / DH).then_inc(s("at_ln"), 1)
                else:
                    a.activation(a_rs[:, 0:SEQ], ps[:, 4, 0:SEQ], ACT.Ln, bias=eps, scale=1.0 / DH).then_inc(s("at_ln"), 1)
                a.wait_ge(s("at_ln"), n + 1)
                a.activation(a_rs[:, 0:width], a_rs[:, 0:width], ACT.Exp, scale=-0.5).then_inc(s("at_rs"), 1)

            for j in range(2):
                blk = Blk(B_KV, 0, j)
                step(blk)
                if j:
                    a.wait_ge(s("at_nrm"), j)
                read_out(blk, lambda l, h_: a_raw[:, l:h_], segs_all)
                a.wait_ge(psum_read[blk.pair], blk.turn + 2)
                item_norm(j, T)
            for j in range(2, 4):
                blk = Blk(B_KV, 0, j)
                step(blk)
                a.wait_ge(s("at_nrm"), 2)
                if j == 3:
                    a.wait_ge(s("at_vt"), 1)
                read_out(blk, lambda l, h_: a_raw[:, l:h_], segs_all)
                a.wait_ge(s("at_vt"), j - 1)
                a.activation(a_v[:, :, j - 2, :].rearrange("p (b c) n -> p b c n", b=2),
                             ps[:, 6:8, 0:384].rearrange("p b (c n) -> p b c n", c=3), ACT.Copy).then_inc(s("at_vc"), 1)
            blk = Blk(B_KV, 0, 4)
            step(blk)
            read_out(blk, lambda l, h_: ba[:, l:h_], segs_all)
            a.wait_ge(psum_read[blk.pair], blk.turn + 2)
            a.activation(bt[0:16, 0, :], ba[0:16, :], ACT.Exp, scale=-1.0).then_inc(s("ba_e"), 1)
            a.activation(small[32:48, 8:9], vec[32:48, V_ALOG:V_ALOG + 1], ACT.Exp).then_inc(s("ba_e"), 1)
            a.wait_ge(s("ba_abs"), 2)
            a.activation(bt[32:48, 0, :], bt[32:48, 0, :], ACT.Exp, scale=-1.0).then_inc(s("ba_e"), 1)
            a.wait_ge(s("ba_e"), 3)
            a.activation(bt[32:48, 0, :], bt[32:48, 0, :], ACT.Ln, bias=one[32:48]).then_inc(s("ba_e"), 1)
            a.wait_ge(s("ba_gc"), 1)
            a.activation(bgt[:, 1, :], bgt[:, 0, :], ACT.Exp).then_inc(s("ba_x"), 1)
            a.wait_ge(s("ba_gt"), 1)
            for d in range(2):
                a.activation(gall[:, :, G_DCY + 6 * d:G_DCY + 6 * d + 6],
                             ps[:, 6, 96:192].rearrange("p (c e h) -> p e h c", c=NCH, e=2)[:, d], ACT.Exp)\
                 .then_inc(s("ba_x"), 1)
            a.activation(bgt[:, 2, :], bgt[:, 2, :], ACT.Exp).then_inc(s("ba_x"), 1)

            a.wait_ge(s("x_spilled"), 16)

            def q_rstd(n, sl):
                a.wait_ge(s("at_ss"), n + 3)
                a.activation(q_rs[sl], ps[:, 4 + sl, 0:SEQ], ACT.Ln, bias=eps, scale=1.0 / DH).then_inc(s("at_ln"), 1)
                a.wait_ge(s("at_ln"), n + 3)
                a.activation(q_rs[sl], q_rs[sl], ACT.Exp, scale=-0.5).then_inc(s("at_rs"), 1)

            def queries(it):
                for j in range(4):
                    n = it * 4 + j
                    blk = Blk(B_Q, it, j)
                    step(blk)
                    a.wait_ge(s("at_nrm"), n + 1)
                    a.activation(q_raw[j % 2], bank(blk, 1), ACT.Copy).then_inc(psum_read[blk.pair], 1)
                    a.wait_ge(psum_read[blk.pair], blk.turn + 2)
                    a.activation(q_sq[j % 2], q_raw[j % 2], ACT.Square).then_inc(s("at_sq"), 1)
                    if j:
                        q_rstd(it * 4 + (j - 1), (j - 1) % 2)
                q_rstd(it * 4 + 3, 1)
            loop(a, 2, queries)

            a.wait_ge(s("gall"), 1)
            a.wait_ge(s("at_rot"), H + 2)

            def heads(it):
                a.wait_ge(s("o_at"), it * 4 + 1)
                a.activation(a_vc[:], a_v[:, :, bass.ds(it, 1), :].rearrange("p c a n -> p (c a) n"),
                             ACT.Copy).then_inc(s("at_vcur"), 1)

                def evac_pt(i):
                    a.wait_ge(s("at_tr"), it * 16 + (i + 1))
                    t = i % 4
                    a.activation(a_pt[i // 4 % 2][:, :, P * t:P * t + P].rearrange("p (b c) n -> p b c n", b=2),
                                 ps[:, 0:2, 0:384].rearrange("p b (c n) -> p b c n", c=3), ACT.Copy)\
                     .then_inc(s("at_pt"), 1)

                def out_head(j):
                    n = it * 4 + j
                    a.wait_ge(s("at_pv"), n + 1)
                    a.activation(o_at[:, bass.ds(n, 1), :].rearrange("p a n -> p (a n)"), ps[:, 2 + j % 2, 0:SEQ], ACT.Copy)\
                     .then_inc(s("o_at"), 1)
                for i in range(16):
                    t = i % 4
                    a.wait_ge(s("at_max"), it * 16 + (i + 1))
                    a.activation(a_p[:, i % 2, :].rearrange("p (b n) -> p b n", b=2),
                                 ps[:, 4 + 2 * (i % 2):6 + 2 * (i % 2), 0:384],
                                 ACT.Exp, bias=a_m[:, 1, t:t + 1], scale=DH ** -0.5,
                                 accum_out=a_m[:, 2, t:t + 1]).then_inc(s("at_p"), 1)
                    if i:
                        evac_pt(i - 1)
                    if i >= 4 and t == 2:
                        out_head(i // 4 - 1)
                evac_pt(15)
                out_head(3)
            loop(a, 2, heads)

            def take(b):
                a.wait_ge(s("gemm_done"), b.n + 1)
                if b.j:
                    a.wait_ge(s("conv"), b.it * 3 + b.j)
                    a.activation(d_up[:, 1:CTX + 1], bank(b, 0), ACT.Copy)
                a.activation(d_up[:, CTX + 3:T + 3], bank(b, 1), ACT.Copy).then_inc(psum_read[b.pair], 1)
                split(b.ahead(2))

            def dn_head(h, final):
                b = [Blk(B_DN, h, j) for j in range(4)]
                take(b[0])
                for d in range(2):
                    a.wait_ge(s("d_mn"), h * 4 + 2 * d + 1)
                    a.activation(d_t[:, d], d_t[:, d], ACT.Exp).then_inc(s("d_e1"), 1)
                    a.wait_ge(s("d_mn"), h * 4 + 2 * d + 2)
                    a.activation(d_r[:, d, 0:NC_X], d_r[:, d, 0:NC_X], ACT.Exp, scale=-1.0).then_inc(s("d_e2"), 1)
                    a.activation(d_qd[:, d, 0], ps[:, 4 + 2 * d, 2 * P:3 * P], ACT.Exp)
                    a.activation(d_qd[:, d, 1:NC_X].rearrange("p c n -> p (c n)"), ps[:, 5 + 2 * d, 0:384], ACT.Exp)\
                     .then_inc(s("d_qe"), 1)
                take(b[1])
                a.activation(d_c[:, 0, CTX + 2:], d_c[:, 0, CTX + 2:], ACT.Silu).then_inc(s("d_silu"), 1)
                a.wait_ge(s("d_silu"), h * 3 + 1)
                a.activation(d_sq[:, 0:SEQ], d_c[:, 0, CTX + 2:], ACT.Square)
                a.wait_ge(s("conv"), h * 3 + 2)
                a.activation(d_c[:, 1, :], d_c[:, 1, :], ACT.Silu).then_inc(s("d_silu"), 1)
                a.wait_ge(s("d_silu"), h * 3 + 2)
                a.activation(d_sq[:, SEQ:SEQ + CTX], d_c[:, 1, 0:CTX], ACT.Square)
                a.activation(d_sq[:, SEQ + CTX:], d_c[:, 1, CTX + 2:], ACT.Square).then_inc(s("d_sq"), 1)
                take(b[2])
                a.wait_ge(s("d_ss"), h + 1)
                a.activation(d_rs[:, 0:SEQ], ps[:, 4, :], ACT.Ln, bias=eps_q, scale=float(DH))
                a.activation(d_rs[:, SEQ:SEQ + CTX], ps[:, 5, 0:CTX], ACT.Ln, bias=eps)
                a.activation(d_rs[:, SEQ + CTX:], ps[:, 6, :], ACT.Ln, bias=eps).then_inc(s("d_ln"), 1)
                a.wait_ge(s("d_ln"), h * 2 + 1)
                a.activation(d_rs[:], d_rs[:], ACT.Exp, scale=-0.5).then_inc(s("d_rstd"), 1)
                a.wait_ge(s("conv"), h * 3 + 3)
                a.activation(d_c[:, 2, :], d_c[:, 2, :], ACT.Silu).then_inc(s("d_silu"), 1)
                a.wait_ge(s("gemm_done"), b[3].n + 1)
                a.wait_ge(s("head_done"), h + 1)
                a.activation(d_z[:], bank(b[3], 1), ACT.Silu).then_inc(psum_read[b[3].pair], 1)
                for i, dst in enumerate((d_ktok, d_vtok)):
                    a.wait_ge(s("d_tok"), h * 2 + (i + 1))
                    a.activation(dst[:].rearrange("p (b c) n -> p b (c n)", b=2), ps[:, 2 - 2 * i:4 - 2 * i, 0:384], ACT.Copy)\
                     .then_inc(s("d_tokc"), 1)
                    if i == 0:
                        split(b[3].ahead(2))
                for lv in range(1, LEVELS):
                    for gr in range(4):
                        d, hf = gr // 2, gr % 2
                        a.wait_ge(s("sv_q"), h * 28 + 4 * lv + gr + 1)
                        a.activation(d_q[:, d, 3 * hf:3 * hf + 3].rearrange("p c n -> p (c n)"), ps[:, 4 + gr, 0:384],
                                     ACT.Copy).then_inc(s("sv_qc"), 1)
                for gr in range(4):
                    d, hf = gr // 2, gr % 2
                    a.wait_ge(s("uw"), h * 4 + gr + 1)
                    a.activation(d_q[:, d, 3 * hf:3 * hf + 3].rearrange("p c n -> p (c n)"), ps[:, 4 + gr, 0:384],
                                 ACT.Copy).then_inc(s("u_c"), 1)
                a.wait_ge(s("sc_o"), h * 8 + 8)
                a.activation(d_o[:], ps[:, 0, :], ACT.Copy).then_inc(s("od_copy"), 1)
                a.wait_ge(s("od_sum"), h + 1)
                a.activation(d_sq[:, 0:SEQ], d_o[:], ACT.Square).then_inc(s("od_sq"), 1)
                a.wait_ge(s("od_ss"), h + 1)
                a.activation(d_rs[:, 0:SEQ], ps[:, 2, :], ACT.Ln, bias=eps, scale=1.0 / DH).then_inc(s("d_ln"), 1)
                a.wait_ge(s("d_ln"), h * 2 + 2)
                a.activation(d_rs[:, 0:SEQ], d_rs[:, 0:SEQ], ACT.Exp, scale=-0.5).then_inc(s("od_rstd"), 1)
            a.wait_ge(s("d_up0"), 1)
            with a.Fori(0, H - 1, 1) as h:
                dn_head(h, False)
            dn_head(H - 1, True)

            a.wait_ge(s("head_done"), H + 1)
            for src, dst in ((o_dn, odn_hi), (o_at, oat_hi)):
                a.activation(dst[:], src[:], ACT.Copy).then_inc(s("o_rounded"), 1)

            def merge(it):
                for j in range(4):
                    blk = Blk(B_MERGE, it, j)
                    step(blk)
                    dst = (m_a[:], m_s[:, 0, :], m_b[:], m_s[:, 1, :])[j]
                    if j < 2:
                        a.wait_ge(s("merged"), it + 1)
                    if j == 2:
                        a.wait_ge(s("gated"), it * 2 + 1)
                    read_out(blk, lambda l, h_: dst, segs_x, ACT.Sigmoid if j % 2 else ACT.Copy)
                a.wait_ge(s("merged"), it + 2)
                a.activation(m_hi[:, bass.ds(it, 1), :].rearrange("p a n -> p (a n)"), m_b[:], ACT.Copy).then_inc(s("m_rounded"), 1)
            loop(a, KT, merge)

            def out_proj(it):
                for j in range(4):
                    blk = Blk(B_OUT, it, j)
                    step(blk)
                    read_out(blk, lambda l, h_: Y[:, bass.ds(it * 4 + j, 1), l:h_].rearrange("p a n -> p (a n)"), segs_x)
            a.wait_ge(s("gemm_done"), B_OUT)
            loop(a, KT // 4, out_proj)
            all_read(a, B_OUT + KT)
            sumsq(3, lambda k: Y[:, k, CTX:T], CTX)
            a.wait_ge(s("x_new"), 2 * KT)
            pre_norm(4, 2, CTX)
            ffn(1, B_FFN2, segs_x, True)
            all_read(a, NBLK)
            sumsq(5, lambda k: Y[:, k, CTX:T], CTX)

        @block.vector
        def _(v):
            def split(b):
                v.wait_ge(s("w_hi"), b.n + 1)
                v.tensor_tensor(w_lo[:, b.pair], raw[:, b.raw], w_hi[:, b.pair].bitcast(F32), ALU.subtract)\
                 .then_inc(s("w_split"), 1)

            def step(b):
                if not (isinstance(b.n, int) and b.n + 2 >= NBLK):
                    split(b.ahead(2))

            def mod_out(u, slot):
                v.wait_ge(s("mod_mm"), u + 1)
                if isinstance(u, int):
                    dst, bias = mod[:, u, :], vec[:, V_BMOD + u:V_BMOD + u + 1]
                else:
                    dst = mod[:, bass.ds(u, 1), :].rearrange("p a c -> p (a c)")
                    bias = vec[:, bass.ds(u + V_BMOD, 1)]
                v.tensor_scalar(dst, ps[:, 6 + slot, 0:2], bias, None, ALU.add).then_inc(s("mod_out"), 1)

            def derive(i, mi, vcol, add, mul):
                gain = vec[:, vcol:vcol + KT].unsqueeze(2).to_broadcast([P, KT, 2])
                return v.scalar_tensor_tensor(drv[:, i], mod[:, 8 * mi:8 * mi + 8, :], add if add else mul, gain,
                                              ALU.add if add else ALU.mult, ALU.mult)

            def rstd(r, lo):
                for k in range(KT):
                    v.wait_ge(s("sq_ready"), KT * r + k + 1)
                    if k == 0:
                        if r:
                            v.wait_ge(s("sq_used"), KT * r)
                        v.tensor_copy(n_acc[:, lo:T], n_sq[:, 0, lo:T]).then_inc(s("sq_used"), 1)
                    else:
                        v.wait_ge(s("sq_used"), KT * r + k)
                        v.tensor_tensor(n_acc[:, lo:T], n_acc[:, lo:T], n_sq[:, k % 2, lo:T], ALU.add).then_inc(s("sq_used"), 1)
                v.wait_ge(s("rstd"), r + 1)

            def pre_norm(r, p, lo):
                rstd(r, lo)
                mi = (0, 3, 6)[p]
                segs = segs_all if lo == 0 else segs_x

                def low(k):
                    v.wait_ge(s("h_rounded"), KT * p + k + 1)
                    v.wait_ge(s("h_full"), KT * p + k + 1)
                    v.tensor_tensor(h_lo[:, k, lo:T], n_t2[:, k % 2, lo:T], h_hi[:, k, lo:T].bitcast(F32), ALU.subtract)\
                     .then_inc(s("h_ready"), 1)
                if p:
                    v.wait_ge(s("h_ready"), KT * p)
                for k in range(KT):
                    v.tensor_tensor(n_t[:, k % 2, lo:T], X[:, k, lo:T], n_rs[:, lo:T], ALU.mult).then_inc(s("nrm_ready"), 1)
                    if k:
                        low(k - 1)
                    else:
                        v.wait_ge(s("nrm_ready"), KT * p + k + 1)
                    v.wait_ge(s("nrm_ready"), KT * p + k + 1)
                    if k >= 2:
                        v.wait_ge(s("h_ready"), KT * p + k - 1)
                    for l, h_, sg_ in segs:
                        last = v.tensor_scalar(n_t2[:, k % 2, l:h_], n_t[:, k % 2, l:h_], drv[:, 2 * p, k, sg_:sg_ + 1],
                                               mod[:, 8 * mi + k, sg_:sg_ + 1], ALU.mult, ALU.add)
                    last.then_inc(s("h_full"), 1)
                low(KT - 1)

            def post_norm(r, p, lo):
                rstd(r, lo)
                v.wait_ge(s("h_ready"), KT * (p + 1))
                for k in range(KT):
                    if k >= 2:
                        v.wait_ge(s("x_new"), KT * p + k - 1)
                    v.tensor_tensor(n_t[:, k % 2, lo:T], Y[:, k, lo:T], n_rs[:, lo:T], ALU.mult).then_inc(s("yn"), 1)
                    v.wait_ge(s("yn"), KT * p + k + 1)
                    for l, h_, sg_ in (segs_all if lo == 0 else segs_x):
                        last = v.scalar_tensor_tensor(X[:, k, l:h_], n_t[:, k % 2, l:h_], drv[:, 2 * p + 1, k, sg_:sg_ + 1],
                                                      X[:, k, l:h_], ALU.mult, ALU.add)
                    last.then_inc(s("x_new"), 1)
                v.wait_ge(s("x_new"), KT * (p + 1))

            def ffn(i, b0, seg_list, peel_last, mod_from=None):
                lo = seg_list[0][0]
                u0 = mod_from
                pairs = i * HID
                ys = 2 * KT * i
                for kind, b, n, c, hid in ffn_parts(b0):
                    lastpart = peel_last and kind == "down" and c == 2

                    def up(it, b=b, hid=hid, u0=u0):
                        for j in range(4):
                            blk = Blk(b, it, j)
                            step(blk)
                            if j % 2:
                                v.wait_ge(s("gemm_done"), blk.n + 1)
                                v.wait_ge(psum_read[1 - blk.pair], blk.ahead(-1).turn + 2)
                                v.wait_ge(s("g_ready"), it * 2 + (pairs + hid + j // 2 + 1))
                                for l, h_, sg_ in seg_list:
                                    last = v.tensor_tensor(gt[:, l:h_], sg[:, l:h_], bank(blk, sg_), ALU.mult)
                                last.then_inc(psum_read[blk.pair], 1)
                                p_ = it * 2 + j // 2
                                v.wait_ge(s("g_rounded"), it * 2 + (pairs + hid + j // 2 + 1))
                                v.tensor_tensor(g_lo[:, bass.ds(p_, 1), lo:T].rearrange("p a n -> p (a n)"), gt[:, lo:T],
                                                g_hi[:, bass.ds(p_, 1), lo:T].rearrange("p a n -> p (a n)").bitcast(F32),
                                                ALU.subtract).then_inc(s("g_ready"), 1)
                            if u0 is not None:
                                mod_out(it * 4 + (u0 + j), j % 2)

                    def down(it, b=b, c=c, u0=u0):
                        for j in range(4):
                            blk = Blk(b, it, j)
                            step(blk)
                            if c:
                                v.wait_ge(s("gemm_done"), blk.n + 1)
                                yk = Y[:, bass.ds(it * 4 + j, 1), :].rearrange("p a n -> p (a n)")
                                for l, h_, sg_ in seg_list:
                                    last = v.tensor_tensor(yk[:, l:h_], yk[:, l:h_], bank(blk, sg_), ALU.add)
                                last.then_inc(psum_read[blk.pair], 1)
                            if u0 is not None and j % 2:
                                mod_out(it * 2 + (u0 + j // 2), j // 2)
                    if kind == "down" and c:
                        all_read(v, b - 2 * FCH[c])
                    loop(v, n // 4, up if kind == "up" else down, lastpart)
                    if u0 is not None:
                        u0 += n if kind == "up" else n // 2
                all_read(v, b0 + N_FFN)

            zero, one, eps, eps_q = (small[:, i:i + 1] for i in range(4))
            v.memset(zero, 0.0)
            v.memset(one, 1.0)
            v.memset(eps, EPS)
            v.memset(eps_q, EPS * DH).then_inc(s("small_set"), 1)
            v.wait_ge(s("tables_loaded"), 16)
            split(Blk(0, 0, 0))
            split(Blk(0, 0, 1))
            for u in range(2):
                mod_out(u, u)

            def mod_pair_out(it):
                for j in range(2):
                    mod_out(it * 2 + (2 + j), j)
            loop(v, 7, mod_pair_out)
            v.wait_ge(s("mod_out"), 16)
            derive(0, 1, V_PRE1, 1.0, None).then_inc(s("drv"), 1)
            v.wait_ge(s("drv"), 1)
            pre_norm(0, 0, 0)
            ffn(0, B_FFN1, segs_all, False, 16)
            v.wait_ge(s("mod_out"), N_MOD)
            derive(1, 2, V_POST1, None, 0.5)
            derive(2, 4, V_PREM, 1.0, None)
            derive(3, 5, V_POSTM, None, 1.0)
            derive(4, 7, V_PRE2, 1.0, None)
            derive(5, 8, V_POST2, None, 0.5).then_inc(s("drv"), 1)
            v.wait_ge(s("drv"), 2)
            post_norm(1, 0, 0)
            pre_norm(2, 1, 0)

            def item(n, width, gain, dst_x, dst_c=None, bufs=(a_raw, a_rs, a_n), bk=6):
                v.wait_ge(s("at_rs"), n + 1)
                if dst_c is not None:
                    v.scalar_tensor_tensor(dst_c, bufs[0][:, 0:CTX], gain, bufs[1][:, 0:CTX], ALU.mult, ALU.mult)
                o = width - SEQ
                v.scalar_tensor_tensor(bufs[2][:, 0:SEQ], bufs[0][:, o:width], gain, bufs[1][:, o:width], ALU.mult, ALU.mult)\
                 .then_inc(s("at_nrm"), 1)
                v.wait_ge(s("at_nrm"), n + 1)
                if not (isinstance(n, int) and n == 0):
                    v.wait_ge(s("at_rot"), n)
                v.tensor_tensor(a_t1[:], bufs[2][:, 0:SEQ], rope_c, ALU.mult)
                v.wait_ge(s("at_swap"), n + 1)
                v.tensor_tensor(a_t2[:], ps[:, bk, :], rope_s, ALU.mult).then_inc(s("at_t2"), 1)
                v.wait_ge(s("at_t2"), n + 1)
                v.tensor_tensor(dst_x, a_t1[:], a_t2[:], ALU.add).then_inc(s("at_rot"), 1)

            v.wait_ge(s("cb_loaded"), 16)
            for j in range(2):
                step(Blk(B_KV, 0, j))
                item(j, T, vec[:, V_KN:V_KN + 1], a_kt[:, j, CTX:T], a_kt[:, j, 0:CTX])
            for j in range(2, 5):
                step(Blk(B_KV, 0, j))
            v.memset(bx[:], 0.0).then_inc(s("ba_bx"), 1)
            blk = Blk(B_KV, 0, 4)
            v.wait_ge(psum_read[blk.pair], blk.turn + 2)
            v.wait_ge(s("ba_bx"), 1)
            v.tensor_scalar(ba[32:48, :], ba[32:48, :], vec[32:48, V_DT:V_DT + 1], None, ALU.add).then_inc(s("ba_abs"), 1)
            v.wait_ge(s("ba_abs"), 1)
            v.scalar_tensor_tensor(bt[32:48, 0, :], ba[32:48, :], -1.0, ba[32:48, :], ALU.mult, ALU.max).then_inc(s("ba_abs"), 1)
            v.wait_ge(s("ba_e"), 1)
            v.tensor_scalar(bt[0:16, 1, :], bt[0:16, 0, :], 1.0, None, ALU.add).then_inc(s("ba_v"), 1)
            v.wait_ge(s("ba_v"), 1)
            v.reciprocal(bx[0:16, :], bt[0:16, 1, :])
            v.wait_ge(s("ba_e"), 4)
            v.scalar_tensor_tensor(bt[32:48, 1, :], ba[32:48, :], 0.0, bt[32:48, 0, :], ALU.max, ALU.add).then_inc(s("ba_v"), 1)
            v.wait_ge(s("ba_v"), 2)
            v.tensor_scalar(bx[32:48, :], bt[32:48, 1, :], small[32:48, 8:9], -1.0, ALU.mult, ALU.mult).then_inc(s("ba_bx"), 1)
            v.wait_ge(s("ba_tr"), 1)
            v.tensor_copy(bg[:].rearrange("p (b c) n -> p b c n", b=2),
                          ps[:, 6:8, 0:384].rearrange("p b (c n) -> p b c n", c=3)[:, :, :, 0:48]).then_inc(s("ba_bg"), 1)
            v.wait_ge(s("ba_sum"), 1)
            v.tensor_copy(bgt[:, 0, :], ps[:, 6, 0:96]).then_inc(s("ba_gc"), 1)
            v.wait_ge(s("ba_gc"), 1)
            def hc_of(t, d):
                return t[:, 48 * d:48 * d + 48].rearrange("p (c h) -> p h c", c=NCH)
            for d in range(2):
                v.tensor_copy(gall[:, :, G_GC + 6 * d:G_GC + 6 * d + 6], hc_of(bgt[:, 0], d))
                last = v.tensor_copy(gall[:, :, G_BETA + 6 * d:G_BETA + 6 * d + 6],
                                     bg[:, :, 8 * d:8 * d + 8].rearrange("p c h -> p h c"))
            last.then_inc(s("ba_gc"), 1)
            for d in range(2):
                last = v.tensor_tensor(hc_of(bgt[:, 2], d),
                                       ps[:, 6, 96:192].rearrange("p (c e h) -> p e h c", c=NCH, e=2)[:, d],
                                       hc_of(bgt[:, 0], d), ALU.subtract)
            last.then_inc(s("ba_gt"), 1)
            v.wait_ge(s("ba_x"), 1)
            v.wait_ge(s("ba_gc"), 2)
            for d in range(2):
                last = v.tensor_tensor(gall[:, :, G_BEG + 6 * d:G_BEG + 6 * d + 6],
                                       gall[:, :, G_BETA + 6 * d:G_BETA + 6 * d + 6], hc_of(bgt[:, 1], d), ALU.mult)
            v.wait_ge(s("ba_x"), 4)
            for d in range(2):
                last = v.tensor_copy(gall[:, :, G_KD + 6 * d:G_KD + 6 * d + 6], hc_of(bgt[:, 2], d))
            last.then_inc(s("gall"), 1)

            v.wait_ge(s("x_spilled"), 16)

            def queries(it):
                def query(j):
                    n = it * 4 + j
                    item(n + 2, SEQ, vec[:, V_QN:V_QN + 1], o_at[:, bass.ds(n, 1), :].rearrange("p a n -> p (a n)"),
                         bufs=(q_raw[j % 2], q_rs[j % 2], q_n[j % 2]), bk=6 + j % 2)
                for j in range(4):
                    step(Blk(B_Q, it, j))
                    if j:
                        query(j - 1)
                query(3)
            loop(v, 2, queries)

            def heads(it):
                def normalise(i):
                    t = i % 4
                    v.wait_ge(s("at_p"), it * 16 + (i + 1))
                    v.reciprocal(a_m[:, 2, t:t + 1], a_m[:, 2, t:t + 1]).then_inc(s("at_rc"), 1)
                    v.wait_ge(s("at_rc"), it * 16 + (i + 1))
                    v.tensor_scalar(a_p[:, i % 2, :], a_p[:, i % 2, :], a_m[:, 2, t:t + 1], None, ALU.mult)\
                     .then_inc(s("at_pn"), 1)
                for i in range(16):
                    t = i % 4
                    v.wait_ge(s("at_s"), it * 16 + (i + 1))
                    v.tensor_reduce(out=a_m[:, 0, t:t + 1], in_=ps[:, 4 + 2 * (i % 2):6 + 2 * (i % 2), 0:384],
                                    op=ALU.max, axis=AX.XY).then_inc(s("at_mx"), 1)
                    v.wait_ge(s("at_mx"), it * 16 + (i + 1))
                    v.tensor_scalar(a_m[:, 1, t:t + 1], a_m[:, 0, t:t + 1], -DH ** -0.5, None, ALU.mult)\
                     .then_inc(s("at_max"), 1)
                    if i:
                        normalise(i - 1)
                normalise(15)
            loop(v, 2, heads)

            def bc(x):
                return x.unsqueeze(2).to_broadcast([P, x.shape[1], P])

            v.wait_ge(s("gall"), 1)
            v.wait_ge(s("d_up0"), 1)

            def tables(h):
                v.tensor_copy(hc[:], gall[:, bass.ds(h, 1), :].rearrange("p a n -> p (a n)")).then_inc(s("hc"), 1)

            def dn_head(h, final):
                b = [Blk(B_DN, h, j) for j in range(4)]

                def conv(j):
                    v.wait_ge(psum_read[b[j].pair], b[j].turn + 2)
                    lo = CTX + 2 if j == 0 else 0
                    n = T + 2 - lo
                    c = d_c[:, j, lo:]
                    tap = [hc[:, 3 * j + i:3 * j + i + 1] for i in range(3)]
                    v.tensor_scalar(c, d_up[:, lo:lo + n], tap[0], None, ALU.mult).then_inc(s("tap"), 1)
                    v.wait_ge(s("tap"), h * 6 + 2 * j + 1)
                    v.scalar_tensor_tensor(c, d_up[:, lo + 1:lo + 1 + n], tap[1], c, ALU.mult, ALU.add).then_inc(s("tap"), 1)
                    v.wait_ge(s("tap"), h * 6 + 2 * j + 2)
                    v.scalar_tensor_tensor(c, d_up[:, lo + 2:lo + 2 + n], tap[2], c, ALU.mult, ALU.add).then_inc(s("conv"), 1)
                    step(b[j])
                v.wait_ge(s("hc"), h + 1)
                conv(0)
                for d in range(2):
                    v.wait_ge(s("d_row"), h * 2 + (d + 1))
                    v.tensor_tensor(d_q[:, d].rearrange("p (b c) n -> p b c n", b=2),
                                    hc[:, G_GC + 6 * d:G_GC + 6 * d + 6].rearrange("p (b c) -> p b c", b=2)
                                    .unsqueeze(3).to_broadcast([P, 2, 3, P]),
                                    ps[:, 4 + 2 * d:6 + 2 * d, 0:384].rearrange("p b (c n) -> p b c n", c=3), ALU.subtract)\
                     .then_inc(s("d_diff"), 1)
                    v.wait_ge(s("d_diff"), h * 2 + (d + 1))
                    v.tensor_scalar(d_t[:, d], d_q[:, d], 0.0, None, ALU.min).then_inc(s("d_mn"), 1)
                    v.tensor_scalar(d_r[:, d, 0:NC_X], d_q[:, d, NC_CTX:], 0.0, None, ALU.max).then_inc(s("d_mn"), 1)
                conv(1)
                conv(2)
                v.wait_ge(s("d_rstd"), h + 1)
                v.tensor_tensor(d_c[:, 1, 0:CTX], d_c[:, 1, 0:CTX], d_rs[:, SEQ:SEQ + CTX], ALU.mult)
                v.tensor_tensor(d_c[:, 1, CTX + 2:], d_c[:, 1, CTX + 2:], d_rs[:, SEQ + CTX:], ALU.mult).then_inc(s("d_qk"), 1)
                v.tensor_tensor(d_c[:, 0, CTX + 2:], d_c[:, 0, CTX + 2:], d_rs[:, 0:SEQ], ALU.mult).then_inc(s("d_qk"), 1)
                v.wait_ge(s("d_e1"), h * 2 + 1)
                v.tensor_tensor(d_t[:, 0], d_t[:, 0], bc(hc[:, G_BETA:G_BETA + 6]), ALU.mult).then_inc(s("d_eb0"), 1)

                def level(lv):
                    v.tensor_tensor(d_s[lv % 2][:, 0], d_l[:, 0], masks[:, 0, lv, :].unsqueeze(1).to_broadcast([P, NCH, P]),
                                    ALU.mult).then_inc(s("lvl0"), 1)
                for d in range(2):
                    v.wait_ge(s(f"d_eb{d}"), h + 1)
                    v.wait_ge(s("d_kk"), h + 1)
                    v.tensor_tensor(d_l[:, d].rearrange("p (b c) n -> p b (c n)", b=2),
                                    d_t[:, d].rearrange("p (b c) n -> p b (c n)", b=2), ps[:, 4:6, 0:384], ALU.mult)\
                     .then_inc(s("d_l"), 1)
                v.wait_ge(s("d_l"), h * 2 + 1)
                level(0)
                for d in range(2):
                    v.wait_ge(s("d_e2"), h * 2 + (d + 1))
                    v.tensor_tensor(d_at[:, d].rearrange("p c n -> p (c n)"), d_r[:, d, 0:NC_X].rearrange("p c n -> p (c n)"),
                                    ps[:, 6, :], ALU.mult).then_inc(s("d_am"), 1)
                step(b[3])
                for d in range(2):
                    v.wait_ge(s(f"lvl{d}"), h * 7 + 1)
                    v.tensor_tensor(d_t[:, d], ident.unsqueeze(1).to_broadcast([P, NCH, P]), d_s[0][:, d], ALU.subtract)
                level(1)
                for gr in range(4):
                    d, hf = gr // 2, gr % 2
                    v.wait_ge(s("sv_q"), h * 28 + gr + 1)
                    v.tensor_tensor(d_r[:, d, 3 * hf:3 * hf + 3], ident.unsqueeze(1).to_broadcast([P, 3, P]),
                                    ps[:, 4 + gr, 0:384].rearrange("p (c n) -> p c n", c=3), ALU.subtract)\
                     .then_inc(s("sv_r"), 1)
                v.wait_ge(s("sv_r"), h * 28 + 4)
                level(2)
                for lv in range(1, LEVELS):
                    for gr in range(4):
                        d, hf = gr // 2, gr % 2
                        v.wait_ge(s("sv_d"), h * 24 + 4 * (lv - 1) + gr + 1)
                        r_ = half(d_r[:, d, 3 * hf:3 * hf + 3], lv, 1 - d)
                        t_ = half(d_t[:, d, 3 * hf:3 * hf + 3], lv, d)
                        if lv < LEVELS - 1:
                            v.tensor_tensor(t_, t_, halves(ps[:, gr, 0:192], lv), ALU.subtract)
                        v.tensor_tensor(r_, r_, halves(ps[:, 4 + gr, 0:192], lv), ALU.subtract).then_inc(s("sv_r"), 1)
                    if lv + 2 < LEVELS:
                        level(lv + 2)
                    elif lv == LEVELS - 2:
                        v.wait_ge(s("d_tokc"), h * 2 + 2)
                        v.tensor_tensor(d_s[1][:, 0], d_ktok[:], bc(hc[:, G_BEG:G_BEG + 6]), ALU.mult).then_inc(s("d_kb0"), 1)
                for gr in range(4):
                    d, hf = gr // 2, gr % 2
                    v.wait_ge(s("uw"), h * 4 + gr + 1)
                    v.tensor_copy(d_t[:, d, 3 * hf:3 * hf + 3].rearrange("p c n -> p (c n)"), ps[:, gr, 0:384])\
                     .then_inc(s("w_c"), 1)
                v.wait_ge(s("u_c"), h * 4 + 4)
                for t in range(NCH):
                    for d in range(2):
                        c = ORDER[d][t]
                        if t:
                            v.wait_ge(s("sc_w"), h * 10 + 2 * (t - 1) + d + 1)
                            v.tensor_tensor(d_vn[:, d], d_q[:, d, c], ps[:, 4 + d, 0:P], ALU.subtract).then_inc(s("sc_v"), 1)
                    if t < NCH - 1:
                        for d in range(2):
                            c = ORDER[d][t]
                            v.wait_ge(s("sc_s"), h * 10 + 2 * t + d + 1)
                            if t == 0:
                                v.tensor_copy(d_st[:, d], ps[:, 6 + d, 0:P]).then_inc(s("sc_st"), 1)
                            else:
                                v.scalar_tensor_tensor(d_st[:, d], d_st[:, d], hc[:, G_DCY + 6 * d + c:G_DCY + 6 * d + c + 1],
                                                       ps[:, 6 + d, 0:P], ALU.mult, ALU.add).then_inc(s("sc_st"), 1)
                if not final:
                    v.wait_ge(s("sc_st"), h * 10 + 10)
                    tables(h + 1)
                v.wait_ge(s("od_copy"), h + 1)
                v.tensor_tensor(d_o[:], d_o[:], ps[:, 1, :], ALU.add).then_inc(s("od_sum"), 1)
                v.wait_ge(s("od_rstd"), h + 1)
                v.scalar_tensor_tensor(d_o[:], d_o[:], vec[:, V_DN:V_DN + 1], d_rs[:, 0:SEQ], ALU.mult, ALU.mult)\
                 .then_inc(s("od_v"), 1)
                v.wait_ge(s("od_v"), h + 1)
                v.tensor_tensor(o_dn[:, bass.ds(h, 1), :].rearrange("p a n -> p (a n)"), d_o[:], d_z[:], ALU.mult)\
                 .then_inc(s("head_done"), 1)
            tables(0)
            with v.Fori(0, H - 1, 1) as h:
                dn_head(h, False)
            dn_head(H - 1, True)

            for i, (src, hi, lo) in enumerate(((o_dn, odn_hi, odn_lo), (o_at, oat_hi, oat_lo))):
                v.wait_ge(s("o_rounded"), i + 1)
                v.tensor_tensor(lo[:], src[:], hi[:].bitcast(F32), ALU.subtract).then_inc(s("o_split"), 1)
            v.wait_ge(s("o_split"), 2)
            v.sem_inc(s("merged"), 1)

            def merge(it):
                for j in range(4):
                    blk = Blk(B_MERGE, it, j)
                    step(blk)
                    if j % 2:
                        v.wait_ge(psum_read[blk.pair], blk.turn + 2)
                        v.wait_ge(psum_read[1 - blk.pair], blk.ahead(-1).turn + 2)
                        m = (m_a, m_b)[j // 2]
                        v.tensor_tensor(m[:], m[:], m_s[:, j // 2, :], ALU.mult).then_inc(s("gated"), 1)
                v.wait_ge(s("gated"), it * 2 + 2)
                v.tensor_tensor(m_b[:], m_a[:], m_b[:], ALU.add).then_inc(s("merged"), 1)
                v.wait_ge(s("m_rounded"), it + 1)
                v.tensor_tensor(m_lo[:, bass.ds(it, 1), :].rearrange("p a n -> p (a n)"), m_b[:],
                                m_hi[:, bass.ds(it, 1), :].rearrange("p a n -> p (a n)").bitcast(F32), ALU.subtract)\
                 .then_inc(s("m_ready"), 1)
            loop(v, KT, merge)

            def out_proj(it):
                for j in range(4):
                    step(Blk(B_OUT, it, j))
            loop(v, KT // 4, out_proj)
            v.wait_ge(s("x_back"), 16)
            post_norm(3, 1, CTX)
            pre_norm(4, 2, CTX)
            ffn(1, B_FFN2, segs_x, True)
            post_norm(5, 2, CTX)

        @block.tensor
        def _(pe):
            def mm(out, lhsT, rhs, start=True, stop=True):
                return pe.matmul(out, lhsT, rhs, start=start, stop=stop)

            def gemm(b, hi, lo, seg_list, kt=KT, off=0, ready=None):
                pe.wait_ge(s("w_split"), b.n + 1)
                pe.wait_ge(psum_read[b.pair], b.turn + 1)
                for k in range(kt):
                    if ready is not None:
                        pe.wait_ge(s("h_ready"), ready + k + 1)
                    for i, (w, x) in enumerate(((w_hi, hi), (w_hi, lo), (w_lo, hi))):
                        for l, h_, sg_ in seg_list:
                            last = mm(bank(b, sg_), w[:, b.pair, k, :], x[:, k, l - off:h_ - off],
                                      k == 0 and i == 0, k == kt - 1 and i == 2)
                last.then_inc(s("gemm_done"), 1)

            def mod_mm(u, slot, load, first=False):
                pe.wait_ge(wmod_loaded[slot], (load + 1) * 16)
                if not first:
                    pe.wait_ge(s("mod_out"), u - 1)
                for k in range(KT):
                    last = mm(ps[:, 6 + slot, 0:2], w_mod[:, slot, k, :], silc[:, k, :], k == 0, k == KT - 1)
                last.then_inc(s("mod_mm"), 1)

            def sum_partitions(r, lo):
                pe.wait_ge(s("sq_used"), KT * (r + 1))
                for l, h_, sg_ in (segs_all if lo == 0 else segs_x):
                    last = mm(ps[:, 4 + sg_, 0:h_ - l], ones, n_acc[:, l:h_])
                last.then_inc(s("ss_ready"), 1)

            def ffn(i, b0, seg_list, mod_from=None):
                u0 = mod_from
                pairs = i * HID
                for kind, b, n, c, hid in ffn_parts(b0):
                    if kind == "up":
                        def body(it, b=b, u0=u0, c=c):
                            for j in range(4):
                                gemm(Blk(b, it, j), h_hi, h_lo, seg_list)
                                if u0 is not None:
                                    mod_mm(it * 4 + (u0 + j), j % 2, it * 2 + (u0 // 2 + j // 2))
                    else:
                        pe.wait_ge(s("g_ready"), pairs + hid + FCH[c] + 1)

                        def body(it, b=b, u0=u0, c=c):
                            for j in range(4):
                                gemm(Blk(b, it, j), g_hi, g_lo, seg_list, FCH[c])
                                if u0 is not None and j % 2:
                                    mod_mm(it * 2 + (u0 + j // 2), j // 2, it + u0 // 2)
                    loop(pe, n // 4, body)
                    if u0 is not None:
                        u0 += n if kind == "up" else n // 2

            pe.wait_ge(s("silc"), 1)
            for u in range(2):
                mod_mm(u, u, 0, True)

            def mod_pair(it):
                for j in range(2):
                    mod_mm(it * 2 + (2 + j), j, it + 1)
            loop(pe, 7, mod_pair)
            pe.wait_ge(s("ca_loaded"), 16)
            sum_partitions(0, 0)
            pe.wait_ge(s("h_ready"), KT)
            ffn(0, B_FFN1, segs_all, 16)
            sum_partitions(1, 0)
            sum_partitions(2, 0)
            pe.wait_ge(s("h_ready"), 2 * KT)

            for j in range(2):
                gemm(Blk(B_KV, 0, j), h_hi, h_lo, segs_all)
                pe.wait_ge(s("at_sq"), j + 1)
                mm(ps[:, 4, 0:CTX], ones, a_sq[:, 0:CTX])
                mm(ps[:, 5, 0:SEQ], ones, a_sq[:, CTX:T]).then_inc(s("at_ss"), 1)
                if j:
                    pe.wait_ge(s("at_rot"), j)
                pe.wait_ge(s("at_nrm"), j + 1)
                mm(ps[:, 6, :], swap, a_n[:, 0:SEQ]).then_inc(s("at_swap"), 1)
            pe.wait_ge(s("at_rot"), 2)
            for j in range(2, 4):
                blk = Blk(B_KV, 0, j)
                gemm(blk, h_hi, h_lo, segs_all)
                pe.wait_ge(psum_read[blk.pair], blk.turn + 2)
                if j == 3:
                    pe.wait_ge(s("at_vc"), 1)
                for c in range(NCH):
                    last = pe.transpose(ps[:, 6 + c // 3, P * (c % 3):P * (c % 3) + P], a_raw[:, P * c:P * c + P], ident)
                last.then_inc(s("at_vt"), 1)
            gemm(Blk(B_KV, 0, 4), h_hi, h_lo, segs_all)
            pe.wait_ge(s("ba_bx"), 2)
            pe.wait_ge(s("at_vc"), 2)
            for c in range(NCH):
                last = pe.transpose(ps[:, 6 + c // 3, P * (c % 3):P * (c % 3) + P], bx[:, P * c:P * c + P], ident)
            last.then_inc(s("ba_tr"), 1)
            pe.wait_ge(s("ba_bg"), 1)
            mm(ps[:, 6, 0:48], tri_le, bg[:, :, 32:40])
            mm(ps[:, 6, 48:96], tri_ge, bg[:, :, 40:48])
            mm(ps[:, 6, 96:192], ones, bg[:, :, 32:48]).then_inc(s("ba_sum"), 1)
            pe.wait_ge(s("ba_x"), 3)

            def queries(it):
                def q_sum(j):
                    n = it * 4 + j
                    pe.wait_ge(s("at_sq"), n + 3)
                    mm(ps[:, 4 + j % 2, :], ones, q_sq[j % 2]).then_inc(s("at_ss"), 1)

                def q_swap(j):
                    n = it * 4 + j
                    pe.wait_ge(s("at_nrm"), n + 3)
                    mm(ps[:, 6 + j % 2, :], swap, q_n[j % 2]).then_inc(s("at_swap"), 1)
                for j in range(4):
                    gemm(Blk(B_Q, it, j), h_hi, h_lo, segs_x)
                    if j >= 1:
                        q_sum(j - 1)
                    if j >= 2:
                        q_swap(j - 2)
                q_swap(2)
                q_sum(3)
                q_swap(3)
            loop(pe, 2, queries)
            pe.wait_ge(s("at_rot"), H + 2)

            def heads(it):
                pe.wait_ge(s("o_at"), it * 4 + 1)

                def scores(i):
                    j, t = i // 4, i % 4
                    if t == 0:
                        pe.wait_ge(s("at_qc"), it * 4 + (j + 1))
                    if i >= 2:
                        pe.wait_ge(s("at_p"), it * 16 + (i - 1))
                    for k in range(2):
                        last = mm(ps[:, 4 + 2 * (i % 2) + k, 0:384], a_q[:, j % 2, P * t:P * t + P],
                                  a_kt[:, bass.ds(it, 1), 384 * k:384 * k + 384].rearrange("p a n -> p (a n)"))
                    last.then_inc(s("at_s"), 1)
                scores(0)
                scores(1)
                for i in range(16):
                    j, t = i // 4, i % 4
                    pe.wait_ge(s("at_pn"), it * 16 + (i + 1))
                    if i:
                        pe.wait_ge(s("at_pt"), it * 16 + i)
                    for c in range(NCH):
                        last = pe.transpose(ps[:, c // 3, P * (c % 3):P * (c % 3) + P],
                                            a_p[:, i % 2, P * c:P * c + P], ident)
                    last.then_inc(s("at_tr"), 1)
                    if i < 14:
                        scores(i + 2)
                    if t == 3:
                        pe.wait_ge(s("at_pt"), it * 16 + (i + 1))
                        if j == 0:
                            pe.wait_ge(s("at_vcur"), it + 1)
                        if j >= 2:
                            pe.wait_ge(s("o_at"), it * 4 + j)
                        for c in range(NCH):
                            last = mm(ps[:, 2 + j % 2, :], a_vc[:, c], a_pt[j % 2][:, c], c == 0, c == NCH - 1)
                        last.then_inc(s("at_pv"), 1)
            loop(pe, 2, heads)

            pe.wait_ge(s("o_at"), H + 1)

            def dn_gemm(h, j):
                gemm(Blk(B_DN, h, j), h_hi, h_lo, segs_x if j in (0, 3, 4) else segs_all)

            def dn_head(h, final):
                b = [Blk(B_DN, h, j) for j in range(4)]
                pe.wait_ge(s("hc"), h + 1)
                for d in range(2):
                    for c in range(NCH):
                        g_ = hc[:, G_GC + 6 * d + c:G_GC + 6 * d + c + 1]
                        last = mm(ps[:, 4 + 2 * d + c // 3, P * (c % 3):P * (c % 3) + P], g_.to_broadcast([P, P]), ident)
                    last.then_inc(s("d_row"), 1)
                dn_gemm(h, 1)
                dn_gemm(h, 2)
                pe.wait_ge(s("d_sq"), h + 1)
                pe.wait_ge(s("d_qe"), h * 2 + 2)
                mm(ps[:, 4, :], ones, d_sq[:, 0:SEQ])
                mm(ps[:, 5, 0:CTX], ones, d_sq[:, SEQ:SEQ + CTX])
                mm(ps[:, 6, :], ones, d_sq[:, SEQ + CTX:]).then_inc(s("d_ss"), 1)
                dn_gemm(h, 3)
                off = [c * P + (2 if c >= NC_CTX else 0) for c in range(NCH)]

                def tokens(i):
                    for c in range(NCH):
                        last = pe.transpose(ps[:, 2 - 2 * i + c // 3, P * (c % 3):P * (c % 3) + P],
                                             d_c[:, 1 + i, off[c]:off[c] + P], ident)
                    last.then_inc(s("d_tok"), 1)
                pe.wait_ge(s("d_qk"), h * 2 + 1)
                for c in range(NCH):
                    kc = d_c[:, 1, off[c]:off[c] + P]
                    mm(ps[:, 4 + c // 3, P * (c % 3):P * (c % 3) + P], kc, kc)
                pe.wait_ge(s("d_qk"), h * 2 + 2)
                for c in range(NC_X):
                    last = mm(ps[:, 6, P * c:P * c + P], d_c[:, 1, off[c + NC_CTX]:off[c + NC_CTX] + P],
                               d_c[:, 0, off[c + NC_CTX]:off[c + NC_CTX] + P])
                last.then_inc(s("d_kk"), 1)
                pe.wait_ge(psum_read[b[2].pair], b[2].turn + 2)
                tokens(0)
                pe.wait_ge(psum_read[b[3].pair], b[3].turn + 2)
                pe.wait_ge(s("d_silu"), h * 3 + 3)
                tokens(1)
                pe.wait_ge(s("d_l"), h * 2 + 2)
                pe.wait_ge(s("d_am"), h * 2 + 2)
                for gr in range(4):
                    d, hf = gr // 2, gr % 2
                    pe.wait_ge(s(f"lvl{d}"), h * 7 + 1)
                    for i in range(3):
                        last = pe.transpose(ps[:, 4 + gr, P * i:P * i + P], d_s[0][:, d, 3 * hf + i], ident)
                    last.then_inc(s("sv_q"), 1)
                pe.wait_ge(s("d_tokc"), h * 2 + 2)
                for lv in range(1, LEVELS):
                    for gr in range(4):
                        d, hf = gr // 2, gr % 2
                        pe.wait_ge(s(f"lvl{d}"), h * 7 + lv + 1)
                        pe.wait_ge(s("sv_r"), h * 28 + 4 * (lv - 1) + gr + 1)
                        for i in range(3):
                            last = mm(ps[:, 4 + gr, P * i:P * i + P], d_s[lv % 2][:, d, 3 * hf + i], d_r[:, d, 3 * hf + i])
                        last.then_inc(s("sv_q"), 1)
                    for gr in range(4):
                        d, hf = gr // 2, gr % 2
                        pe.wait_ge(s("sv_qc"), h * 24 + 4 * (lv - 1) + gr + 1)
                        q3, t3 = (half(x[:, d, 3 * hf:3 * hf + 3], lv, o) for x, o in ((d_q, 1 - d), (d_t, d)))
                        for i in range(3):
                            last = mm(ps[:, 4 + gr, 64 * i:64 * i + 64], d_t[:, d, 3 * hf + i], q3[:, i])
                        if lv < LEVELS - 1:
                            for i in range(3):
                                last = mm(ps[:, gr, 64 * i:64 * i + 64], d_q[:, d, 3 * hf + i], t3[:, i])
                        last.then_inc(s("sv_d"), 1)
                pe.wait_ge(s("d_kbvb"), h * 3 + 3)
                pe.wait_ge(s("d_kb0"), h + 1)
                for gr in range(4):
                    d, hf = gr // 2, gr % 2
                    pe.wait_ge(s("sv_r"), h * 28 + 24 + gr + 1)
                    for i in range(3):
                        mm(ps[:, 4 + gr, P * i:P * i + P], d_r[:, d, 3 * hf + i], d_l[:, d, 3 * hf + i])
                    for i in range(3):
                        last = mm(ps[:, gr, P * i:P * i + P], d_s[1][:, d, 3 * hf + i], d_r[:, d, 3 * hf + i])
                    last.then_inc(s("uw"), 1)
                pe.wait_ge(s("w_c"), h * 4 + 4)
                pe.wait_ge(s("u_c"), h * 4 + 4)
                pe.wait_ge(s("d_kd"), h * 2 + 2)
                pe.wait_ge(s("d_qd"), h * 2 + 2)
                pe.wait_ge(s("d_at"), h * 2 + 2)
                for t in range(NCH):
                    if t:
                        for d in range(2):
                            pe.wait_ge(s("sc_st"), h * 10 + 2 * (t - 1) + d + 1)
                            mm(ps[:, 4 + d, 0:P], d_t[:, d, ORDER[d][t]], d_st[:, d]).then_inc(s("sc_w"), 1)
                    for d in range(2):
                        c = ORDER[d][t]
                        vn = d_q[:, d, c]
                        if t:
                            vn = d_vn[:, d]
                            if c >= NC_CTX:
                                mm(ps[:, d, P * (c - NC_CTX):P * (c - NC_CTX) + P], d_st[:, d], d_qd[:, d, c - NC_CTX], True, False)
                            pe.wait_ge(s("sc_v"), h * 10 + 2 * (t - 1) + d + 1)
                        if t < NCH - 1:
                            mm(ps[:, 6 + d, 0:P], d_kd[:, d, c], vn).then_inc(s("sc_s"), 1)
                        if c >= NC_CTX:
                            mm(ps[:, d, P * (c - NC_CTX):P * (c - NC_CTX) + P], vn, d_at[:, d, c - NC_CTX], False, True)\
                                .then_inc(s("sc_o"), 1)
                if not final:
                    dn_gemm(h, 4)
                pe.wait_ge(s("od_sq"), h + 1)
                mm(ps[:, 2, :], ones, d_sq[:, 0:SEQ]).then_inc(s("od_ss"), 1)
            dn_gemm(0, 0)
            with pe.Fori(0, H - 1, 1) as h:
                dn_head(h, False)
            dn_head(H - 1, True)

            pe.wait_ge(s("o_split"), 2)

            def merge(it):
                for j in range(4):
                    hi, lo, off = ((odn_hi, odn_lo, CTX), (h_hi, h_lo, 0), (oat_hi, oat_lo, CTX), (h_hi, h_lo, 0))[j]
                    gemm(Blk(B_MERGE, it, j), hi, lo, segs_x, off=off)
            loop(pe, KT, merge)
            pe.wait_ge(s("m_ready"), KT)

            def out_proj(it):
                for j in range(4):
                    gemm(Blk(B_OUT, it, j), m_hi, m_lo, segs_x, off=CTX)
            loop(pe, KT // 4, out_proj)
            sum_partitions(3, CTX)
            sum_partitions(4, CTX)
            pe.wait_ge(s("h_ready"), 3 * KT)
            ffn(1, B_FFN2, segs_x)
            sum_partitions(5, CTX)


ORDER = [list(range(NCH)), list(range(NC_CTX))[::-1] + list(range(NC_CTX, NCH))[::-1]]


def _constants():
    i = np.arange(P)
    eye = np.eye(P, dtype=np.float32)
    swap = np.zeros((P, P), np.float32)
    swap[i ^ 32, i] = 1.0
    ca = np.stack([eye, np.ones((P, P), np.float32), (i[:, None] >= i[None, :]).astype(np.float32),
                   (i[:, None] <= i[None, :]).astype(np.float32), swap], 1)
    masks = np.zeros((P, 2, LEVELS, P), np.float32)
    for l in range(LEVELS):
        b = 1 << l
        m = (i[:, None] // (2 * b) == i[None, :] // (2 * b)) & (i[:, None] // b % 2 == 1) & (i[None, :] // b % 2 == 0)
        masks[:, 0, l] = m
        masks[:, 1, l] = m.T
    nf = DH // 4
    inv = (np.float32(10000.0) ** (-np.arange(nf, dtype=np.float32) / np.float32(nf))).astype(np.float32)
    pos = np.stack([np.repeat(np.arange(SEQ // 64), 64), np.tile(np.arange(64), SEQ // 64)]).astype(np.float32)
    ang = pos[:, None, :] * inv[None, :, None]
    cos = np.cos(ang, dtype=np.float32)
    sin = np.sin(ang, dtype=np.float32)
    c = np.stack([cos, cos], 1).reshape(P, SEQ)
    s_ = np.stack([-sin, sin], 1).reshape(P, SEQ)
    cb = np.concatenate([masks.reshape(P, -1), c, s_], 1)
    return np.ascontiguousarray(ca), np.ascontiguousarray(cb, dtype=np.float32)


def _tiles(w):
    K, N = w.shape
    t = w.reshape(K // P, P, N // P, P).transpose(2, 1, 0, 3)
    if K < D:
        t = np.concatenate([t, np.zeros((N // P, P, KT - K // P, P), w.dtype)], 2)
    return t.reshape(N // P, P, D)


def _ffn_blocks(w_gu, w_down):
    gu = _tiles(w_gu)
    out, hid = [], 0
    for n in FCH:
        pair = np.stack([gu[hid:hid + n], gu[HID + hid:HID + hid + n]], 1)
        out += [pair.reshape(2 * n, P, D), _tiles(w_down[hid * P:(hid + n) * P])]
        hid += n
    return out


def layout(i):
    w_in = i["w_in"][0]
    qkv, z = w_in[:, 0:3072], w_in[:, 3072:4096]
    w_ba, w_q, w_kv, w_g = w_in[:, 4096:4128], w_in[:, 4128:5152], w_in[:, 5152:5664], w_in[:, 5664:7712]
    pad = np.zeros((D, P), w_in.dtype)
    pad[:, 0:16] = w_ba[:, 0:16]
    pad[:, 32:48] = w_ba[:, 16:32]
    dn = np.stack([_tiles(qkv[:, 0:1024]), _tiles(qkv[:, 1024:2048]), _tiles(qkv[:, 2048:3072]), _tiles(z)], 1)
    mg = np.stack([_tiles(i["w_dn_out"][0]), _tiles(w_g[:, 0:1024]), _tiles(i["w_attn_out"][0]),
                   _tiles(w_g[:, 1024:2048])], 1)
    W = np.concatenate(_ffn_blocks(i["ffn1_w_gu"][0], i["ffn1_w_down"][0])
                       + [_tiles(w_kv), _tiles(pad), _tiles(w_q), dn.reshape(-1, P, D), mg.reshape(-1, P, D),
                          _tiles(i["w_out"][0])]
                       + _ffn_blocks(i["ffn2_w_gu"][0], i["ffn2_w_down"][0]))
    col = lambda a: a.reshape(-1, P).T
    gates = np.zeros((P, 2), np.float32)
    gates[32:48, 0] = i["dn_a_log"][0].reshape(-1)
    gates[32:48, 1] = i["dn_dt_bias"][0].reshape(-1)
    cc = np.stack([col(i["c_ctx"]), col(i["c"][0])], 2).reshape(P, -1)
    vec = np.concatenate([col(i[n][0]) for n in ("ffn1_pre", "ffn1_post", "mix_pre", "mix_post", "ffn2_pre", "ffn2_post",
                                                 "b_mod", "attn_q_norm", "attn_k_norm", "dn_out_norm")] + [gates, cc], 1)
    conv = i["dn_conv"][0].reshape(3, 3, H, P).transpose(3, 2, 1, 0).reshape(P, H, 9)
    ca, cb = _constants()
    return dict(W=W, WMOD=_tiles(i["w_mod"][0]), XT=np.concatenate([i["ctx"][0], i["x"][0]]).T,
                VEC=vec, CONV=conv, CA=ca, CB=cb)


def kernel(**inputs):
    import concourse.bacc as bacc
    from concourse.bass_utils import run_bass_kernel_spmd as run

    arrays = {k: np.ascontiguousarray(a) for k, a in layout({k: np.asarray(a) for k, a in inputs.items()}).items()}
    nc = bacc.Bacc("TRN2", target_bir_lowering=False, num_devices=1)
    args = [nc.dram_tensor(k, a.shape, F32, kind="ExternalInput").ap() for k, a in arrays.items()]
    out = nc.dram_tensor("out", [D, SEQ], F32, kind="ExternalOutput").ap()
    spill = nc.dram_tensor("x_spill", [P, KT, SEQ], F32, kind="Internal").ap()
    build(nc, *args, out, spill)
    r = run(nc, [arrays], core_ids=[0])
    return np.ascontiguousarray(r.results[0]["out"].T).reshape(1, SEQ, D)
```

```python
import numpy as np

import concourse.bass as bass
from concourse import mybir
from concourse.alu_op_type import AluOpType as ALU
from contextlib import ExitStack

ACT = mybir.ActivationFunctionType
AX = mybir.AxisListType
F32 = mybir.dt.float32
F32R = mybir.dt.float32r

P = 128
D = 1024
KT = D // P
CTX, SEQ = 256, 512
T = CTX + SEQ
NC_CTX, NC_X = CTX // P, SEQ // P
NCH = NC_CTX + NC_X
EPS = 1e-6
H = 8
HKV = 2
DH = 128
HID = 2816 // P
FCH = [8, 8, 6]
RING = 4

N_FFN = 2 * HID + 3 * KT
B_FFN1 = 0
B_KV = B_FFN1 + N_FFN
B_Q = B_KV + 5
B_DN = B_Q + H
B_MERGE = B_DN + 4 * H
B_OUT = B_MERGE + 4 * KT
B_FFN2 = B_OUT + KT
NBLK = B_FFN2 + N_FFN

N_MOD = 72
N_MOD0 = 16
DVE_MOD0 = [8, 9, 10, 11, 12, 13]
LEVELS = 7

V_PRE1, V_POST1, V_PREM, V_POSTM, V_PRE2, V_POST2 = range(0, 48, 8)
V_BMOD = 48
V_QN, V_KN, V_DN, V_ALOG, V_DT = range(V_BMOD + N_MOD, V_BMOD + N_MOD + 5)
V_C = V_DT + 1
NV = V_C + 2 * KT
G_CONV, G_BETA, G_GC, G_BEG, G_KD, G_DCY = 0, 9, 21, 33, 45, 57
NG = 69


class Blk:

    def __init__(self, base, it, j):
        at = base + j
        self.n = at + it * 4
        self.raw = at % RING
        self.pair = at % 2
        self.turn = at // 2 + it * 2
        self.load = at // RING + it
        self.base, self.it, self.j = base, it, j

    def ahead(self, d):
        return Blk(self.base, self.it, self.j + d)


def build(nc, W, WMOD, XT, VEC, CONV, CA, CB, OUT, XS):
    ctx = ExitStack()
    with ctx:
        base0 = 16512

        def at(name, kb, shape, dt=F32):
            return nc.alloc_sbuf_tensor_at(name, [P] + shape, dt, offset=base0 + int(kb * 1024))

        def sem(name):
            return ctx.enter_context(nc.semaphore(name))

        raw = at("raw", 0, [RING, KT, P])
        w_hi = at("w_hi", 16, [2, KT, P], F32R)
        w_lo = at("w_lo", 24, [2, KT, P], F32R)
        h_hi = at("h_hi", 32, [KT, T], F32R)
        h_lo = at("h_lo", 56, [KT, T], F32R)
        ca = at("ca", 80, [5, P])
        vec = at("vec", 82.5, [NV])
        mod = at("mod", 83.25, [N_MOD, 2])
        drv = at("drv", 84, [6, KT, 2])
        silc = at("silc", 84.5, [KT, 2])
        small = at("small", 84.625, [32])
        gall = at("gall", 85, [H, NG])
        cb = at("cb", 87.5, [14 * P + 2 * SEQ])
        w_mod = at("w_mod", 87.5, [2, KT, P])
        ident, ones, tri_ge, tri_le, swap = (ca[:, i, :] for i in range(5))
        masks = cb[:, 0:14 * P].rearrange("p (d l m) -> p d l m", d=2, l=LEVELS)
        rope_c = cb[:, 14 * P:14 * P + SEQ]
        rope_s = cb[:, 14 * P + SEQ:14 * P + 2 * SEQ]
        X = at("X", 100, [KT, T])
        g_hi = at("g_hi", 124, [8, T], F32R)
        g_lo = at("g_lo", 148, [8, T], F32R)
        Y = at("Y", 172, [KT, T])
        sg = at("sg", 196, [T])
        gt = at("gt", 199, [T])
        w_mod0 = [at("w_mod0", 56, [4, KT * P])] + [at(f"w_mod{4 * i}", 132 + 16 * i, [4, KT * P]) for i in (1, 2, 3)]
        m_part = at("m_part", 203, [2, 2, P])
        m0_part = at("m0_part", 196, [len(DVE_MOD0), 2, P])
        y_acc = at("y_acc", 95.5, [T])

        n_sq = at("n_sq", 124, [2, T])
        n_acc = at("n_acc", 130, [T])
        n_rs = at("n_rs", 133, [T])
        n_t = at("n_t", 136, [2, T])
        n_t2 = at("n_t2", 142, [2, T])
        o_at = at("o_at", 100, [H, SEQ])
        a_kt = at("a_kt", 132, [HKV, T])
        a_v = at("a_v", 138, [NCH, HKV, P])
        a_vc = at("a_vc", 144, [NCH, P])
        a_raw = at("a_raw", 147, [T])
        a_sq = at("a_sq", 150, [T])
        a_rs = at("a_rs", 153, [T])
        a_n = at("a_n", 156, [T])
        a_t1 = at("a_t1", 159, [SEQ])
        a_t2 = at("a_t2", 161, [SEQ])
        a_q = at("a_q", 163, [2, SEQ])
        a_p = at("a_p", 200, [2, T])
        a_pt = [at("a_pt0", 167, [NCH, SEQ]), at("a_pt1", 184, [NCH, SEQ])]
        a_m = at("a_m", 183, [3, 4])
        q_raw, q_sq, q_rs, q_n = ([b0[:, 0:SEQ], at(f"q_{n}1", 171 + 2 * i, [SEQ])[:]]
                                  for i, (n, b0) in enumerate((("raw", a_raw), ("sq", a_sq), ("rs", a_rs), ("n", a_n))))
        ba = at("ba", 184, [T])
        bx = at("bx", 187, [T])
        bt = at("bt", 190, [2, T])
        bg = at("bg", 196, [NCH, 48])
        bgt = at("bgt", 197.25, [3, 96])
        o_dn = at("o_dn", 116, [H, SEQ])
        M6 = NCH * P
        d_l = at("d_l", 132, [2, NCH, P])
        d_t = at("d_t", 138, [2, NCH, P])
        d_r = at("d_r", 144, [2, NCH, P])
        d_q = at("d_q", 150, [2, NCH, P])
        d_s = [at(f"d_s{i}", 156 + 6 * i, [2, NCH, P]) for i in range(2)]
        d_kd = at("d_kd", 168, [2, NCH, P])
        d_rs = at("d_rs", 168, [SEQ + T])
        d_at = at("d_at", 174, [2, NC_X, P])
        d_qd = at("d_qd", 178, [2, NC_X, P])
        d_ktok = at("d_ktok", 182, [NCH, P])
        d_vtok = at("d_vtok", 185, [NCH, P])
        d_sq = at("d_sq", 182, [SEQ + T])
        d_c = at("d_c", 188, [3, T + 2])
        d_up = at("d_up", 197.125, [T + 4])
        d_z = at("d_z", 200.25, [SEQ])
        d_st = at("d_st", 202.25, [2, P])
        d_vn = at("d_vn", 203.25, [2, P])
        d_o = at("d_o", 204.25, [SEQ])
        hc = at("hc", 206.25, [NG])
        odn_hi = at("odn_hi", 132, [H, SEQ], F32R)
        odn_lo = at("odn_lo", 148, [H, SEQ], F32R)
        oat_hi = at("oat_hi", 164, [H, SEQ], F32R)
        oat_lo = at("oat_lo", 180, [H, SEQ], F32R)
        m_hi = at("m_hi", 100, [KT, SEQ], F32R)
        m_lo = at("m_lo", 116, [KT, SEQ], F32R)
        m_a = at("m_a", 196, [SEQ])
        m_b = at("m_b", 198, [SEQ])
        m_s = at("m_s", 200, [2, SEQ])
        y_o = at("y_o", 132, [KT, SEQ])

        ps = ctx.enter_context(nc.psum_tensor("ps", [P, 8, 512], F32))

        S = {}

        def s(name):
            if name not in S:
                S[name] = sem(name)
            return S[name]

        w_loaded = [s(f"w_loaded{i}") for i in range(RING)]
        wmod_loaded = [s(f"wmod_loaded{i}") for i in range(2)]
        psum_read = [s(f"psum_read{i}") for i in range(2)]

        SQ = {0: 0, 2: 1, 4: 2}
        segs_all = [(0, CTX, 0), (CTX, T, 1)]
        segs_x = [(CTX, T, 1)]

        def bank(blk, seg):
            b = 2 * blk.pair + seg
            return ps[:, b, 0:(CTX, SEQ)[seg]]

        def half(x, lv, odd):
            n = 1 << lv
            return x.rearrange("p c (b e n) -> p c b e n", e=2, n=n)[:, :, :, odd, :]

        def halves(x, lv):
            return x.rearrange("p (c b n) -> p c b n", c=3, n=1 << lv)

        def loop(eng, iters, body, peel=False):
            if iters - peel > 0:
                with eng.Fori(0, iters - peel, 1) as it:
                    body(it)
            if peel:
                body(iters - 1)

        def all_read(eng, blocks):
            for p_ in range(2):
                eng.wait_ge(psum_read[p_], (blocks + 1 - p_) // 2 + 1)

        def ffn_parts(b0):
            b, hid = b0, 0
            for c, n in enumerate(FCH):
                yield "up", b, 2 * n, c, hid
                b += 2 * n
                yield "down", b, KT, c, hid
                b += KT
                hid += n


        block = ctx.enter_context(nc.Block())

        @block.sync
        def _(sp):
            sp.dma_start(vec[:], VEC).then_inc(s("tables_loaded"), 16)
            for i in range(N_MOD0 // 4):
                sp.dma_start(w_mod0[i][:], WMOD[4 * i:4 * i + 4].rearrange("u p n -> p u n")).then_inc(s(f"mod0_loaded{i}"), 16)
                if i == 0:
                    sp.dma_start(X[:], XT.rearrange("(k p) t -> p k t", p=P)).then_inc(s("x_loaded"), 16)
            sp.dma_start(ca[:], CA).then_inc(s("ca_loaded"), 16)
            sp.dma_start(gall[:, :, 0:9], CONV).then_inc(s("conv_loaded"), 16)
            Wv = W.rearrange("b p (k n) -> b p k n", k=KT)
            for b in range(RING):
                sp.dma_start(raw[:, b], Wv[b]).then_inc(w_loaded[b], 16)

            def load(n, slot):
                sp.wait_ge(s("w_split"), n - RING + 1)
                sp.dma_start(raw[:, slot], Wv[bass.ds(n, 1)].rearrange("b p k n -> p (b k) n"))\
                  .then_inc(w_loaded[slot], 16)

            with sp.Fori(0, NBLK // RING - 1, 1) as it:
                for j in range(RING):
                    load(it * RING + (RING + j), j)
            for n in range(NBLK // RING * RING, NBLK):
                load(n, n % RING)
            for k in range(0, KT, 2):
                sp.wait_ge(s("x_new"), 2 * KT + k + 2)
                sp.dma_start(OUT.rearrange("(k p) t -> p k t", p=P)[:, k:k + 2], X[:, k:k + 2, CTX:T]).then_inc(s("stored"), 16)
            sp.wait_ge(s("stored"), 16 * (KT // 2))

        @block.gpsimd
        def _(g):
            g.sem_inc(psum_read[0], 1)
            g.sem_inc(psum_read[1], 1)
            g.sem_inc(s("g_ready"), 1)
            g.sem_inc(s("o_at"), 1)
            g.sem_inc(s("head_done"), 1)

            g.sem_inc(s("mod_fold"), 1)
            g.sem_inc(s("ysq_used"), 1)

            Mv = WMOD.rearrange("u p (k n) -> u p k n", k=KT)
            for u in range(2):
                g.dma_start(w_mod[:, u], Mv[N_MOD0 + u]).then_inc(wmod_loaded[u], 16)
            with g.Fori(0, (N_MOD - N_MOD0) // 2 - 1, 1) as it:
                for u in range(2):
                    g.wait_ge(s("mod_part"), it * 2 + (u + 2))
                    g.dma_start(w_mod[:, u], Mv[bass.ds(it * 2 + (N_MOD0 + 2 + u), 1)].rearrange("b p k n -> p (b k) n"))\
                     .then_inc(wmod_loaded[u], 16)
            g.wait_ge(s("mod_part"), N_MOD - N_MOD0 + 1)
            g.wait_ge(s("ss_ready"), 2)
            g.dma_start(cb[:], CB).then_inc(s("cb_loaded"), 16)
            g.wait_ge(s("h_ready"), 2 * KT)
            g.dma_start(XS, X[:, :, CTX:T]).then_inc(s("x_spilled"), 16)
            g.wait_ge(s("x_spilled"), 16)
            def q_copies(it):
                g.wait_ge(s("o_at"), it * 4 + 1)
                for j in range(4):
                    g.wait_ge(s("at_rot"), it * 4 + (j + 3))
                    if j >= 2:
                        g.wait_ge(s("at_s"), it * 16 + 4 * (j - 1))
                    g.tensor_copy(a_q[:, j % 2, :], o_at[:, bass.ds(it * 4 + j, 1), :].rearrange("p a n -> p (a n)"))\
                     .then_inc(s("at_qc"), 1)
            loop(g, 2, q_copies)
            g.wait_ge(s("cb_loaded"), 16)
            g.wait_ge(s("o_at"), H + 1)
            g.memset(d_up[:], 0.0).then_inc(s("d_up0"), 1)

            def bc(x):
                return x.unsqueeze(2).to_broadcast([P, x.shape[1], P])

            def head(h):
                g.wait_ge(s("d_e1"), h * 2 + 2)
                g.tensor_tensor(d_t[:, 1], d_t[:, 1], bc(hc[:, G_BETA + 6:G_BETA + 12]), ALU.mult).then_inc(s("d_eb1"), 1)

                def level(lv):
                    g.tensor_tensor(d_s[lv % 2][:, 1], d_l[:, 1], masks[:, 1, lv, :].unsqueeze(1).to_broadcast([P, NCH, P]),
                                    ALU.mult).then_inc(s("lvl1"), 1)
                g.wait_ge(s("d_l"), h * 2 + 1)
                level(0)
                level(1)
                for d in range(2):
                    g.wait_ge(s("d_am"), h * 2 + (d + 1))
                    tri = (tri_le, tri_ge)[d]
                    g.tensor_tensor(d_at[:, d], d_at[:, d], tri.unsqueeze(1).to_broadcast([P, NC_X, P]),
                                    ALU.mult).then_inc(s("d_at"), 1)
                for lv in range(2, LEVELS):
                    if lv == 2:
                        g.wait_ge(s("t_set"), h + 1)
                    g.wait_ge(s("sv_q"), h * 28 + 4 * (lv - 2) + 4)
                    level(lv)
                    if lv == 2:
                        for d in range(2):
                            g.wait_ge(s("d_qe"), h * 2 + (d + 1))
                            g.tensor_tensor(d_qd[:, d], d_qd[:, d],
                                            d_c[:, 0, CTX + 2:T + 2].rearrange("p (c n) -> p c n", c=NC_X),
                                            ALU.mult).then_inc(s("d_qd"), 1)
                        g.wait_ge(s("d_tokc"), h * 2 + 2)
                    if lv in (3, 4):
                        d = lv - 3
                        g.tensor_tensor(d_kd[:, d], d_ktok[:], bc(hc[:, G_KD + 6 * d:G_KD + 6 * d + 6]),
                                        ALU.mult).then_inc(s("d_kd"), 1)
                for d in range(2):
                    g.wait_ge(s(f"lvl{d}"), h * 7 + 7)
                    g.tensor_tensor(d_l[:, d], d_vtok[:], bc(hc[:, G_BETA + 6 * d:G_BETA + 6 * d + 6]),
                                    ALU.mult).then_inc(s("d_kbvb"), 1)
                g.wait_ge(s("sv_q"), h * 28 + 24)
                g.tensor_tensor(d_s[1][:, 1], d_ktok[:], bc(hc[:, G_BEG + 6:G_BEG + 12]), ALU.mult).then_inc(s("d_kbvb"), 1)

            with g.Fori(0, H, 1) as h:
                head(h)
            g.wait_ge(s("gemm_done"), B_OUT + KT)
            g.dma_start(X[:, :, CTX:T], XS).then_inc(s("x_back"), 16)
            g.wait_ge(s("x_back"), 16)

        @block.scalar
        def _(a):
            zero, one, eps, eps_q = (small[:, i:i + 1] for i in range(4))

            def split(b):
                a.wait_ge(w_loaded[b.raw], (b.load + 1) * 16)
                a.activation(w_hi[:, b.pair], raw[:, b.raw], ACT.Copy).then_inc(s("w_hi"), 1)

            def step(b):
                a.wait_ge(s("gemm_done"), b.n + 1)
                if not (isinstance(b.n, int) and b.n + 2 >= NBLK):
                    split(b.ahead(2))

            def read_out(b, dst, seg_list, func=ACT.Copy):
                for lo, hi, sg_ in seg_list:
                    last = a.activation(dst(lo, hi), bank(b, sg_), func)
                last.then_inc(psum_read[b.pair], 1)

            def squares(r, src, lo, ready=None):
                q = SQ[r]
                for k in range(KT):
                    if q or k >= 2:
                        a.wait_ge(s("sq_used"), KT * q + k - 1)
                    if ready is not None:
                        a.wait_ge(s("x_new"), ready + k + 1)
                    a.activation(n_sq[:, k % 2, lo:T], src(k), ACT.Square).then_inc(s("sq_ready"), 1)

            def rstd(r, lo):
                if r in (2, 4):
                    a.wait_ge(s("sq_used"), KT * (SQ[r] + 1))
                else:
                    a.wait_ge(s("ss_ready"), (r + 1) // 2 + 1)
                segs = segs_all if lo == 0 else segs_x
                for l, h_, sg_ in segs:
                    last = a.activation(n_rs[:, l:h_], ps[:, 4 + sg_, 0:h_ - l], ACT.Ln, bias=eps, scale=1.0 / D)
                last.then_inc(s("ln_ready"), 1)
                a.wait_ge(s("ln_ready"), r + 1)
                a.activation(n_rs[:, lo:T], n_rs[:, lo:T], ACT.Exp, scale=-0.5).then_inc(s("rstd"), 1)

            def pre_norm(r, p, lo):
                if r:
                    squares(r, lambda k: X[:, k, lo:T], lo, KT * (p - 1))
                rstd(r, lo)
                mi = (0, 3, 6)[p]
                for k in range(KT):
                    a.wait_ge(s("nrm_ready"), KT * p + k + 1)
                    if k >= 2:
                        a.wait_ge(s("h_ready"), KT * p + k - 1)
                    for l, h_, sg_ in (segs_all if lo == 0 else segs_x):
                        last = a.activation(n_t2[:, k % 2, l:h_], n_t[:, k % 2, l:h_], ACT.Identity,
                                            bias=mod[:, 8 * mi + k, sg_:sg_ + 1], scale=drv[:, 2 * p, k, sg_:sg_ + 1])
                    last.then_inc(s("h_full"), 1)
                    a.wait_ge(s("h_full"), KT * p + k + 1)
                    a.activation(h_hi[:, k, lo:T], n_t2[:, k % 2, lo:T], ACT.Copy).then_inc(s("h_rounded"), 1)

            def ffn(i, b0, seg_list, peel_last):
                lo = seg_list[0][0]
                for kind, b, n, c, hid in ffn_parts(b0):
                    lastpart = peel_last and kind == "down" and c == 2

                    def up(it):
                        for j in range(4):
                            blk = Blk(b, it, j)
                            step(blk)
                            if j % 2 == 0:
                                read_out(blk, lambda l, h_: sg[:, l:h_], seg_list, ACT.Silu)
                            else:
                                a.wait_ge(psum_read[blk.pair], blk.turn + 2)
                                p_ = it * 2 + j // 2
                                a.activation(g_hi[:, bass.ds(p_, 1), lo:T].rearrange("p a n -> p (a n)"), gt[:, lo:T],
                                             ACT.Copy).then_inc(s("g_rounded"), 1)

                    def down(it):
                        for j in range(4):
                            blk = Blk(b, it, j)
                            step(blk)
                            if c == 0:
                                read_out(blk, lambda l, h_: Y[:, bass.ds(it * 4 + j, 1), l:h_].rearrange("p a n -> p (a n)"),
                                         seg_list)
                            if c == len(FCH) - 1:
                                a.wait_ge(psum_read[blk.pair], blk.turn + 2)
                                a.wait_ge(s("ysq_used"), it * 4 + (18 * i + j + 1))
                                a.activation((sg, gt)[j % 2][:, lo:T], Y[:, bass.ds(it * 4 + j, 1), lo:T].rearrange("p a n -> p (a n)"),
                                             ACT.Square).then_inc(s("ysq"), 1)
                    loop(a, n // 4, up if kind == "up" else down, lastpart)

            a.wait_ge(s("small_set"), 1)
            a.wait_ge(s("tables_loaded"), 16)
            a.activation(silc[:], vec[:, V_C:V_C + 2 * KT].rearrange("p (k c) -> p k c", c=2), ACT.Silu).then_inc(s("silc"), 1)
            a.wait_ge(s("x_loaded"), 16)
            squares(0, lambda k: X[:, k, :], 0)
            split(Blk(0, 0, 0))
            split(Blk(0, 0, 1))
            pre_norm(0, 0, 0)
            ffn(0, B_FFN1, segs_all, False)
            all_read(a, B_FFN1 + N_FFN)
            rstd(1, 0)
            pre_norm(2, 1, 0)

            def item_norm(n, width):
                a.activation(a_sq[:, 0:width], a_raw[:, 0:width], ACT.Square).then_inc(s("at_sq"), 1)
                a.wait_ge(s("at_ss"), n + 1)
                if width == T:
                    a.activation(a_rs[:, 0:CTX], ps[:, 4, 0:CTX], ACT.Ln, bias=eps, scale=1.0 / DH)
                    a.activation(a_rs[:, CTX:T], ps[:, 5, 0:SEQ], ACT.Ln, bias=eps, scale=1.0 / DH).then_inc(s("at_ln"), 1)
                else:
                    a.activation(a_rs[:, 0:SEQ], ps[:, 4, 0:SEQ], ACT.Ln, bias=eps, scale=1.0 / DH).then_inc(s("at_ln"), 1)
                a.wait_ge(s("at_ln"), n + 1)
                a.activation(a_rs[:, 0:width], a_rs[:, 0:width], ACT.Exp, scale=-0.5).then_inc(s("at_rs"), 1)

            for j in range(2):
                blk = Blk(B_KV, 0, j)
                step(blk)
                if j:
                    a.wait_ge(s("at_nrm"), j)
                read_out(blk, lambda l, h_: a_raw[:, l:h_], segs_all)
                a.wait_ge(psum_read[blk.pair], blk.turn + 2)
                item_norm(j, T)
            for j in range(2, 4):
                blk = Blk(B_KV, 0, j)
                step(blk)
                a.wait_ge(s("at_nrm"), 2)
                if j == 3:
                    a.wait_ge(s("at_vt"), 1)
                read_out(blk, lambda l, h_: a_raw[:, l:h_], segs_all)
                a.wait_ge(s("at_vt"), j - 1)
                a.activation(a_v[:, :, j - 2, :].rearrange("p (b c) n -> p b c n", b=2),
                             ps[:, 6:8, 0:384].rearrange("p b (c n) -> p b c n", c=3), ACT.Copy).then_inc(s("at_vc"), 1)
            blk = Blk(B_KV, 0, 4)
            step(blk)
            read_out(blk, lambda l, h_: ba[:, l:h_], segs_all)
            a.wait_ge(psum_read[blk.pair], blk.turn + 2)
            a.activation(bt[0:16, 0, :], ba[0:16, :], ACT.Exp, scale=-1.0).then_inc(s("ba_e"), 1)
            a.activation(small[32:48, 8:9], vec[32:48, V_ALOG:V_ALOG + 1], ACT.Exp).then_inc(s("ba_e"), 1)
            a.wait_ge(s("ba_abs"), 2)
            a.activation(bt[32:48, 0, :], bt[32:48, 0, :], ACT.Exp, scale=-1.0).then_inc(s("ba_e"), 1)
            a.wait_ge(s("ba_e"), 3)
            a.activation(bt[32:48, 0, :], bt[32:48, 0, :], ACT.Ln, bias=one[32:48]).then_inc(s("ba_e"), 1)
            a.wait_ge(s("ba_gc"), 1)
            a.activation(bgt[:, 1, :], bgt[:, 0, :], ACT.Exp).then_inc(s("ba_x"), 1)
            a.wait_ge(s("ba_gt"), 1)
            for d in range(2):
                a.activation(gall[:, :, G_DCY + 6 * d:G_DCY + 6 * d + 6],
                             ps[:, 6, 96:192].rearrange("p (c e h) -> p e h c", c=NCH, e=2)[:, d], ACT.Exp)\
                 .then_inc(s("ba_x"), 1)
            a.activation(bgt[:, 2, :], bgt[:, 2, :], ACT.Exp).then_inc(s("ba_x"), 1)

            a.wait_ge(s("x_spilled"), 16)

            def q_rstd(n, sl):
                a.wait_ge(s("at_ss"), n + 3)
                a.activation(q_rs[sl], ps[:, 4 + sl, 0:SEQ], ACT.Ln, bias=eps, scale=1.0 / DH).then_inc(s("at_ln"), 1)
                a.wait_ge(s("at_ln"), n + 3)
                a.activation(q_rs[sl], q_rs[sl], ACT.Exp, scale=-0.5).then_inc(s("at_rs"), 1)

            def queries(it):
                for j in range(4):
                    n = it * 4 + j
                    blk = Blk(B_Q, it, j)
                    step(blk)
                    a.wait_ge(s("at_nrm"), n + 1)
                    a.activation(q_raw[j % 2], bank(blk, 1), ACT.Copy).then_inc(psum_read[blk.pair], 1)
                    a.wait_ge(psum_read[blk.pair], blk.turn + 2)
                    a.activation(q_sq[j % 2], q_raw[j % 2], ACT.Square).then_inc(s("at_sq"), 1)
                    if j:
                        q_rstd(it * 4 + (j - 1), (j - 1) % 2)
                q_rstd(it * 4 + 3, 1)
            loop(a, 2, queries)

            a.wait_ge(s("gall"), 1)
            a.wait_ge(s("at_rot"), H + 2)

            def heads(it):
                a.wait_ge(s("o_at"), it * 4 + 1)
                a.activation(a_vc[:], a_v[:, :, bass.ds(it, 1), :].rearrange("p c a n -> p (c a) n"),
                             ACT.Copy).then_inc(s("at_vcur"), 1)

                def evac_pt(i):
                    a.wait_ge(s("at_tr"), it * 16 + (i + 1))
                    t = i % 4
                    a.activation(a_pt[i // 4 % 2][:, :, P * t:P * t + P].rearrange("p (b c) n -> p b c n", b=2),
                                 ps[:, 0:2, 0:384].rearrange("p b (c n) -> p b c n", c=3), ACT.Copy)\
                     .then_inc(s("at_pt"), 1)

                def out_head(j):
                    n = it * 4 + j
                    a.wait_ge(s("at_pv"), n + 1)
                    a.activation(o_at[:, bass.ds(n, 1), :].rearrange("p a n -> p (a n)"), ps[:, 2 + j % 2, 0:SEQ], ACT.Copy)\
                     .then_inc(s("o_at"), 1)
                for i in range(16):
                    t = i % 4
                    a.wait_ge(s("at_max"), it * 16 + (i + 1))
                    a.activation(a_p[:, i % 2, :].rearrange("p (b n) -> p b n", b=2),
                                 ps[:, 4 + 2 * (i % 2):6 + 2 * (i % 2), 0:384],
                                 ACT.Exp, bias=a_m[:, 1, t:t + 1], scale=DH ** -0.5,
                                 accum_out=a_m[:, 2, t:t + 1]).then_inc(s("at_p"), 1)
                    if i:
                        evac_pt(i - 1)
                    if i >= 4 and t == 2:
                        out_head(i // 4 - 1)
                evac_pt(15)
                out_head(3)
            loop(a, 2, heads)

            def take(b):
                a.wait_ge(s("gemm_done"), b.n + 1)
                if b.j:
                    a.wait_ge(s("conv"), b.it * 3 + b.j)
                    a.activation(d_up[:, 1:CTX + 1], bank(b, 0), ACT.Copy)
                a.activation(d_up[:, CTX + 3:T + 3], bank(b, 1), ACT.Copy).then_inc(psum_read[b.pair], 1)
                split(b.ahead(2))

            def dn_head(h, final):
                b = [Blk(B_DN, h, j) for j in range(4)]
                take(b[0])
                for d in range(2):
                    a.wait_ge(s("d_mn"), h * 4 + 2 * d + 1)
                    a.activation(d_t[:, d], d_t[:, d], ACT.Exp).then_inc(s("d_e1"), 1)
                    a.wait_ge(s("d_mn"), h * 4 + 2 * d + 2)
                    a.activation(d_r[:, d, 0:NC_X], d_r[:, d, 0:NC_X], ACT.Exp, scale=-1.0).then_inc(s("d_e2"), 1)
                    a.activation(d_qd[:, d, 0], ps[:, 4 + 2 * d, 2 * P:3 * P], ACT.Exp)
                    a.activation(d_qd[:, d, 1:NC_X].rearrange("p c n -> p (c n)"), ps[:, 5 + 2 * d, 0:384], ACT.Exp)\
                     .then_inc(s("d_qe"), 1)
                take(b[1])
                a.activation(d_c[:, 0, CTX + 2:], d_c[:, 0, CTX + 2:], ACT.Silu).then_inc(s("d_silu"), 1)
                a.wait_ge(s("d_silu"), h * 3 + 1)
                a.activation(d_sq[:, 0:SEQ], d_c[:, 0, CTX + 2:], ACT.Square)
                a.wait_ge(s("conv"), h * 3 + 2)
                a.activation(d_c[:, 1, :], d_c[:, 1, :], ACT.Silu).then_inc(s("d_silu"), 1)
                a.wait_ge(s("d_silu"), h * 3 + 2)
                a.activation(d_sq[:, SEQ:SEQ + CTX], d_c[:, 1, 0:CTX], ACT.Square)
                a.activation(d_sq[:, SEQ + CTX:], d_c[:, 1, CTX + 2:], ACT.Square).then_inc(s("d_sq"), 1)
                take(b[2])
                a.wait_ge(s("d_ss"), h + 1)
                a.activation(d_rs[:, 0:SEQ], ps[:, 4, :], ACT.Ln, bias=eps_q, scale=float(DH))
                a.activation(d_rs[:, SEQ:SEQ + CTX], ps[:, 5, 0:CTX], ACT.Ln, bias=eps)
                a.activation(d_rs[:, SEQ + CTX:], ps[:, 6, :], ACT.Ln, bias=eps).then_inc(s("d_ln"), 1)
                a.wait_ge(s("d_ln"), h * 2 + 1)
                a.activation(d_rs[:], d_rs[:], ACT.Exp, scale=-0.5).then_inc(s("d_rstd"), 1)
                a.wait_ge(s("conv"), h * 3 + 3)
                a.activation(d_c[:, 2, :], d_c[:, 2, :], ACT.Silu).then_inc(s("d_silu"), 1)
                a.wait_ge(s("gemm_done"), b[3].n + 1)
                a.wait_ge(s("head_done"), h + 1)
                a.activation(d_z[:], bank(b[3], 1), ACT.Silu).then_inc(psum_read[b[3].pair], 1)
                for i, dst in enumerate((d_ktok, d_vtok)):
                    a.wait_ge(s("d_tok"), h * 2 + (i + 1))
                    a.activation(dst[:].rearrange("p (b c) n -> p b (c n)", b=2), ps[:, 2 - 2 * i:4 - 2 * i, 0:384], ACT.Copy)\
                     .then_inc(s("d_tokc"), 1)
                    if i == 0:
                        split(b[3].ahead(2))
                for lv in range(1, LEVELS):
                    for gr in range(4):
                        d, hf = gr // 2, gr % 2
                        a.wait_ge(s("sv_q"), h * 28 + 4 * lv + gr + 1)
                        a.activation(d_q[:, d, 3 * hf:3 * hf + 3].rearrange("p c n -> p (c n)"), ps[:, 4 + gr, 0:384],
                                     ACT.Copy).then_inc(s("sv_qc"), 1)
                for gr in range(4):
                    d, hf = gr // 2, gr % 2
                    a.wait_ge(s("uw"), h * 4 + gr + 1)
                    a.activation(d_q[:, d, 3 * hf:3 * hf + 3].rearrange("p c n -> p (c n)"), ps[:, 4 + gr, 0:384],
                                 ACT.Copy).then_inc(s("u_c"), 1)
                a.wait_ge(s("sc_o"), h * 8 + 8)
                a.activation(d_o[:], ps[:, 0, :], ACT.Copy).then_inc(s("od_copy"), 1)
                a.wait_ge(s("od_sum"), h + 1)
                a.activation(d_sq[:, 0:SEQ], d_o[:], ACT.Square).then_inc(s("od_sq"), 1)
                a.wait_ge(s("od_ss"), h + 1)
                a.activation(d_rs[:, 0:SEQ], ps[:, 2, :], ACT.Ln, bias=eps, scale=1.0 / DH).then_inc(s("d_ln"), 1)
                a.wait_ge(s("d_ln"), h * 2 + 2)
                a.activation(d_rs[:, 0:SEQ], d_rs[:, 0:SEQ], ACT.Exp, scale=-0.5).then_inc(s("od_rstd"), 1)
            a.wait_ge(s("d_up0"), 1)
            with a.Fori(0, H - 1, 1) as h:
                dn_head(h, False)
            dn_head(H - 1, True)

            a.wait_ge(s("head_done"), H + 1)
            for src, dst in ((o_dn, odn_hi), (o_at, oat_hi)):
                for k in range(H):
                    a.activation(dst[:, k], src[:, k], ACT.Copy).then_inc(s("o_rounded"), 1)

            def merge(it):
                for j in range(4):
                    blk = Blk(B_MERGE, it, j)
                    step(blk)
                    dst = (m_a[:], m_s[:, 0, :], m_b[:], m_s[:, 1, :])[j]
                    if j < 2:
                        a.wait_ge(s("merged"), it + 1)
                    if j == 2:
                        a.wait_ge(s("gated"), it * 2 + 1)
                    read_out(blk, lambda l, h_: dst, segs_x, ACT.Sigmoid if j % 2 else ACT.Copy)
                a.wait_ge(s("merged"), it + 2)
                a.activation(m_hi[:, bass.ds(it, 1), :].rearrange("p a n -> p (a n)"), m_b[:], ACT.Copy).then_inc(s("m_rounded"), 1)
            loop(a, KT, merge)

            def out_proj(it):
                for j in range(4):
                    blk = Blk(B_OUT, it, j)
                    step(blk)
                    a.wait_ge(s("ysq_used"), it * 4 + (9 + j + 1))
                    a.activation((m_a, m_b)[j % 2][:], bank(blk, 1), ACT.Square).then_inc(s("ysq"), 1)
                    read_out(blk, lambda l, h_: Y[:, bass.ds(it * 4 + j, 1), l:h_].rearrange("p a n -> p (a n)"), segs_x)
            a.wait_ge(s("gemm_done"), B_OUT)
            loop(a, KT // 4, out_proj)
            all_read(a, B_OUT + KT)
            rstd(3, CTX)
            pre_norm(4, 2, CTX)
            ffn(1, B_FFN2, segs_x, True)
            all_read(a, NBLK)
            rstd(5, CTX)

        @block.vector
        def _(v):
            def split(b):
                v.wait_ge(s("w_hi"), b.n + 1)
                v.tensor_tensor(w_lo[:, b.pair], raw[:, b.raw], w_hi[:, b.pair].bitcast(F32), ALU.subtract)\
                 .then_inc(s("w_split"), 1)

            def step(b):
                if not (isinstance(b.n, int) and b.n + 2 >= NBLK):
                    split(b.ahead(2))

            def mod_part(done, load, slot):
                v.wait_ge(wmod_loaded[slot], (load + 1) * 16)
                v.wait_ge(s("mod_fold"), done + 1)
                for k in range(KT):
                    for c in range(2):
                        acc = m_part[:, slot, c, :]
                        if k == 0:
                            x = v.tensor_scalar(acc, w_mod[:, slot, k, :], silc[:, k, c:c + 1], None, ALU.mult)
                        else:
                            v.wait_ge(s("mod_acc"), done * 14 + (2 * k + c - 1))
                            x = v.scalar_tensor_tensor(acc, w_mod[:, slot, k, :], silc[:, k, c:c + 1], acc, ALU.mult, ALU.add)
                        if k < KT - 1:
                            x.then_inc(s("mod_acc"), 1)
                x.then_inc(s("mod_part"), 1)

            def mod_sums(u0, u1, bank_):
                bias = vec[:, V_BMOD + u0:V_BMOD + u1].unsqueeze(2).to_broadcast([P, u1 - u0, 2])
                v.tensor_tensor(mod[:, u0:u1, :], ps[:, bank_, 2 * u0:2 * u1].rearrange("p (u c) -> p u c", c=2), bias, ALU.add)\
                 .then_inc(s("mod_out"), 1)

            def derive(i, mi, vcol, add, mul):
                gain = vec[:, vcol:vcol + KT].unsqueeze(2).to_broadcast([P, KT, 2])
                return v.scalar_tensor_tensor(drv[:, i], mod[:, 8 * mi:8 * mi + 8, :], add if add else mul, gain,
                                              ALU.add if add else ALU.mult, ALU.mult)

            def sum_squares(r, lo):
                r = SQ[r]
                for k in range(KT):
                    v.wait_ge(s("sq_ready"), KT * r + k + 1)
                    if k == 0:
                        if r:
                            v.wait_ge(s("sq_used"), KT * r)
                        v.tensor_copy(n_acc[:, lo:T], n_sq[:, 0, lo:T]).then_inc(s("sq_used"), 1)
                    else:
                        v.wait_ge(s("sq_used"), KT * r + k)
                        v.tensor_tensor(n_acc[:, lo:T], n_acc[:, lo:T], n_sq[:, k % 2, lo:T], ALU.add).then_inc(s("sq_used"), 1)

            def pre_norm(r, p, lo):
                v.wait_ge(s("rstd"), r + 1)
                def low(k):
                    v.wait_ge(s("h_rounded"), KT * p + k + 1)
                    v.tensor_tensor(h_lo[:, k, lo:T], n_t2[:, k % 2, lo:T], h_hi[:, k, lo:T].bitcast(F32), ALU.subtract)\
                     .then_inc(s("h_ready"), 1)
                for k in range(KT):
                    if k >= 2:
                        v.wait_ge(s("h_full"), KT * p + k - 1)
                    v.tensor_tensor(n_t[:, k % 2, lo:T], X[:, k, lo:T], n_rs[:, lo:T], ALU.mult).then_inc(s("nrm_ready"), 1)
                    if k:
                        low(k - 1)
                low(KT - 1)

            def post_norm(r, p, lo):
                v.wait_ge(s("rstd"), r + 1)
                v.wait_ge(s("h_ready"), KT * (p + 1))
                for k in range(KT):
                    if k >= 2:
                        v.wait_ge(s("x_new"), KT * p + k - 1)
                    v.tensor_tensor(n_t[:, k % 2, lo:T], Y[:, k, lo:T], n_rs[:, lo:T], ALU.mult).then_inc(s("yn"), 1)
                    v.wait_ge(s("yn"), KT * p + k + 1)
                    for l, h_, sg_ in (segs_all if lo == 0 else segs_x):
                        last = v.scalar_tensor_tensor(X[:, k, l:h_], n_t[:, k % 2, l:h_], drv[:, 2 * p + 1, k, sg_:sg_ + 1],
                                                      X[:, k, l:h_], ALU.mult, ALU.add)
                    last.then_inc(s("x_new"), 1)
                v.wait_ge(s("x_new"), KT * (p + 1))

            def ffn(i, b0, seg_list, peel_last, mod_from=None):
                lo = seg_list[0][0]
                u0 = mod_from
                pairs = i * HID
                ys = 2 * KT * i
                for kind, b, n, c, hid in ffn_parts(b0):
                    lastpart = peel_last and kind == "down" and c == 2

                    def up(it, b=b, hid=hid, u0=u0):
                        for j in range(4):
                            blk = Blk(b, it, j)
                            if j % 2 == 0:
                                step(blk)
                            else:
                                v.wait_ge(s("gemm_done"), blk.n + 1)
                                v.wait_ge(psum_read[1 - blk.pair], blk.ahead(-1).turn + 2)
                                v.wait_ge(s("g_ready"), it * 2 + (pairs + hid + j // 2 + 1))
                                for l, h_, sg_ in seg_list:
                                    last = v.tensor_tensor(gt[:, l:h_], sg[:, l:h_], bank(blk, sg_), ALU.mult)
                                last.then_inc(psum_read[blk.pair], 1)
                                step(blk)
                                p_ = it * 2 + j // 2
                                v.wait_ge(s("g_rounded"), it * 2 + (pairs + hid + j // 2 + 1))
                                v.tensor_tensor(g_lo[:, bass.ds(p_, 1), lo:T].rearrange("p a n -> p (a n)"), gt[:, lo:T],
                                                g_hi[:, bass.ds(p_, 1), lo:T].rearrange("p a n -> p (a n)").bitcast(F32),
                                                ALU.subtract).then_inc(s("g_ready"), 1)
                            if u0 is not None:
                                mod_part(it * 4 + (u0 + j), it * 2 + (u0 // 2 + j // 2), j % 2)

                    def down(it, b=b, c=c, u0=u0):
                        for j in range(4):
                            blk = Blk(b, it, j)
                            step(blk)
                            if c:
                                v.wait_ge(s("gemm_done"), blk.n + 1)
                                yk = Y[:, bass.ds(it * 4 + j, 1), :].rearrange("p a n -> p (a n)")
                                for l, h_, sg_ in seg_list:
                                    last = v.tensor_tensor(yk[:, l:h_], yk[:, l:h_], bank(blk, sg_), ALU.add)
                                last.then_inc(psum_read[blk.pair], 1)
                            if u0 is not None and j == 1:
                                mod_part(it * 2 + (u0 + j // 2), it + u0 // 2, j // 2)
                            if c == len(FCH) - 1:
                                v.wait_ge(s("ysq"), it * 4 + (2 * KT * i + j + 1))
                                v.wait_ge(s("ysq_used"), it * 4 + (18 * i + j + 2))
                                v.tensor_tensor(y_acc[:, lo:T], y_acc[:, lo:T], (sg, gt)[j % 2][:, lo:T], ALU.add)\
                                 .then_inc(s("ysq_used"), 1)
                            if u0 is not None and j == 3:
                                mod_part(it * 2 + (u0 + j // 2), it + u0 // 2, j // 2)
                    if kind == "down" and c == len(FCH) - 1:
                        v.memset(y_acc[:], 0.0).then_inc(s("ysq_used"), 1)
                    if kind == "down" and c:
                        all_read(v, b - 2 * FCH[c])
                    loop(v, n // 4, up if kind == "up" else down, lastpart)
                    if u0 is not None:
                        u0 += n if kind == "up" else n // 2
                all_read(v, b0 + N_FFN)

            zero, one, eps, eps_q = (small[:, i:i + 1] for i in range(4))
            v.memset(zero, 0.0)
            v.memset(one, 1.0)
            v.memset(eps, EPS)
            v.memset(eps_q, EPS * DH).then_inc(s("small_set"), 1)
            v.memset(m_part[:, 1], 0.0).then_inc(s("mod_part"), 1)
            sum_squares(0, 0)
            v.wait_ge(s("silc"), 1)
            for i, u in enumerate(DVE_MOD0):
                v.wait_ge(s(f"mod0_loaded{u // 4}"), 16)
                for k in range(KT):
                    for c in range(2):
                        acc, w = m0_part[:, i, c, :], w_mod0[u // 4][:, u % 4, P * k:P * k + P]
                        if k == 0:
                            x = v.tensor_scalar(acc, w, silc[:, k, c:c + 1], None, ALU.mult)
                        else:
                            v.wait_ge(s("mod0_acc"), 14 * i + 2 * k + c - 1)
                            x = v.scalar_tensor_tensor(acc, w, silc[:, k, c:c + 1], acc, ALU.mult, ALU.add)
                        if k < KT - 1:
                            x.then_inc(s("mod0_acc"), 1)
                x.then_inc(s("mod0_part"), 1)
            v.wait_ge(s("tables_loaded"), 16)
            v.wait_ge(s("mod_mm"), N_MOD0)
            mod_sums(0, N_MOD0, 7)
            v.wait_ge(s("mod_out"), 1)
            derive(0, 1, V_PRE1, 1.0, None).then_inc(s("drv"), 1)
            split(Blk(0, 0, 0))
            split(Blk(0, 0, 1))
            v.wait_ge(s("drv"), 1)
            pre_norm(0, 0, 0)
            ffn(0, B_FFN1, segs_all, False, 0)
            v.wait_ge(s("mod_fold"), N_MOD - N_MOD0 + 2)
            mod_sums(N_MOD0, N_MOD, 6)
            v.wait_ge(s("mod_out"), 2)
            derive(1, 2, V_POST1, None, 0.5)
            derive(2, 4, V_PREM, 1.0, None)
            derive(3, 5, V_POSTM, None, 1.0)
            derive(4, 7, V_PRE2, 1.0, None)
            derive(5, 8, V_POST2, None, 0.5).then_inc(s("drv"), 1)
            v.wait_ge(s("drv"), 2)
            post_norm(1, 0, 0)
            pre_norm(2, 1, 0)

            def item(n, width, gain, dst_x, dst_c=None, bufs=(a_raw, a_rs, a_n), bk=6):
                v.wait_ge(s("at_rs"), n + 1)
                if dst_c is not None:
                    v.scalar_tensor_tensor(dst_c, bufs[0][:, 0:CTX], gain, bufs[1][:, 0:CTX], ALU.mult, ALU.mult)
                o = width - SEQ
                v.scalar_tensor_tensor(bufs[2][:, 0:SEQ], bufs[0][:, o:width], gain, bufs[1][:, o:width], ALU.mult, ALU.mult)\
                 .then_inc(s("at_nrm"), 1)
                v.wait_ge(s("at_nrm"), n + 1)
                if not (isinstance(n, int) and n == 0):
                    v.wait_ge(s("at_rot"), n)
                v.tensor_tensor(a_t1[:], bufs[2][:, 0:SEQ], rope_c, ALU.mult)
                v.wait_ge(s("at_swap"), n + 1)
                v.tensor_tensor(a_t2[:], ps[:, bk, :], rope_s, ALU.mult).then_inc(s("at_t2"), 1)
                v.wait_ge(s("at_t2"), n + 1)
                v.tensor_tensor(dst_x, a_t1[:], a_t2[:], ALU.add).then_inc(s("at_rot"), 1)

            v.wait_ge(s("cb_loaded"), 16)
            for j in range(2):
                step(Blk(B_KV, 0, j))
                item(j, T, vec[:, V_KN:V_KN + 1], a_kt[:, j, CTX:T], a_kt[:, j, 0:CTX])
            for j in range(2, 5):
                step(Blk(B_KV, 0, j))
            v.memset(bx[:], 0.0).then_inc(s("ba_bx"), 1)
            blk = Blk(B_KV, 0, 4)
            v.wait_ge(psum_read[blk.pair], blk.turn + 2)
            v.wait_ge(s("ba_bx"), 1)
            v.tensor_scalar(ba[32:48, :], ba[32:48, :], vec[32:48, V_DT:V_DT + 1], None, ALU.add).then_inc(s("ba_abs"), 1)
            v.wait_ge(s("ba_abs"), 1)
            v.scalar_tensor_tensor(bt[32:48, 0, :], ba[32:48, :], -1.0, ba[32:48, :], ALU.mult, ALU.max).then_inc(s("ba_abs"), 1)
            v.wait_ge(s("ba_e"), 1)
            v.tensor_scalar(bt[0:16, 1, :], bt[0:16, 0, :], 1.0, None, ALU.add).then_inc(s("ba_v"), 1)
            v.wait_ge(s("ba_v"), 1)
            v.reciprocal(bx[0:16, :], bt[0:16, 1, :])
            v.wait_ge(s("ba_e"), 4)
            v.scalar_tensor_tensor(bt[32:48, 1, :], ba[32:48, :], 0.0, bt[32:48, 0, :], ALU.max, ALU.add).then_inc(s("ba_v"), 1)
            v.wait_ge(s("ba_v"), 2)
            v.tensor_scalar(bx[32:48, :], bt[32:48, 1, :], small[32:48, 8:9], -1.0, ALU.mult, ALU.mult).then_inc(s("ba_bx"), 1)
            v.wait_ge(s("ba_tr"), 1)
            v.tensor_copy(bg[:].rearrange("p (b c) n -> p b c n", b=2),
                          ps[:, 6:8, 0:384].rearrange("p b (c n) -> p b c n", c=3)[:, :, :, 0:48]).then_inc(s("ba_bg"), 1)
            v.wait_ge(s("ba_sum"), 1)
            v.tensor_copy(bgt[:, 0, :], ps[:, 6, 0:96]).then_inc(s("ba_gc"), 1)
            v.wait_ge(s("ba_gc"), 1)
            def hc_of(t, d):
                return t[:, 48 * d:48 * d + 48].rearrange("p (c h) -> p h c", c=NCH)
            for d in range(2):
                v.tensor_copy(gall[:, :, G_GC + 6 * d:G_GC + 6 * d + 6], hc_of(bgt[:, 0], d))
                last = v.tensor_copy(gall[:, :, G_BETA + 6 * d:G_BETA + 6 * d + 6],
                                     bg[:, :, 8 * d:8 * d + 8].rearrange("p c h -> p h c"))
            last.then_inc(s("ba_gc"), 1)
            for d in range(2):
                last = v.tensor_tensor(hc_of(bgt[:, 2], d),
                                       ps[:, 6, 96:192].rearrange("p (c e h) -> p e h c", c=NCH, e=2)[:, d],
                                       hc_of(bgt[:, 0], d), ALU.subtract)
            last.then_inc(s("ba_gt"), 1)
            v.wait_ge(s("ba_x"), 1)
            v.wait_ge(s("ba_gc"), 2)
            for d in range(2):
                last = v.tensor_tensor(gall[:, :, G_BEG + 6 * d:G_BEG + 6 * d + 6],
                                       gall[:, :, G_BETA + 6 * d:G_BETA + 6 * d + 6], hc_of(bgt[:, 1], d), ALU.mult)
            v.wait_ge(s("ba_x"), 4)
            for d in range(2):
                last = v.tensor_copy(gall[:, :, G_KD + 6 * d:G_KD + 6 * d + 6], hc_of(bgt[:, 2], d))
            last.then_inc(s("gall"), 1)

            v.wait_ge(s("x_spilled"), 16)

            def queries(it):
                def query(j):
                    n = it * 4 + j
                    item(n + 2, SEQ, vec[:, V_QN:V_QN + 1], o_at[:, bass.ds(n, 1), :].rearrange("p a n -> p (a n)"),
                         bufs=(q_raw[j % 2], q_rs[j % 2], q_n[j % 2]), bk=6 + j % 2)
                for j in range(4):
                    step(Blk(B_Q, it, j))
                    if j:
                        query(j - 1)
                query(3)
            loop(v, 2, queries)

            def heads(it):
                def normalise(i):
                    t = i % 4
                    v.wait_ge(s("at_p"), it * 16 + (i + 1))
                    v.reciprocal(a_m[:, 2, t:t + 1], a_m[:, 2, t:t + 1]).then_inc(s("at_rc"), 1)
                    v.wait_ge(s("at_rc"), it * 16 + (i + 1))
                    v.tensor_scalar(a_p[:, i % 2, :], a_p[:, i % 2, :], a_m[:, 2, t:t + 1], None, ALU.mult)\
                     .then_inc(s("at_pn"), 1)
                for i in range(16):
                    t = i % 4
                    v.wait_ge(s("at_s"), it * 16 + (i + 1))
                    v.tensor_reduce(out=a_m[:, 0, t:t + 1], in_=ps[:, 4 + 2 * (i % 2):6 + 2 * (i % 2), 0:384],
                                    op=ALU.max, axis=AX.XY).then_inc(s("at_mx"), 1)
                    v.wait_ge(s("at_mx"), it * 16 + (i + 1))
                    v.tensor_scalar(a_m[:, 1, t:t + 1], a_m[:, 0, t:t + 1], -DH ** -0.5, None, ALU.mult)\
                     .then_inc(s("at_max"), 1)
                    if i:
                        normalise(i - 1)
                normalise(15)
            loop(v, 2, heads)

            def bc(x):
                return x.unsqueeze(2).to_broadcast([P, x.shape[1], P])

            v.wait_ge(s("gall"), 1)
            v.wait_ge(s("d_up0"), 1)

            def tables(h):
                v.tensor_copy(hc[:], gall[:, bass.ds(h, 1), :].rearrange("p a n -> p (a n)")).then_inc(s("hc"), 1)

            def dn_head(h, final):
                b = [Blk(B_DN, h, j) for j in range(4)]

                def conv(j):
                    v.wait_ge(psum_read[b[j].pair], b[j].turn + 2)
                    lo = CTX + 2 if j == 0 else 0
                    n = T + 2 - lo
                    c = d_c[:, j, lo:]
                    tap = [hc[:, 3 * j + i:3 * j + i + 1] for i in range(3)]
                    v.tensor_scalar(c, d_up[:, lo:lo + n], tap[0], None, ALU.mult).then_inc(s("tap"), 1)
                    v.wait_ge(s("tap"), h * 6 + 2 * j + 1)
                    v.scalar_tensor_tensor(c, d_up[:, lo + 1:lo + 1 + n], tap[1], c, ALU.mult, ALU.add).then_inc(s("tap"), 1)
                    v.wait_ge(s("tap"), h * 6 + 2 * j + 2)
                    v.scalar_tensor_tensor(c, d_up[:, lo + 2:lo + 2 + n], tap[2], c, ALU.mult, ALU.add).then_inc(s("conv"), 1)
                    step(b[j])
                v.wait_ge(s("hc"), h + 1)
                conv(0)
                for d in range(2):
                    v.wait_ge(s("d_row"), h * 2 + (d + 1))
                    v.tensor_tensor(d_q[:, d].rearrange("p (b c) n -> p b c n", b=2),
                                    hc[:, G_GC + 6 * d:G_GC + 6 * d + 6].rearrange("p (b c) -> p b c", b=2)
                                    .unsqueeze(3).to_broadcast([P, 2, 3, P]),
                                    ps[:, 4 + 2 * d:6 + 2 * d, 0:384].rearrange("p b (c n) -> p b c n", c=3), ALU.subtract)\
                     .then_inc(s("d_diff"), 1)
                    v.wait_ge(s("d_diff"), h * 2 + (d + 1))
                    v.tensor_scalar(d_t[:, d], d_q[:, d], 0.0, None, ALU.min).then_inc(s("d_mn"), 1)
                    v.tensor_scalar(d_r[:, d, 0:NC_X], d_q[:, d, NC_CTX:], 0.0, None, ALU.max).then_inc(s("d_mn"), 1)
                conv(1)
                conv(2)
                v.wait_ge(s("d_rstd"), h + 1)
                v.tensor_tensor(d_c[:, 1, 0:CTX], d_c[:, 1, 0:CTX], d_rs[:, SEQ:SEQ + CTX], ALU.mult)
                v.tensor_tensor(d_c[:, 1, CTX + 2:], d_c[:, 1, CTX + 2:], d_rs[:, SEQ + CTX:], ALU.mult).then_inc(s("d_qk"), 1)
                v.tensor_tensor(d_c[:, 0, CTX + 2:], d_c[:, 0, CTX + 2:], d_rs[:, 0:SEQ], ALU.mult).then_inc(s("d_qk"), 1)
                v.wait_ge(s("d_e1"), h * 2 + 1)
                v.tensor_tensor(d_t[:, 0], d_t[:, 0], bc(hc[:, G_BETA:G_BETA + 6]), ALU.mult).then_inc(s("d_eb0"), 1)

                def level(lv):
                    v.tensor_tensor(d_s[lv % 2][:, 0], d_l[:, 0], masks[:, 0, lv, :].unsqueeze(1).to_broadcast([P, NCH, P]),
                                    ALU.mult).then_inc(s("lvl0"), 1)
                for d in (1, 0):
                    v.wait_ge(s(f"d_eb{d}"), h + 1)
                    v.wait_ge(s("d_kk"), h + 1)
                    v.tensor_tensor(d_l[:, d].rearrange("p (b c) n -> p b (c n)", b=2),
                                    d_t[:, d].rearrange("p (b c) n -> p b (c n)", b=2), ps[:, 4:6, 0:384], ALU.mult)\
                     .then_inc(s("d_l"), 1)
                v.wait_ge(s("d_l"), h * 2 + 2)
                level(0)
                v.wait_ge(s("d_kq"), h + 1)
                for d in range(2):
                    v.wait_ge(s("d_e2"), h * 2 + (d + 1))
                    v.tensor_tensor(d_at[:, d].rearrange("p c n -> p (c n)"), d_r[:, d, 0:NC_X].rearrange("p c n -> p (c n)"),
                                    ps[:, 6, :], ALU.mult).then_inc(s("d_am"), 1)
                level(1)
                v.wait_ge(s("d_am"), h * 2 + 2)
                for gr in range(4):
                    d, hf = gr // 2, gr % 2
                    v.wait_ge(s("sv_q"), h * 28 + gr + 1)
                    v.tensor_tensor(d_r[:, d, 3 * hf:3 * hf + 3], ident.unsqueeze(1).to_broadcast([P, 3, P]),
                                    ps[:, 4 + gr, 0:384].rearrange("p (c n) -> p c n", c=3), ALU.subtract)\
                     .then_inc(s("sv_r"), 1)
                for d in range(2):
                    v.wait_ge(s(f"lvl{d}"), h * 7 + 1)
                    last = v.tensor_tensor(d_t[:, d], ident.unsqueeze(1).to_broadcast([P, NCH, P]), d_s[0][:, d], ALU.subtract)
                last.then_inc(s("t_set"), 1)
                v.wait_ge(s("t_set"), h + 1)
                level(2)
                step(b[3])
                for lv in range(1, LEVELS):
                    for gr in range(4):
                        d, hf = gr // 2, gr % 2
                        v.wait_ge(s("sv_d"), h * 24 + 4 * (lv - 1) + gr + 1)
                        r_ = half(d_r[:, d, 3 * hf:3 * hf + 3], lv, 1 - d)
                        t_ = half(d_t[:, d, 3 * hf:3 * hf + 3], lv, d)
                        if lv < LEVELS - 1:
                            v.tensor_tensor(t_, t_, halves(ps[:, gr, 0:192], lv), ALU.subtract)
                        v.tensor_tensor(r_, r_, halves(ps[:, 4 + gr, 0:192], lv), ALU.subtract).then_inc(s("sv_r"), 1)
                    if lv + 2 < LEVELS:
                        level(lv + 2)
                    elif lv == LEVELS - 2:
                        v.wait_ge(s("d_tokc"), h * 2 + 2)
                        v.tensor_tensor(d_s[1][:, 0], d_ktok[:], bc(hc[:, G_BEG:G_BEG + 6]), ALU.mult).then_inc(s("d_kb0"), 1)
                for gr in range(4):
                    d, hf = gr // 2, gr % 2
                    v.wait_ge(s("uw"), h * 4 + gr + 1)
                    v.tensor_copy(d_t[:, d, 3 * hf:3 * hf + 3].rearrange("p c n -> p (c n)"), ps[:, gr, 0:384])\
                     .then_inc(s("w_c"), 1)
                v.wait_ge(s("u_c"), h * 4 + 4)
                for t in range(NCH):
                    for d in range(2):
                        c = ORDER[d][t]
                        if t:
                            v.wait_ge(s("sc_w"), h * 10 + 2 * (t - 1) + d + 1)
                            v.tensor_tensor(d_vn[:, d], d_q[:, d, c], ps[:, 4 + d, 0:P], ALU.subtract).then_inc(s("sc_v"), 1)
                    if t < NCH - 1:
                        for d in range(2):
                            c = ORDER[d][t]
                            v.wait_ge(s("sc_s"), h * 10 + 2 * t + d + 1)
                            if t == 0:
                                v.tensor_copy(d_st[:, d], ps[:, 6 + d, 0:P]).then_inc(s("sc_st"), 1)
                            else:
                                v.scalar_tensor_tensor(d_st[:, d], d_st[:, d], hc[:, G_DCY + 6 * d + c:G_DCY + 6 * d + c + 1],
                                                       ps[:, 6 + d, 0:P], ALU.mult, ALU.add).then_inc(s("sc_st"), 1)
                if not final:
                    v.wait_ge(s("sc_st"), h * 10 + 10)
                    tables(h + 1)
                v.wait_ge(s("od_copy"), h + 1)
                v.tensor_tensor(d_o[:], d_o[:], ps[:, 1, :], ALU.add).then_inc(s("od_sum"), 1)
                v.wait_ge(s("od_rstd"), h + 1)
                v.scalar_tensor_tensor(d_o[:], d_o[:], vec[:, V_DN:V_DN + 1], d_rs[:, 0:SEQ], ALU.mult, ALU.mult)\
                 .then_inc(s("od_v"), 1)
                v.wait_ge(s("od_v"), h + 1)
                v.tensor_tensor(o_dn[:, bass.ds(h, 1), :].rearrange("p a n -> p (a n)"), d_o[:], d_z[:], ALU.mult)\
                 .then_inc(s("head_done"), 1)
            tables(0)
            with v.Fori(0, H - 1, 1) as h:
                dn_head(h, False)
            dn_head(H - 1, True)

            for i, (src, hi, lo) in enumerate(((o_dn, odn_hi, odn_lo), (o_at, oat_hi, oat_lo))):
                for k in range(H):
                    v.wait_ge(s("o_rounded"), i * H + k + 1)
                    v.tensor_tensor(lo[:, k], src[:, k], hi[:, k].bitcast(F32), ALU.subtract).then_inc(s("o_split"), 1)
            v.wait_ge(s("o_split"), 2 * H)
            v.sem_inc(s("merged"), 1)

            def merge(it):
                for j in range(4):
                    blk = Blk(B_MERGE, it, j)
                    step(blk)
                    if j % 2:
                        v.wait_ge(psum_read[blk.pair], blk.turn + 2)
                        v.wait_ge(psum_read[1 - blk.pair], blk.ahead(-1).turn + 2)
                        m = (m_a, m_b)[j // 2]
                        v.tensor_tensor(m[:], m[:], m_s[:, j // 2, :], ALU.mult).then_inc(s("gated"), 1)
                v.wait_ge(s("gated"), it * 2 + 2)
                v.tensor_tensor(m_b[:], m_a[:], m_b[:], ALU.add).then_inc(s("merged"), 1)
                v.wait_ge(s("m_rounded"), it + 1)
                v.tensor_tensor(m_lo[:, bass.ds(it, 1), :].rearrange("p a n -> p (a n)"), m_b[:],
                                m_hi[:, bass.ds(it, 1), :].rearrange("p a n -> p (a n)").bitcast(F32), ALU.subtract)\
                 .then_inc(s("m_ready"), 1)
            loop(v, KT, merge)

            def out_proj(it):
                for j in range(4):
                    step(Blk(B_OUT, it, j))
                    v.wait_ge(s("ysq"), it * 4 + (KT + j + 1))
                    v.wait_ge(s("ysq_used"), it * 4 + (9 + j + 2))
                    v.tensor_tensor(y_acc[:, CTX:T], y_acc[:, CTX:T], (m_a, m_b)[j % 2][:], ALU.add).then_inc(s("ysq_used"), 1)
            v.memset(y_acc[:], 0.0).then_inc(s("ysq_used"), 1)
            loop(v, KT // 4, out_proj)
            v.wait_ge(s("x_back"), 16)
            post_norm(3, 1, CTX)
            pre_norm(4, 2, CTX)
            ffn(1, B_FFN2, segs_x, True)
            post_norm(5, 2, CTX)

        @block.tensor
        def _(pe):
            def mm(out, lhsT, rhs, start=True, stop=True):
                return pe.matmul(out, lhsT, rhs, start=start, stop=stop)

            def gemm(b, hi, lo, seg_list, kt=KT, off=0, ready=None):
                pe.wait_ge(s("w_split"), b.n + 1)
                pe.wait_ge(psum_read[b.pair], b.turn + 1)
                for k in range(kt):
                    if ready is not None:
                        pe.wait_ge(ready[0], ready[1] + k + 1)
                    for i, (w, x) in enumerate(((w_hi, hi), (w_hi, lo), (w_lo, hi))):
                        for l, h_, sg_ in seg_list:
                            last = mm(bank(b, sg_), w[:, b.pair, k, :], x[:, k, l - off:h_ - off],
                                      k == 0 and i == 0, k == kt - 1 and i == 2)
                last.then_inc(s("gemm_done"), 1)

            def mod_fold(done, slot):
                pe.wait_ge(s("mod_part"), done + 1)
                for c in range(2):
                    col = 2 * (N_MOD0 - 1) + c
                    at_ = slice(2 * done + col, 2 * done + col + 1) if isinstance(done, int) else bass.ds(done * 2 + col, 1)
                    last = mm(ps[:, 6, at_], m_part[:, slot, c, :], ones[:, 0:1])
                last.then_inc(s("mod_fold"), 1)

            def sum_squares(r, lo):
                r = SQ[r]
                for k in range(KT):
                    pe.wait_ge(s("sq_ready"), KT * r + k + 1)
                    for l, h_, sg_ in (segs_all if lo == 0 else segs_x):
                        last = mm(ps[:, 4 + sg_, 0:h_ - l], ones, n_sq[:, k % 2, l:h_], k == 0, k == KT - 1)
                    last.then_inc(s("sq_used"), 1)

            def sum_partitions(r, lo):
                if r in SQ:
                    acc = n_acc
                    pe.wait_ge(s("sq_used"), KT * (SQ[r] + 1))
                else:
                    acc = y_acc
                    pe.wait_ge(s("ysq_used"), 9 * (r + 1) // 2 + 1)
                for l, h_, sg_ in (segs_all if lo == 0 else segs_x):
                    last = mm(ps[:, 4 + sg_, 0:h_ - l], ones, acc[:, l:h_])
                last.then_inc(s("ss_ready"), 1)

            def ffn(i, b0, seg_list, mod_from=None):
                u0 = mod_from
                pairs = i * HID
                for kind, b, n, c, hid in ffn_parts(b0):
                    if kind == "up":
                        def body(it, b=b, u0=u0, c=c):
                            for j in range(4):
                                gemm(Blk(b, it, j), h_hi, h_lo, seg_list, ready=(s("h_ready"), 2 * KT * i) if j == 0 and c == 0 else None)
                                if u0 is not None:
                                    mod_fold(it * 4 + (u0 + j), 1 - j % 2)
                    else:
                        def body(it, b=b, u0=u0, c=c, hid=hid):
                            for j in range(4):
                                gemm(Blk(b, it, j), g_hi, g_lo, seg_list, FCH[c],
                                     ready=(s("g_ready"), pairs + hid + 1) if j == 0 else None)
                                if u0 is not None and j % 2:
                                    mod_fold(it * 2 + (u0 + j // 2), 1 - j // 2)
                    loop(pe, n // 4, body)
                    if u0 is not None:
                        u0 += n if kind == "up" else n // 2

            pe.wait_ge(s("silc"), 1)
            for u in range(N_MOD0):
                if u in DVE_MOD0:
                    continue
                pe.wait_ge(s(f"mod0_loaded{u // 4}"), 16)
                for k in range(KT):
                    last = mm(ps[:, 7, 2 * u:2 * u + 2], w_mod0[u // 4][:, u % 4, P * k:P * k + P], silc[:, k, :],
                              k == 0, k == KT - 1)
                last.then_inc(s("mod_mm"), 1)
            pe.wait_ge(s("ca_loaded"), 16)
            sum_partitions(0, 0)
            for i, u in enumerate(DVE_MOD0):
                pe.wait_ge(s("mod0_part"), i + 1)
                for c in range(2):
                    last = mm(ps[:, 7, 2 * u + c:2 * u + c + 1], m0_part[:, i, c, :], ones[:, 0:1])
                last.then_inc(s("mod_mm"), 1)
            ffn(0, B_FFN1, segs_all, 0)
            sum_partitions(1, 0)
            mod_fold(N_MOD - N_MOD0, 1)
            sum_squares(2, 0)
            def k_sum(j):
                pe.wait_ge(s("at_sq"), j + 1)
                mm(ps[:, 4, 0:CTX], ones, a_sq[:, 0:CTX])
                mm(ps[:, 5, 0:SEQ], ones, a_sq[:, CTX:T]).then_inc(s("at_ss"), 1)

            def k_swap(j):
                if j:
                    pe.wait_ge(s("at_rot"), j)
                pe.wait_ge(s("at_nrm"), j + 1)
                mm(ps[:, 6, :], swap, a_n[:, 0:SEQ]).then_inc(s("at_swap"), 1)

            def v_tokens(j):
                blk = Blk(B_KV, 0, 2 + j)
                pe.wait_ge(psum_read[blk.pair], blk.turn + 2)
                if j:
                    pe.wait_ge(s("at_vc"), 1)
                for c in range(NCH):
                    last = pe.transpose(ps[:, 6 + c // 3, P * (c % 3):P * (c % 3) + P], a_raw[:, P * c:P * c + P], ident)
                last.then_inc(s("at_vt"), 1)
            gemm(Blk(B_KV, 0, 0), h_hi, h_lo, segs_all, ready=(s("h_ready"), KT))
            gemm(Blk(B_KV, 0, 1), h_hi, h_lo, segs_all)
            k_sum(0)
            gemm(Blk(B_KV, 0, 2), h_hi, h_lo, segs_all)
            k_swap(0)
            k_sum(1)
            gemm(Blk(B_KV, 0, 3), h_hi, h_lo, segs_all)
            k_swap(1)
            pe.wait_ge(s("at_rot"), 2)
            v_tokens(0)
            gemm(Blk(B_KV, 0, 4), h_hi, h_lo, segs_all)
            v_tokens(1)
            gemm(Blk(B_Q, 0, 0), h_hi, h_lo, segs_x)
            pe.wait_ge(s("ba_bx"), 2)
            pe.wait_ge(s("at_vc"), 2)
            for c in range(NCH):
                last = pe.transpose(ps[:, 6 + c // 3, P * (c % 3):P * (c % 3) + P], bx[:, P * c:P * c + P], ident)
            last.then_inc(s("ba_tr"), 1)
            gemm(Blk(B_Q, 0, 1), h_hi, h_lo, segs_x)
            pe.wait_ge(s("ba_bg"), 1)
            mm(ps[:, 6, 0:48], tri_le, bg[:, :, 32:40])
            mm(ps[:, 6, 48:96], tri_ge, bg[:, :, 40:48])
            mm(ps[:, 6, 96:192], ones, bg[:, :, 32:48]).then_inc(s("ba_sum"), 1)

            def q_sum(n):
                pe.wait_ge(s("at_sq"), n + 3)
                mm(ps[:, 4 + n % 2, :], ones, q_sq[n % 2]).then_inc(s("at_ss"), 1)

            def q_swap(n):
                if n == 0:
                    pe.wait_ge(s("ba_x"), 3)
                pe.wait_ge(s("at_nrm"), n + 3)
                mm(ps[:, 6 + n % 2, :], swap, q_n[n % 2]).then_inc(s("at_swap"), 1)
            for n in range(H):
                if n == 4:
                    q_swap(3)
                if n + 2 < H:
                    gemm(Blk(B_Q, 0, n + 2), h_hi, h_lo, segs_x)
                q_sum(n)
                if n and n != 4:
                    q_swap(n - 1)
            q_swap(H - 1)
            pe.wait_ge(s("at_rot"), H + 2)

            def heads(it):
                pe.wait_ge(s("o_at"), it * 4 + 1)

                def scores(i):
                    j, t = i // 4, i % 4
                    if t == 0:
                        pe.wait_ge(s("at_qc"), it * 4 + (j + 1))
                    if i >= 2:
                        pe.wait_ge(s("at_p"), it * 16 + (i - 1))
                    for k in range(2):
                        last = mm(ps[:, 4 + 2 * (i % 2) + k, 0:384], a_q[:, j % 2, P * t:P * t + P],
                                  a_kt[:, bass.ds(it, 1), 384 * k:384 * k + 384].rearrange("p a n -> p (a n)"))
                    last.then_inc(s("at_s"), 1)
                scores(0)
                scores(1)
                for i in range(16):
                    j, t = i // 4, i % 4
                    if i < 14:
                        scores(i + 2)
                    pe.wait_ge(s("at_pn"), it * 16 + (i + 1))
                    if i:
                        pe.wait_ge(s("at_pt"), it * 16 + i)
                    for c in range(NCH):
                        last = pe.transpose(ps[:, c // 3, P * (c % 3):P * (c % 3) + P],
                                            a_p[:, i % 2, P * c:P * c + P], ident)
                    last.then_inc(s("at_tr"), 1)
                    if t == 3:
                        pe.wait_ge(s("at_pt"), it * 16 + (i + 1))
                        if j == 0:
                            pe.wait_ge(s("at_vcur"), it + 1)
                        if j >= 2:
                            pe.wait_ge(s("o_at"), it * 4 + j)
                        for c in range(NCH):
                            last = mm(ps[:, 2 + j % 2, :], a_vc[:, c], a_pt[j % 2][:, c], c == 0, c == NCH - 1)
                        last.then_inc(s("at_pv"), 1)
            loop(pe, 2, heads)

            pe.wait_ge(s("o_at"), H + 1)

            def dn_gemm(h, j):
                gemm(Blk(B_DN, h, j), h_hi, h_lo, segs_x if j in (0, 3, 4) else segs_all)

            def dn_head(h, final):
                b = [Blk(B_DN, h, j) for j in range(4)]
                pe.wait_ge(s("hc"), h + 1)
                for d in range(2):
                    for c in range(NCH):
                        g_ = hc[:, G_GC + 6 * d + c:G_GC + 6 * d + c + 1]
                        last = mm(ps[:, 4 + 2 * d + c // 3, P * (c % 3):P * (c % 3) + P], g_.to_broadcast([P, P]), ident)
                    last.then_inc(s("d_row"), 1)
                dn_gemm(h, 1)
                dn_gemm(h, 2)
                pe.wait_ge(s("d_sq"), h + 1)
                pe.wait_ge(s("d_qe"), h * 2 + 2)
                mm(ps[:, 4, :], ones, d_sq[:, 0:SEQ])
                mm(ps[:, 5, 0:CTX], ones, d_sq[:, SEQ:SEQ + CTX])
                mm(ps[:, 6, :], ones, d_sq[:, SEQ + CTX:]).then_inc(s("d_ss"), 1)
                dn_gemm(h, 3)
                off = [c * P + (2 if c >= NC_CTX else 0) for c in range(NCH)]

                def tokens(i):
                    for c in range(NCH):
                        last = pe.transpose(ps[:, 2 - 2 * i + c // 3, P * (c % 3):P * (c % 3) + P],
                                             d_c[:, 1 + i, off[c]:off[c] + P], ident)
                    last.then_inc(s("d_tok"), 1)
                pe.wait_ge(s("d_qk"), h * 2 + 1)
                for c in range(NCH):
                    kc = d_c[:, 1, off[c]:off[c] + P]
                    last = mm(ps[:, 4 + c // 3, P * (c % 3):P * (c % 3) + P], kc, kc)
                last.then_inc(s("d_kk"), 1)
                pe.wait_ge(s("d_qk"), h * 2 + 2)
                for c in range(NC_X):
                    last = mm(ps[:, 6, P * c:P * c + P], d_c[:, 1, off[c + NC_CTX]:off[c + NC_CTX] + P],
                               d_c[:, 0, off[c + NC_CTX]:off[c + NC_CTX] + P])
                last.then_inc(s("d_kq"), 1)
                pe.wait_ge(psum_read[b[2].pair], b[2].turn + 2)
                tokens(0)
                pe.wait_ge(psum_read[b[3].pair], b[3].turn + 2)
                pe.wait_ge(s("d_silu"), h * 3 + 3)
                tokens(1)
                pe.wait_ge(s("d_l"), h * 2 + 2)
                for gr in range(4):
                    d, hf = gr // 2, gr % 2
                    if gr == 2:
                        pe.wait_ge(s("d_am"), h * 2 + 2)
                    pe.wait_ge(s(f"lvl{d}"), h * 7 + 1)
                    for i in range(3):
                        last = pe.transpose(ps[:, 4 + gr, P * i:P * i + P], d_s[0][:, d, 3 * hf + i], ident)
                    last.then_inc(s("sv_q"), 1)
                pe.wait_ge(s("d_tokc"), h * 2 + 2)
                for lv in range(1, LEVELS):
                    for gr in range(4):
                        d, hf = gr // 2, gr % 2
                        pe.wait_ge(s(f"lvl{d}"), h * 7 + lv + 1)
                        pe.wait_ge(s("sv_r"), h * 28 + 4 * (lv - 1) + gr + 1)
                        for i in range(3):
                            last = mm(ps[:, 4 + gr, P * i:P * i + P], d_s[lv % 2][:, d, 3 * hf + i], d_r[:, d, 3 * hf + i])
                        last.then_inc(s("sv_q"), 1)
                    if lv == 1:
                        pe.wait_ge(s("t_set"), h + 1)
                    for gr in range(4):
                        d, hf = gr // 2, gr % 2
                        pe.wait_ge(s("sv_qc"), h * 24 + 4 * (lv - 1) + gr + 1)
                        q3, t3 = (half(x[:, d, 3 * hf:3 * hf + 3], lv, o) for x, o in ((d_q, 1 - d), (d_t, d)))
                        for i in range(3):
                            last = mm(ps[:, 4 + gr, 64 * i:64 * i + 64], d_t[:, d, 3 * hf + i], q3[:, i])
                        if lv < LEVELS - 1:
                            for i in range(3):
                                last = mm(ps[:, gr, 64 * i:64 * i + 64], d_q[:, d, 3 * hf + i], t3[:, i])
                        last.then_inc(s("sv_d"), 1)
                pe.wait_ge(s("d_kbvb"), h * 3 + 3)
                pe.wait_ge(s("d_kb0"), h + 1)
                for gr in range(4):
                    d, hf = gr // 2, gr % 2
                    pe.wait_ge(s("sv_r"), h * 28 + 24 + gr + 1)
                    for i in range(3):
                        mm(ps[:, 4 + gr, P * i:P * i + P], d_r[:, d, 3 * hf + i], d_l[:, d, 3 * hf + i])
                    for i in range(3):
                        last = mm(ps[:, gr, P * i:P * i + P], d_s[1][:, d, 3 * hf + i], d_r[:, d, 3 * hf + i])
                    last.then_inc(s("uw"), 1)
                pe.wait_ge(s("w_c"), h * 4 + 4)
                pe.wait_ge(s("u_c"), h * 4 + 4)
                pe.wait_ge(s("d_kd"), h * 2 + 2)
                pe.wait_ge(s("d_qd"), h * 2 + 2)
                pe.wait_ge(s("d_at"), h * 2 + 2)
                for t in range(NCH):
                    if t:
                        for d in range(2):
                            pe.wait_ge(s("sc_st"), h * 10 + 2 * (t - 1) + d + 1)
                            mm(ps[:, 4 + d, 0:P], d_t[:, d, ORDER[d][t]], d_st[:, d]).then_inc(s("sc_w"), 1)
                    for d in range(2):
                        c = ORDER[d][t]
                        vn = d_q[:, d, c]
                        if t:
                            vn = d_vn[:, d]
                            if c >= NC_CTX:
                                mm(ps[:, d, P * (c - NC_CTX):P * (c - NC_CTX) + P], d_st[:, d], d_qd[:, d, c - NC_CTX], True, False)
                            pe.wait_ge(s("sc_v"), h * 10 + 2 * (t - 1) + d + 1)
                        if t < NCH - 1:
                            mm(ps[:, 6 + d, 0:P], d_kd[:, d, c], vn).then_inc(s("sc_s"), 1)
                        if c >= NC_CTX:
                            mm(ps[:, d, P * (c - NC_CTX):P * (c - NC_CTX) + P], vn, d_at[:, d, c - NC_CTX], False, True)\
                                .then_inc(s("sc_o"), 1)
                if not final:
                    dn_gemm(h, 4)
                pe.wait_ge(s("od_sq"), h + 1)
                mm(ps[:, 2, :], ones, d_sq[:, 0:SEQ]).then_inc(s("od_ss"), 1)
            dn_gemm(0, 0)
            with pe.Fori(0, H - 1, 1) as h:
                dn_head(h, False)
            dn_head(H - 1, True)

            def merge(it):
                for j in range(4):
                    hi, lo, off = ((odn_hi, odn_lo, CTX), (h_hi, h_lo, 0), (oat_hi, oat_lo, CTX), (h_hi, h_lo, 0))[j]
                    gemm(Blk(B_MERGE, it, j), hi, lo, segs_x, off=off, ready=(s("o_split"), H * j // 2) if j % 2 == 0 else None)
            loop(pe, KT, merge)

            def out_proj(it):
                for j in range(4):
                    gemm(Blk(B_OUT, it, j), m_hi, m_lo, segs_x, off=CTX, ready=(s("m_ready"), 0) if j == 0 else None)
            loop(pe, KT // 4, out_proj)
            sum_partitions(3, CTX)
            sum_squares(4, CTX)
            ffn(1, B_FFN2, segs_x)
            sum_partitions(5, CTX)


ORDER = [list(range(NCH)), list(range(NC_CTX))[::-1] + list(range(NC_CTX, NCH))[::-1]]


def _constants():
    i = np.arange(P)
    eye = np.eye(P, dtype=np.float32)
    swap = np.zeros((P, P), np.float32)
    swap[i ^ 32, i] = 1.0
    ca = np.stack([eye, np.ones((P, P), np.float32), (i[:, None] >= i[None, :]).astype(np.float32),
                   (i[:, None] <= i[None, :]).astype(np.float32), swap], 1)
    masks = np.zeros((P, 2, LEVELS, P), np.float32)
    for l in range(LEVELS):
        b = 1 << l
        m = (i[:, None] // (2 * b) == i[None, :] // (2 * b)) & (i[:, None] // b % 2 == 1) & (i[None, :] // b % 2 == 0)
        masks[:, 0, l] = m
        masks[:, 1, l] = m.T
    nf = DH // 4
    inv = (np.float32(10000.0) ** (-np.arange(nf, dtype=np.float32) / np.float32(nf))).astype(np.float32)
    pos = np.stack([np.repeat(np.arange(SEQ // 64), 64), np.tile(np.arange(64), SEQ // 64)]).astype(np.float32)
    ang = pos[:, None, :] * inv[None, :, None]
    cos = np.cos(ang, dtype=np.float32)
    sin = np.sin(ang, dtype=np.float32)
    c = np.stack([cos, cos], 1).reshape(P, SEQ)
    s_ = np.stack([-sin, sin], 1).reshape(P, SEQ)
    cb = np.concatenate([masks.reshape(P, -1), c, s_], 1)
    return np.ascontiguousarray(ca), np.ascontiguousarray(cb, dtype=np.float32)


def _tiles(w):
    K, N = w.shape
    t = w.reshape(K // P, P, N // P, P).transpose(2, 1, 0, 3)
    if K < D:
        t = np.concatenate([t, np.zeros((N // P, P, KT - K // P, P), w.dtype)], 2)
    return t.reshape(N // P, P, D)


def _ffn_blocks(w_gu, w_down):
    gu = _tiles(w_gu)
    out, hid = [], 0
    for n in FCH:
        pair = np.stack([gu[hid:hid + n], gu[HID + hid:HID + hid + n]], 1)
        out += [pair.reshape(2 * n, P, D), _tiles(w_down[hid * P:(hid + n) * P])]
        hid += n
    return out


def layout(i):
    w_in = i["w_in"][0]
    qkv, z = w_in[:, 0:3072], w_in[:, 3072:4096]
    w_ba, w_q, w_kv, w_g = w_in[:, 4096:4128], w_in[:, 4128:5152], w_in[:, 5152:5664], w_in[:, 5664:7712]
    pad = np.zeros((D, P), w_in.dtype)
    pad[:, 0:16] = w_ba[:, 0:16]
    pad[:, 32:48] = w_ba[:, 16:32]
    dn = np.stack([_tiles(qkv[:, 0:1024]), _tiles(qkv[:, 1024:2048]), _tiles(qkv[:, 2048:3072]), _tiles(z)], 1)
    mg = np.stack([_tiles(i["w_dn_out"][0]), _tiles(w_g[:, 0:1024]), _tiles(i["w_attn_out"][0]),
                   _tiles(w_g[:, 1024:2048])], 1)
    W = np.concatenate(_ffn_blocks(i["ffn1_w_gu"][0], i["ffn1_w_down"][0])
                       + [_tiles(w_kv), _tiles(pad), _tiles(w_q), dn.reshape(-1, P, D), mg.reshape(-1, P, D),
                          _tiles(i["w_out"][0])]
                       + _ffn_blocks(i["ffn2_w_gu"][0], i["ffn2_w_down"][0]))
    col = lambda a: a.reshape(-1, P).T
    gates = np.zeros((P, 2), np.float32)
    gates[32:48, 0] = i["dn_a_log"][0].reshape(-1)
    gates[32:48, 1] = i["dn_dt_bias"][0].reshape(-1)
    cc = np.stack([col(i["c_ctx"]), col(i["c"][0])], 2).reshape(P, -1)
    vec = np.concatenate([col(i[n][0]) for n in ("ffn1_pre", "ffn1_post", "mix_pre", "mix_post", "ffn2_pre", "ffn2_post",
                                                 "b_mod", "attn_q_norm", "attn_k_norm", "dn_out_norm")] + [gates, cc], 1)
    conv = i["dn_conv"][0].reshape(3, 3, H, P).transpose(3, 2, 1, 0).reshape(P, H, 9)
    ca, cb = _constants()
    return dict(W=W, WMOD=_tiles(i["w_mod"][0]), XT=np.concatenate([i["ctx"][0], i["x"][0]]).T,
                VEC=vec, CONV=conv, CA=ca, CB=cb)


def kernel(**inputs):
    import concourse.bacc as bacc
    from concourse.bass_utils import run_bass_kernel_spmd as run

    arrays = {k: np.ascontiguousarray(a) for k, a in layout({k: np.asarray(a) for k, a in inputs.items()}).items()}
    nc = bacc.Bacc("TRN2", target_bir_lowering=False, num_devices=1)
    args = [nc.dram_tensor(k, a.shape, F32, kind="ExternalInput").ap() for k, a in arrays.items()]
    out = nc.dram_tensor("out", [D, SEQ], F32, kind="ExternalOutput").ap()
    spill = nc.dram_tensor("x_spill", [P, KT, SEQ], F32, kind="Internal").ap()
    build(nc, *args, out, spill)
    r = run(nc, [arrays], core_ids=[0])
    return np.ascontiguousarray(r.results[0]["out"].T).reshape(1, SEQ, D)
```
